# Optimizing a Trainium2 kernel written in Bass

```python
import jax, jax.numpy as jnp
from jax import lax
import numpy as np

D_MODEL = 1024
BATCH = 1
SEQ = 512
DEPTH = 2

CHUNK = 64
N_MIXERS = 2
N_RET = (DEPTH + 1) // 2
N_MLA = DEPTH // 2
ROPE_THETA = 10000.0
EPS = 1e-6
RET_HEADS = 4
RET_DK = D_MODEL // RET_HEADS
RET_DV = 2 * RET_DK
RET_QK_W = RET_HEADS * RET_DK
RET_V_W = RET_HEADS * RET_DV
RET_IN = 2 * RET_QK_W + 2 * RET_V_W
MLA_HEADS = 8
MLA_NOPE = 128
MLA_ROPE = 64
MLA_QKD = MLA_NOPE + MLA_ROPE
MLA_VD = 128
MLA_Q_RANK = 384
MLA_KV_RANK = 256
MLA_IN = MLA_Q_RANK + MLA_KV_RANK + MLA_ROPE
Q_BLOCK = 128
D_FF = 4 * D_MODEL
PLE_DIM = 256

kernel_name = "hybrid_retention_mla_trunk"

def _rmsnorm(x, g):
    xf = x.astype(jnp.float32)
    y = xf * lax.rsqrt(jnp.mean(xf * xf, axis=-1, keepdims=True) + EPS)
    return (y * g.astype(jnp.float32)).astype(x.dtype)

def _rope_tables(seq, dim, dtype):
    inv = 1.0 / (ROPE_THETA ** (jnp.arange(0, dim, 2, dtype=jnp.float32) / dim))
    ang = jnp.arange(seq, dtype=jnp.float32)[:, None] * inv[None, :]
    return jnp.cos(ang)[:, None, :].astype(dtype), jnp.sin(ang)[:, None, :].astype(dtype)

def _rope(x, cos, sin):
    x1, x2 = jnp.split(x, 2, axis=-1)
    return jnp.concatenate([x1 * cos - x2 * sin, x2 * cos + x1 * sin], axis=-1)

def _retention(h, w_in, gn_gain, w_out):
    B, S, _ = h.shape
    nc = S // CHUNK
    proj = h @ w_in
    q, k, v, g = jnp.split(proj, [RET_QK_W, 2 * RET_QK_W, 2 * RET_QK_W + RET_V_W], axis=-1)
    cos, sin = _rope_tables(S, RET_DK, h.dtype)
    q = _rope(q.reshape(B, S, RET_HEADS, RET_DK), cos, sin)
    k = _rope(k.reshape(B, S, RET_HEADS, RET_DK), cos, sin) * (RET_DK ** -0.5)
    v = v.reshape(B, S, RET_HEADS, RET_DV)

    def to_chunks(t):
        return t.reshape(B, nc, CHUNK, RET_HEADS, t.shape[-1]).transpose(1, 0, 3, 2, 4)

    qc, kc, vc = to_chunks(q), to_chunks(k), to_chunks(v)
    log_gamma = jnp.log(1.0 - 2.0 ** (-5.0 - jnp.arange(RET_HEADS, dtype=jnp.float32)))
    idx = jnp.arange(CHUNK, dtype=jnp.float32)
    dist = jnp.abs(idx[:, None] - idx[None, :])
    intra = jnp.exp(log_gamma[:, None, None] * dist).astype(h.dtype)
    q_decay = jnp.exp(log_gamma[:, None] * (idx + 1.0))[None, :, :, None].astype(h.dtype)
    k_decay = jnp.exp(log_gamma[:, None] * (CHUNK - 1.0 - idx))[None, :, :, None].astype(h.dtype)
    chunk_decay = jnp.exp(log_gamma * CHUNK)[None, :, None, None].astype(h.dtype)

    def step(state, xs):
        qi, ki, vi = xs
        scores = jnp.einsum('bhnd,bhmd->bhnm', qi, ki) * intra
        inner = jnp.einsum('bhnm,bhmv->bhnv', scores, vi)
        cross = jnp.einsum('bhnd,bhdv->bhnv', qi * q_decay, state)
        new_state = state * chunk_decay + jnp.einsum('bhmd,bhmv->bhdv', ki * k_decay, vi)
        return new_state, inner + cross

    state0 = jnp.zeros((B, RET_HEADS, RET_DK, RET_DV), h.dtype)
    _, out = lax.scan(step, state0, (qc, kc, vc))
    out = out.transpose(1, 0, 3, 2, 4).reshape(B, S, RET_HEADS, RET_DV)
    out = _rmsnorm(out, gn_gain).reshape(B, S, RET_V_W)
    return (jax.nn.silu(g) * out) @ w_out

def _mla(h, w_in, q_a_gain, kv_a_gain, w_uq, w_ukv, q_gain, k_gain, w_out):
    B, S, _ = h.shape
    proj = h @ w_in
    c_q, c_kv, k_r = jnp.split(proj, [MLA_Q_RANK, MLA_Q_RANK + MLA_KV_RANK], axis=-1)
    q = (_rmsnorm(c_q, q_a_gain) @ w_uq).reshape(B, S, MLA_HEADS, MLA_QKD)
    kv = (_rmsnorm(c_kv, kv_a_gain) @ w_ukv).reshape(B, S, MLA_HEADS, MLA_NOPE + MLA_VD)
    k_nope, v = jnp.split(kv, [MLA_NOPE], axis=-1)
    k = jnp.concatenate([k_nope, jnp.broadcast_to(k_r[:, :, None, :], (B, S, MLA_HEADS, MLA_ROPE))], axis=-1)
    q = _rmsnorm(q, q_gain)
    k = _rmsnorm(k, k_gain)
    cos, sin = _rope_tables(S, MLA_ROPE, h.dtype)
    q = jnp.concatenate([q[..., :MLA_NOPE], _rope(q[..., MLA_NOPE:], cos, sin)], axis=-1)
    k = jnp.concatenate([k[..., :MLA_NOPE], _rope(k[..., MLA_NOPE:], cos, sin)], axis=-1)
    q = q.transpose(0, 2, 1, 3)
    k = k.transpose(0, 2, 1, 3)
    v = v.transpose(0, 2, 1, 3)
    scale = MLA_QKD ** -0.5
    outs = []
    for blk in range(S // Q_BLOCK):
        q0 = blk * Q_BLOCK
        kend = q0 + Q_BLOCK
        qb = q[:, :, q0:kend]
        kb = k[:, :, :kend]
        vb = v[:, :, :kend]
        s = jnp.einsum('bhqd,bhkd->bhqk', qb, kb).astype(jnp.float32) * scale
        q_chunk = (q0 + jnp.arange(Q_BLOCK)) // CHUNK
        k_chunk = jnp.arange(kend) // CHUNK
        s = jnp.where(k_chunk[None, :] <= q_chunk[:, None], s, -1e30)
        pr = jax.nn.softmax(s, axis=-1).astype(vb.dtype)
        outs.append(jnp.einsum('bhqk,bhkd->bhqd', pr, vb))
    o = jnp.concatenate(outs, axis=2).transpose(0, 2, 1, 3).reshape(B, S, MLA_HEADS * MLA_VD)
    return o @ w_out

def _dense(k, shape, fan_in):
    return jax.random.normal(k, shape, jnp.float32) * (fan_in ** -0.5)

def _gain(k, shape):
    return 1.0 + 0.05 * jax.random.normal(k, shape, jnp.float32)

def setup_inputs(seed: int = 0) -> dict:
    key = jax.random.key(seed)
    ks = jax.random.split(key, 20)
    return {
        "x": jax.random.normal(ks[0], (BATCH, SEQ, D_MODEL), jnp.float32),
        "p": jax.random.normal(ks[1], (DEPTH, BATCH, SEQ, PLE_DIM), jnp.float32),
        "mix_norm": _gain(ks[2], (DEPTH, D_MODEL)),
        "ret_w_in": _dense(ks[3], (N_RET, D_MODEL, RET_IN), D_MODEL),
        "ret_gn": _gain(ks[4], (N_RET, RET_HEADS, RET_DV)),
        "ret_w_out": _dense(ks[5], (N_RET, RET_V_W, D_MODEL), RET_V_W),
        "mla_w_in": _dense(ks[6], (N_MLA, D_MODEL, MLA_IN), D_MODEL),
        "mla_q_a_norm": _gain(ks[7], (N_MLA, MLA_Q_RANK)),
        "mla_kv_a_norm": _gain(ks[8], (N_MLA, MLA_KV_RANK)),
        "mla_w_uq": _dense(ks[9], (N_MLA, MLA_Q_RANK, MLA_HEADS * MLA_QKD), MLA_Q_RANK),
        "mla_w_ukv": _dense(ks[10], (N_MLA, MLA_KV_RANK, MLA_HEADS * (MLA_NOPE + MLA_VD)), MLA_KV_RANK),
        "mla_q_norm": _gain(ks[11], (N_MLA, MLA_QKD)),
        "mla_k_norm": _gain(ks[12], (N_MLA, MLA_QKD)),
        "mla_w_out": _dense(ks[13], (N_MLA, MLA_HEADS * MLA_VD, D_MODEL), MLA_HEADS * MLA_VD),
        "mlp_norm": _gain(ks[14], (DEPTH, D_MODEL)),
        "mlp_w1": _dense(ks[15], (DEPTH, D_MODEL, D_FF), D_MODEL),
        "mlp_w2": _dense(ks[16], (DEPTH, D_FF, D_MODEL), D_FF),
        "ple_norm": _gain(ks[17], (DEPTH, D_MODEL)),
        "ple_gate_w": _dense(ks[18], (DEPTH, D_MODEL, D_MODEL), D_MODEL),
        "ple_proj_w": _dense(ks[19], (DEPTH, PLE_DIM, D_MODEL), PLE_DIM),
    }

def reference(x, p, mix_norm, ret_w_in, ret_gn, ret_w_out, mla_w_in, mla_q_a_norm, mla_kv_a_norm,
              mla_w_uq, mla_w_ukv, mla_q_norm, mla_k_norm, mla_w_out, mlp_norm, mlp_w1, mlp_w2,
              ple_norm, ple_gate_w, ple_proj_w):
    h = x
    for i in range(DEPTH):
        j = i // N_MIXERS
        hn = _rmsnorm(h, mix_norm[i])
        if i % N_MIXERS == 0:
            mixed = _retention(hn, ret_w_in[j], ret_gn[j], ret_w_out[j])
        else:
            mixed = _mla(hn, mla_w_in[j], mla_q_a_norm[j], mla_kv_a_norm[j], mla_w_uq[j], mla_w_ukv[j],
                         mla_q_norm[j], mla_k_norm[j], mla_w_out[j])
        h = h + mixed
        hn = _rmsnorm(h, mlp_norm[i])
        h = h + jnp.square(jax.nn.relu(hn @ mlp_w1[i])) @ mlp_w2[i]
        gate = jax.nn.sigmoid(_rmsnorm(h, ple_norm[i]) @ ple_gate_w[i])
        h = h + gate * (p[i] @ ple_proj_w[i])
    return h


_drawn_inputs = setup_inputs


def setup_inputs(seed=0):
    import zlib

    import numpy as np

    out = dict(_drawn_inputs(seed))
    spreads = {}
    factors = {'mla_q_a_norm': 8.0,
     'mla_kv_a_norm': 6.461,
     'mla_q_norm': 8.0,
     'mla_k_norm': 8.0,
     'ple_norm': 7.429}
    for name, (base, spread) in spreads.items():
        noise = np.random.default_rng([zlib.crc32(name.encode()), seed]).standard_normal(out[name].shape)
        drawn = base * np.exp(spread * noise) if base else spread * noise
        out[name] = __import__('jax').numpy.asarray(drawn.astype(out[name].dtype))
    for name, factor in factors.items():
        out[name] = (out[name] * factor).astype(out[name].dtype)
    return out
```

```python
from contextlib import ExitStack

import numpy as np

import concourse.bass as bass
from concourse import mybir
from concourse.alu_op_type import AluOpType as ALU

F32 = mybir.dt.float32
F32R = mybir.dt.float32r
ACT = mybir.ActivationFunctionType
AX = mybir.AxisListType

P = 128
D = 1024
T = 512
KT = D // P
TT = T // P
CHUNK = 64
EPS = 1e-6
RING = 4
AHEAD = 3
SLOT = 1024

HEADS = 4
DK = D // HEADS
DV = 2 * DK
VT = DV // P

MH = 8
NOPE, ROPE, VD = 128, 64, 128
QKD = NOPE + ROPE
QR, KVR = 384, 256
QF, KVF = QR // P, KVR // P
GH = 2
GROUPS = MH // GH
PLE = 256
PF = PLE // P
QUARTERS = 4

RET_FIRST = 12
RET_HEAD = 16
RET_SLOTS = RET_FIRST + (HEADS - 1) * RET_HEAD + 4
MLP_SLOTS = QUARTERS * 2 * KT
PLE_SLOTS = KT + 2
LAYER0_SLOTS = RET_SLOTS + MLP_SLOTS + PLE_SLOTS
MLA_IN_SLOTS = 8
MLA_GROUP_SLOTS = 4
MLA_SLOTS = MLA_IN_SLOTS + GROUPS * MLA_GROUP_SLOTS + KT
LAYER1_SLOTS = MLP_SLOTS + PLE_SLOTS
MLA_BASE = LAYER0_SLOTS
MLA_GROUP_BASE = MLA_BASE + MLA_IN_SLOTS
MLA_OUT_BASE = MLA_GROUP_BASE + GROUPS * MLA_GROUP_SLOTS
MLP_BASE = (RET_SLOTS, MLA_BASE + MLA_SLOTS)
PLE_BASE = (MLP_BASE[0] + MLP_SLOTS, MLP_BASE[1] + MLP_SLOTS)
SLOTS = PLE_BASE[1] + PLE_SLOTS
assert SLOTS == LAYER0_SLOTS + MLA_SLOTS + LAYER1_SLOTS

RET_FIRST_UNITS = 12
RET_HEAD_UNITS = 20
RET_UNITS = RET_FIRST_UNITS + (HEADS - 1) * RET_HEAD_UNITS + KT
MLP_UNITS = MLP_SLOTS
PLE_UNITS = KT
MLA_IN_UNITS = 8
MLP_UNIT = (RET_UNITS, RET_UNITS + MLP_UNITS + PLE_UNITS + MLA_IN_UNITS + KT)
PLE_UNIT = (MLP_UNIT[0] + MLP_UNITS, MLP_UNIT[1] + MLP_UNITS)
MLA_UNIT = PLE_UNIT[0] + PLE_UNITS
MLA_OUT_UNIT = MLA_UNIT + MLA_IN_UNITS
UB = 4
NORM_BANK = 7

MIX0, MLP0, PLE0, MIX1, MLP1, PLE1 = range(6)
G_GN = 6 * KT
G_QA = G_GN + HEADS * VT
G_KVA = G_QA + QF
G_QN = G_KVA + KVF
G_KN = G_QN + 1
GAINS = G_KN + 1


PLE_PROJ = (2, 7)
PLE_GATE = tuple(s for s in range(KT + 2) if s not in PLE_PROJ)


def gate_unit(v, j, per):
    return RET_FIRST_UNITS - VT + v + (RET_HEAD_UNITS * (j + 1) if per else 0)


def slot_width(n):
    if MLA_BASE <= n < MLA_GROUP_BASE:
        return 2 * QR if n < MLA_BASE + 4 else 2 * (KVR + ROPE)
    if MLA_GROUP_BASE <= n < MLA_OUT_BASE:
        return GH * QKD if (n - MLA_GROUP_BASE) % MLA_GROUP_SLOTS < QF else SLOT
    return SLOT


RET_MARKS = 14
MLA_MARKS = 39


class Chain:

    def __init__(self, engine, sem):
        self.engine, self.sem, self.base, self.local = engine, sem, 0, 0

    def mark(self, ins):
        ins.then_inc(self.sem, 1)
        self.local += 1

    def wait(self):
        self.engine.wait_ge(self.sem, self.base + self.local)

    def enter(self, i, per):
        self.outer = self.base + self.local
        self.base, self.local = self.outer + per * i, 0

    def leave(self, per, turns):
        assert self.local == per, self.local
        self.base, self.local = self.outer + per * turns, 0


def build(nc, a):
    with ExitStack() as ctx:
        def sb(name, shape, dt=F32, scope=ctx):
            return scope.enter_context(nc.sbuf_tensor(name, shape, dt))

        def sem(name):
            return ctx.enter_context(nc.semaphore(name))

        h = sb("h", [P, KT, T])
        x_hi = sb("x_hi", [P, KT, T], F32R)
        x_lo = sb("x_lo", [P, KT, T], F32R)
        w_raw = sb("w_raw", [P, RING, SLOT])
        w_hi = sb("w_hi", [P, RING, SLOT], F32R)
        w_lo = sb("w_lo", [P, RING, SLOT], F32R)
        gains = sb("gains", [P, GAINS])
        ident = sb("ident", [P, P])
        ones = sb("ones", [P, P])
        sq = sb("sq", [P, 2, T])
        sq_sum = sb("sq_sum", [P, T])
        rstd = sb("rstd", [P, T])
        rstd_tok = sb("rstd_tok", [P, TT])
        tmp = sb("tmp", [P, 4, T])
        t_a, t_b = tmp[:, 0:2, :], tmp[:, 2:4, :]

        with ExitStack() as ret:
            qk_hi = sb("qk_hi", [P, 4, T], F32R, ret)
            qk_lo = sb("qk_lo", [P, 4, T], F32R, ret)
            s_hi = sb("s_hi", [P, TT, T], F32R, ret)
            s_lo = sb("s_lo", [P, TT, T], F32R, ret)
            v_hi = sb("v_hi", [P, TT, DV], F32R, ret)
            v_lo = sb("v_lo", [P, TT, DV], F32R, ret)
            y_hi = sb("y_hi", [P, VT, T], F32R, ret)
            y_lo = sb("y_lo", [P, VT, T], F32R, ret)
            sg = sb("sg", [P, VT, T], F32, ret)
            decay = sb("decay", [P, HEADS, T], F32, ret)
            rope_t = sb("rope_t", [P, 2, T], F32, ret)
            gn = sb("gn", [P, VT], F32, ret)
        with ExitStack() as mlp:
            x2_hi = sb("x2_hi", [P, KT, T], F32R, mlp)
            x2_lo = sb("x2_lo", [P, KT, T], F32R, mlp)
            hid_hi = sb("hid_hi", [P, KT, T], F32R, mlp)
            hid_lo = sb("hid_lo", [P, KT, T], F32R, mlp)
            p_raw = sb("p_raw", [P, PF, T], F32, mlp)
            p_hi = sb("p_hi", [P, PF, T], F32R, mlp)
            p_lo = sb("p_lo", [P, PF, T], F32R, mlp)
            proj = sb("proj", [P, 2, T], F32, mlp)
        with ExitStack() as mla:
            qT_hi = sb("qT_hi", [P, GH + 1, T], F32R, mla)
            qT_lo = sb("qT_lo", [P, GH + 1, T], F32R, mla)
            kT_hi = sb("kT_hi", [P, GH + 1, T], F32R, mla)
            kT_lo = sb("kT_lo", [P, GH + 1, T], F32R, mla)
            mv_hi = sb("mv_hi", [P, TT, GH * VD], F32R, mla)
            mv_lo = sb("mv_lo", [P, TT, GH * VD], F32R, mla)
            pT_hi = sb("pT_hi", [P, TT, T], F32R, mla)
            pT_lo = sb("pT_lo", [P, TT, T], F32R, mla)
            c_hi = sb("c_hi", [P, QF + KVF, T], F32R, mla)
            c_lo = sb("c_lo", [P, QF + KVF, T], F32R, mla)
            c_tok = sb("c_tok", [P, TT, QR + KVR + ROPE], F32, mla)
            q_tok = c_tok[:, :, 0:QR]
            k_tok = sb("k_tok", [P, TT, GH * NOPE], F32, mla)
            r_tok = sb("r_tok", [P, TT, GH * ROPE], F32, mla)
            kr_tok = sb("kr_tok", [P, TT, ROPE], F32, mla)
            r_mul = sb("r_mul", [P, TT, GH, ROPE], F32, mla)
            mrope = sb("mrope", [P, 2, TT, ROPE // 2], F32, mla)
            rgain = sb("rgain", [P, 2, ROPE], F32, mla)
            small = sb("small", [P, 64], F32, mla)
            qscale = sb("qscale", [P, TT * GH], F32, mla)
            att = sb("att", [P, 32], F32, mla)
            pr = sb("pr", [P, 2, T], F32, mla)

        ps = ctx.enter_context(nc.psum_tensor("ps", [P, 8, 512], F32))

        operand = {n: (x2_hi, x2_lo) if n in (MIX1, MLP1) else (x_hi, x_lo) for n in range(6)}

        raw_loaded = [sem(f"raw_loaded{r}") for r in range(RING)]
        hi_done = sem("hi_done")
        lo_done = sem("lo_done")
        slot_used = sem("slot_used")
        bank_read = sem("bank_read")
        ones_set = sem("ones_set")
        x_loaded = [sem(f"x_loaded{k}") for k in range(KT)]
        tables_loaded = sem("tables_loaded")
        sq_ready = sem("sq_ready")
        sq_added = sem("sq_added")
        xhi_ready = sem("xhi_ready")
        x_ready = sem("x_ready")
        ss_done = sem("ss_done")
        ms_ready = sem("ms_ready")
        root_ready = sem("root_ready")
        rstd_ready = sem("rstd_ready")
        tok_done = sem("tok_done")
        tok_ready = sem("tok_ready")
        h_ready = sem("h_ready")
        chain = sem("chain")
        out_stored = sem("out_stored")
        qk_rot = sem("qk_rot")
        qkhi_ready = sem("qkhi_ready")
        qk_ready = sem("qk_ready")
        vhi_ready = sem("vhi_ready")
        s_done = sem("s_done")
        s_mul = sem("s_mul")
        shi_ready = sem("shi_ready")
        s_ready = sem("s_ready")
        sig_ready = sem("sig_ready")
        pv_done = sem("pv_done")
        osq_ready = sem("osq_ready")
        osq_added = sem("osq_added")
        hss_done = sem("hss_done")
        hms_ready = sem("hms_ready")
        hroot_ready = sem("hroot_ready")
        y_val = sem("y_val")
        yhi_ready = sem("yhi_ready")
        y_ready = sem("y_ready")
        sqr_ready = sem("sqr_ready")
        hidhi_ready = sem("hidhi_ready")
        hid_ready = sem("hid_ready")
        p_loaded = [sem(f"p_loaded{l}") for l in range(2)]
        phi_ready = sem("phi_ready")
        p_ready = sem("p_ready")
        psig_ready = sem("psig_ready")
        mla_loaded = sem("mla_loaded")
        css_ready = sem("css_ready")
        cms_ready = sem("cms_ready")
        croot_ready = sem("croot_ready")
        cn_ready = sem("cn_ready")
        cT_done = sem("cT_done")
        chi_ready = sem("chi_ready")
        c_ready = sem("c_ready")
        qtok_ready = sem("qtok_ready")
        ktok_ready = sem("ktok_ready")
        mvhi_ready = sem("mvhi_ready")
        mv_ready = sem("mv_ready")
        qkms_ready = sem("qkms_ready")
        qkroot_ready = sem("qkroot_ready")
        qkn_ready = sem("qkn_ready")
        qkT_done = sem("qkT_done")
        qkThi_ready = sem("qkThi_ready")
        qkT_ready = sem("qkT_ready")
        sc_done = sem("sc_done")
        nmax_ready = sem("nmax_ready")
        exp_ready = sem("exp_ready")
        pr_ready = sem("pr_ready")
        pT_done = sem("pT_done")
        pThi_ready = sem("pThi_ready")
        pT_ready = sem("pT_ready")
        o_done = sem("o_done")
        ohi_ready = sem("ohi_ready")
        o_ready = sem("o_ready")

        block = ctx.enter_context(nc.Block())

        def stream_runs():
            return (a["weights0"], 0, LAYER0_SLOTS), (a["weights1"], MLP_BASE[1], LAYER1_SLOTS)

        def mla_source(n):
            s = n - MLA_BASE
            if s < 4:
                return a["mla_in_q"][s]
            if s < MLA_IN_SLOTS:
                return a["mla_in_kv"][s - 4]
            s = n - MLA_GROUP_BASE
            if s < GROUPS * MLA_GROUP_SLOTS:
                g, j = divmod(s, MLA_GROUP_SLOTS)
                return a["mla_uq"][g * QF + j] if j < QF else a["mla_ukv"][g]
            return a["mla_out"][n - MLA_OUT_BASE]

        def walk(engine, one):
            for w, first, count in stream_runs():
                if first:
                    for n in range(MLA_BASE, MLP_BASE[1]):
                        one(n, n % RING, mla_source(n), n // RING)
                head = RING if first == 0 else -first % RING
                for j in range(head):
                    one(first + j, (first + j) % RING, w[j], (first + j) // RING)
                turns = (count - head) // RING
                with engine.Fori(0, turns) as i:
                    for r in range(RING):
                        one(first + head + r + RING * i, r,
                            w[bass.ds(head + r + RING * i, 1)].rearrange("a p n -> (a p) n"),
                            (first + head) // RING + i)
                for j in range(head + turns * RING, count):
                    one(first + j, (first + j) % RING, w[j], (first + j) // RING)

        @block.sync
        def _(sp):
            def load(n, r, source, turn):
                width = slot_width(n) if isinstance(n, int) else SLOT
                if not isinstance(n, int) or n >= RING:
                    sp.wait_ge(lo_done, n - (RING - 1))
                sp.dma_start(w_raw[:, r, 0:width], source).then_inc(raw_loaded[r], 16)
            walk(sp, load)
            for k in range(KT):
                sp.wait_ge(h_ready, KT + k + 1)
                sp.dma_start(a["out"][:, k, :], h[:, k, :]).then_inc(out_stored, 16)
            sp.wait_ge(out_stored, 16 * KT)

        @block.gpsimd
        def _(pool):
            nc.gpsimd.memset(ones[:], 1.0).then_inc(ones_set, 1)

            def low(n, r, source, turn):
                width = slot_width(n) if isinstance(n, int) else SLOT
                pool.wait_ge(hi_done, n + 1)
                nc.gpsimd.tensor_tensor(w_lo[:, r, 0:width], w_raw[:, r, 0:width],
                                        w_hi[:, r, 0:width].bitcast(F32), ALU.subtract).then_inc(lo_done, 1)
            walk(pool, low)

        @block.scalar
        def _(act):
            def w_high(c, i=0, per=0):
                if c >= SLOTS:
                    return
                width, r = slot_width(c), c % RING
                if c >= RING:
                    act.wait_ge(slot_used, c - (RING - 1) + per * i)
                act.wait_ge(raw_loaded[r], 16 * (c // RING + 1 + (per // RING) * i))
                nc.scalar.activation(w_hi[:, r, 0:width], w_raw[:, r, 0:width], ACT.Copy).then_inc(hi_done, 1)

            def step(n, i=0, per=0):
                w_high(n + AHEAD, i, per)

            def finish(norm, k):
                n = norm * KT + k
                if n >= 2:
                    act.wait_ge(sq_added, n - 1)
                nc.scalar.activation(sq[:, k % 2, :], h[:, k, :], ACT.Square).then_inc(sq_ready, 1)
                nc.scalar.activation(operand[norm][0][:, k, :], h[:, k, :], ACT.Copy,
                                     scale=gains[:, n:n + 1]).then_inc(xhi_ready, 1)

            def root(norm):
                act.wait_ge(ms_ready, norm + 1)
                nc.scalar.activation(t_b[:, 1, :], t_b[:, 0, :], ACT.Sqrt).then_inc(root_ready, 1)

            act.dma_start(gains[:], a["gains"]).then_inc(tables_loaded, 16)
            for k in range(KT):
                act.dma_start(h[:, k, :], a["x"][:, k, :]).then_inc(x_loaded[k], 16)
            act.dma_start(rope_t[:], a["rope"]).then_inc(tables_loaded, 16)
            act.dma_start(ident[:], a["ident"]).then_inc(tables_loaded, 16)
            act.dma_start(decay[:], a["decay"]).then_inc(tables_loaded, 16)
            act.wait_ge(tables_loaded, 64)
            for k in range(KT):
                act.wait_ge(x_loaded[k], 16)
                finish(MIX0, k)
                if k < AHEAD:
                    w_high(k)

            def ret_output(i):
                for v in range(VT):
                    act.wait_ge(pv_done, VT * i + v + 1)
                    if v >= 2:
                        act.wait_ge(osq_added, VT * i + v - 1)
                    nc.scalar.activation(sq[:, v % 2, :], ps[:, 4 + v, :], ACT.Square).then_inc(osq_ready, 1)

            def ret_y(i):
                act.wait_ge(hms_ready, i + 1)
                nc.scalar.activation(t_b[:, 1, :], t_b[:, 0, :], ACT.Sqrt).then_inc(hroot_ready, 1)
                for v in range(VT):
                    act.wait_ge(y_val, VT * i + v + 1)
                    nc.scalar.activation(y_hi[:, v, :], sg[:, v, :], ACT.Copy).then_inc(yhi_ready, 1)

            def ret_rotated(i, first):
                for j in range(2):
                    act.wait_ge(qk_rot, 4 * i + first + j + 1)
                    nc.scalar.activation(qk_hi[:, first + j, :], t_a[:, j, :], ACT.Copy).then_inc(qkhi_ready, 1)

            def ret_head(i, n, j, per):
                first = per == 0
                step(n, j, per)
                if first:
                    root(MIX0)
                step(n + 1, j, per)
                if not first:
                    ret_y(i - 1)
                step(n + 2, j, per)
                ret_rotated(i, 0)
                step(n + 3, j, per)
                n += 4
                if not first:
                    step(n, j, per)
                ret_rotated(i, 2)
                if not first:
                    for m in range(1, 4):
                        step(n + m, j, per)
                    n += 4
                for m in range(4):
                    step(n + m, j, per)
                n += 4
                step(n, j, per)
                act.wait_ge(tok_ready, 1)
                for t in range(TT):
                    nc.scalar.activation(v_hi[:, t, :], ps[:, t, :], ACT.Copy,
                                         scale=rstd_tok[:, t:t + 1]).then_inc(vhi_ready, 1)
                for kt in range(TT):
                    act.wait_ge(s_mul, TT * i + kt + 1)
                    nc.scalar.activation(s_hi[:, kt, kt * P:T], tmp[:, kt, kt * P:T],
                                         ACT.Copy).then_inc(shi_ready, 1)
                for v in range(VT):
                    if v + 1 < VT:
                        step(n + v + 1, j, per)
                    act.wait_ge(bank_read, gate_unit(v, j, per) + 1)
                    nc.scalar.activation(t_b[:, v % 2, :], t_a[:, v % 2, :], ACT.Sigmoid).then_inc(sig_ready, 1)
                ret_output(i)

            ret_head(0, 0, 0, 0)
            with act.Fori(1, HEADS) as i:
                ret_head(i, RET_FIRST, i - 1, RET_HEAD)
            n = RET_SLOTS - 4
            for m in range(5):
                if m < 4:
                    step(n + m)
                if m == 0:
                    ret_y(HEADS - 1)
                else:
                    for k in (2 * m - 2, 2 * m - 1):
                        act.wait_ge(bank_read, RET_UNITS - KT + k + 1)
                        finish(MLP0, k)

            def hidden(L, q, m):
                act.wait_ge(bank_read, MLP_UNIT[L] + 2 * KT * q + m + 1)
                done = KT * QUARTERS * L + KT * q + m + 1
                nc.scalar.activation(t_b[:, m % 2, :], t_a[:, m % 2, :], ACT.Square).then_inc(sqr_ready, 1)
                act.wait_ge(sqr_ready, done)
                nc.scalar.activation(hid_hi[:, m, :], t_b[:, m % 2, :], ACT.Copy).then_inc(hidhi_ready, 1)

            def mlp_quarter(L, q, looped, start=None, norm=None):
                for s in range(2 * KT):
                    if looped:
                        step(MLP_BASE[L] + s, q, 2 * KT)
                    else:
                        step(MLP_BASE[L] + 2 * KT * q + s)
                    if start is not None and s == 0:
                        start()
                    if 1 <= s <= KT:
                        hidden(L, q, s - 1)
                    if norm is not None and s > KT:
                        act.wait_ge(bank_read, MLP_UNIT[L] + 2 * KT * q + s)
                        finish(norm, s - KT - 1)
                if norm is not None:
                    act.wait_ge(bank_read, MLP_UNIT[L] + MLP_UNITS)
                    finish(norm, KT - 1)

            def mlp_act(L, mlp_norm, ple_norm, before):
                def start():
                    before()
                    root(mlp_norm)
                mlp_quarter(L, 0, False, start)
                with act.Fori(1, QUARTERS - 1) as q:
                    mlp_quarter(L, q, True)
                mlp_quarter(L, QUARTERS - 1, False, None, ple_norm)

            def ple_act(L, norm, next_norm):
                act.wait_ge(p_loaded[L], 16)
                for f in range(PF):
                    nc.scalar.activation(p_hi[:, f, :], p_raw[:, f, :], ACT.Copy).then_inc(phi_ready, 1)
                m = 0
                for s in range(PLE_SLOTS):
                    step(PLE_BASE[L] + s)
                    if s == 0:
                        root(norm)
                    if s > 0 and s - 1 not in PLE_PROJ:
                        ple_gate(L, m, next_norm)
                        m += 1
                ple_gate(L, m, next_norm)
                if next_norm is not None:
                    act.wait_ge(h_ready, KT * L + KT)
                    finish(next_norm, KT - 1)

            def ple_gate(L, m, next_norm):
                act.wait_ge(bank_read, PLE_UNIT[L] + m + 1)
                nc.scalar.activation(t_b[:, m % 2, :], t_a[:, m % 2, :], ACT.Sigmoid).then_inc(psig_ready, 1)
                if next_norm is not None and m >= 1:
                    act.wait_ge(h_ready, KT * L + m)
                    finish(next_norm, m - 1)

            def load_p(L, slots):
                def go():
                    act.wait_ge(slot_used, slots)
                    act.dma_start(p_raw[:], a["p"][L]).then_inc(p_loaded[L], 16)
                return go

            mlp_act(0, MLP0, PLE0, load_p(0, RET_SLOTS))
            ple_act(0, PLE0, MIX1)

            act.wait_ge(slot_used, MLA_BASE)
            act.dma_start(mrope[:], a["mrope"]).then_inc(mla_loaded, 16)
            act.dma_start(rgain[:], a["rgain"]).then_inc(mla_loaded, 16)
            for s in range(4):
                step(MLA_BASE + s)
            step(MLA_BASE + 4)
            root(MIX1)
            for s in range(5, MLA_IN_SLOTS):
                step(MLA_BASE + s)
            act.wait_ge(bank_read, MLA_UNIT + MLA_IN_UNITS)
            for j, (lo, hi) in enumerate(((0, QR), (QR, QR + KVR))):
                for t in range(TT):
                    if j or t:
                        act.wait_ge(css_ready, 4 * j + t)
                    nc.scalar.activation(sq[:, 0, 0:hi - lo], c_tok[:, t, lo:hi], ACT.Square,
                                         accum_out=small[:, 4 * j + t:4 * j + t + 1]).then_inc(css_ready, 1)
            act.wait_ge(cms_ready, 2)
            nc.scalar.activation(small[:, 16:24], small[:, 8:16], ACT.Sqrt).then_inc(croot_ready, 1)
            for f in range(QF + KVF):
                act.wait_ge(cT_done, f + 1)
                nc.scalar.activation(c_hi[:, f, :], ps[:, 4 + f % 4, :], ACT.Copy,
                                     scale=gains[:, G_QA + f:G_QA + f + 1]).then_inc(chi_ready, 1)

            def qk_transposed(g, which):
                for x in range(GH + 1):
                    act.wait_ge(qkT_done, 6 * g + 3 * which + x + 1)
                    dst, gain = (qT_hi, G_QN) if which == 0 else (kT_hi, G_KN)
                    scale = gains[:, gain:gain + 1] if x < GH else 1.0
                    nc.scalar.activation(dst[:, x, :], ps[:, 4 * which + x, :], ACT.Copy,
                                         scale=scale).then_inc(qkThi_ready, 1)

            def mla_group(g, n, i, per):
                for f in range(MLA_GROUP_SLOTS):
                    step(n + f, i, per)
                for t in range(TT):
                    nc.scalar.activation(q_tok[:, t, :], ps[:, t, 0:GH * QKD], ACT.Copy).then_inc(qtok_ready, 1)
                act.wait_ge(slot_used, n + MLA_GROUP_SLOTS + per * i)
                for t in range(TT):
                    kv = ps[:, 4 + t, :].rearrange("p (h c) -> p h c", h=GH)
                    nc.scalar.activation(k_tok[:, t, :].rearrange("p (h c) -> p h c", h=GH),
                                         kv[:, :, 0:NOPE], ACT.Copy).then_inc(ktok_ready, 1)
                    nc.scalar.activation(mv_hi[:, t, :].rearrange("p (h c) -> p h c", h=GH),
                                         kv[:, :, NOPE:NOPE + VD], ACT.Copy).then_inc(mvhi_ready, 1)
                act.wait_ge(qkms_ready, 2 * g + 1)
                nc.scalar.activation(small[:, 32:40], small[:, 24:32], ACT.Sqrt).then_inc(qkroot_ready, 1)
                qk_transposed(g, 0)
                act.wait_ge(qkms_ready, 2 * g + 2)
                nc.scalar.activation(small[:, 48:56], small[:, 40:48], ACT.Sqrt).then_inc(qkroot_ready, 1)
                qk_transposed(g, 1)

                def exponent(u):
                    hh, b = divmod(u, TT)
                    kend = (b + 1) * P
                    act.wait_ge(nmax_ready, 8 * g + u + 1)
                    if u >= 2:
                        act.wait_ge(pT_done, 8 * g + u - 1)
                    nc.scalar.activation(pr[:, u % 2, 0:kend], ps[:, 4 + u % 2, 0:kend], ACT.Exp,
                                         bias=att[:, 8 + u:9 + u], scale=qscale[:, b * GH + hh:b * GH + hh + 1],
                                         accum_out=att[:, 16 + u:17 + u]).then_inc(exp_ready, 1)

                def transposed(u):
                    b = u % TT
                    act.wait_ge(pT_done, 8 * g + u + 1)
                    nc.scalar.activation(pT_hi[:, 0:b + 1, b * P:(b + 1) * P],
                                         ps[:, 6, 0:(b + 1) * P].rearrange("p (k q) -> p k q", k=b + 1),
                                         ACT.Copy).then_inc(pThi_ready, 1)

                def output(hh):
                    act.wait_ge(o_done, GH * g + hh + 1)
                    nc.scalar.activation(x_hi[:, bass.ds(GH * g + hh, 1), :].rearrange("p a t -> p (a t)"),
                                         ps[:, 7, :], ACT.Copy).then_inc(ohi_ready, 1)

                for u in range(GH * TT):
                    exponent(u)
                    if u == TT + 1:
                        output(0)
                    if u >= 1:
                        transposed(u - 1)
                transposed(GH * TT - 1)
                output(1)

            mla_group(0, MLA_GROUP_BASE, 0, 0)
            with act.Fori(1, GROUPS - 1) as g:
                mla_group(g, MLA_GROUP_BASE + MLA_GROUP_SLOTS, g - 1, MLA_GROUP_SLOTS)
            mla_group(GROUPS - 1, MLA_GROUP_BASE + (GROUPS - 1) * MLA_GROUP_SLOTS, 0, 0)
            for m in range(KT):
                step(MLA_OUT_BASE + m)
                if m >= 1:
                    act.wait_ge(bank_read, MLA_OUT_UNIT + m)
                    finish(MLP1, m - 1)
            act.wait_ge(bank_read, MLA_OUT_UNIT + KT)
            finish(MLP1, KT - 1)

            mlp_act(1, MLP1, PLE1, load_p(1, MLA_BASE + MLA_SLOTS))
            ple_act(1, PLE1, None)

        @block.vector
        def _(dve):
            own = Chain(dve, chain)

            def finish(norm, k):
                n = norm * KT + k
                dve.wait_ge(sq_ready, n + 1)
                if k == 0:
                    nc.vector.tensor_copy(sq_sum[:], sq[:, 0, :]).then_inc(sq_added, 1)
                else:
                    dve.wait_ge(sq_added, n)
                    nc.vector.tensor_tensor(sq_sum[:], sq_sum[:], sq[:, k % 2, :], ALU.add).then_inc(sq_added, 1)
                dve.wait_ge(xhi_ready, n + 1)
                hi, lo = operand[norm]
                nc.vector.scalar_tensor_tensor(lo[:, k, :], h[:, k, :], gains[:, n:n + 1],
                                               hi[:, k, :].bitcast(F32), ALU.mult, ALU.subtract
                                               ).then_inc(x_ready, 1)

            def norm_scale(norm):
                dve.wait_ge(ss_done, norm + 1)
                nc.vector.tensor_scalar(t_b[:, 0, :], ps[:, NORM_BANK, :], 1.0 / D, EPS, ALU.mult,
                                        ALU.add).then_inc(ms_ready, 1)
                dve.wait_ge(root_ready, norm + 1)
                nc.vector.reciprocal(rstd[:], t_b[:, 1, :]).then_inc(rstd_ready, 1)
                if norm in (MIX0, MIX1):
                    dve.wait_ge(tok_done, 1 + (norm == MIX1))
                    nc.vector.tensor_copy(rstd_tok[:], ps[:, NORM_BANK, 0:TT]).then_inc(tok_ready, 1)
                dve.wait_ge(rstd_ready, norm + 1)

            dve.wait_ge(tables_loaded, 64)
            for k in range(KT):
                dve.wait_ge(x_loaded[k], 16)
                finish(MIX0, k)

            def rotate(i, first, unit):
                one, two = ps[:, first, :], ps[:, first + 1, :]
                cos, sin = rope_t[:, 0, :], rope_t[:, 1, :]
                if first:
                    dve.wait_ge(qk_ready, 4 * i + 2)
                own.mark(nc.vector.tensor_tensor(t_a[:, 0, :], one, cos, ALU.mult))
                nc.vector.tensor_tensor(t_b[:, 1, :], one, sin, ALU.mult).then_inc(bank_read, 1)
                own.mark(nc.vector.tensor_tensor(t_b[:, 0, :], two, sin, ALU.mult))
                nc.vector.tensor_tensor(t_a[:, 1, :], two, cos, ALU.mult).then_inc(bank_read, 1)
                own.wait()
                nc.vector.tensor_tensor(t_a[:, 0, :], t_a[:, 0, :], t_b[:, 0, :], ALU.subtract).then_inc(qk_rot, 1)
                dve.wait_ge(bank_read, unit + 2)
                nc.vector.tensor_tensor(t_a[:, 1, :], t_a[:, 1, :], t_b[:, 1, :], ALU.add).then_inc(qk_rot, 1)
                for j in range(2):
                    dve.wait_ge(qkhi_ready, 4 * i + first + j + 1)
                    nc.vector.tensor_tensor(qk_lo[:, first + j, :], t_a[:, j, :],
                                            qk_hi[:, first + j, :].bitcast(F32), ALU.subtract).then_inc(qk_ready, 1)

            def ret_output(i):
                for v in range(VT):
                    dve.wait_ge(osq_ready, VT * i + v + 1)
                    own.mark(nc.vector.tensor_tensor(sg[:, v, :], sg[:, v, :], ps[:, 4 + v, :], ALU.mult))
                    if v == 0:
                        nc.vector.tensor_copy(sq_sum[:], sq[:, 0, :]).then_inc(osq_added, 1)
                    else:
                        dve.wait_ge(osq_added, VT * i + v)
                        nc.vector.tensor_tensor(sq_sum[:], sq_sum[:], sq[:, v % 2, :],
                                                ALU.add).then_inc(osq_added, 1)

            def ret_y(i):
                cols = (gains[:, G_GN + VT * i:G_GN + VT * (i + 1)] if isinstance(i, int)
                        else gains[:, bass.ds(G_GN + VT * i, VT)])
                own.mark(nc.vector.tensor_copy(gn[:], cols))
                dve.wait_ge(hss_done, i + 1)
                nc.vector.tensor_scalar(t_b[:, 0, :], ps[:, NORM_BANK, :], 1.0 / DV, EPS, ALU.mult,
                                        ALU.add).then_inc(hms_ready, 1)
                dve.wait_ge(hroot_ready, i + 1)
                own.mark(nc.vector.reciprocal(t_b[:, 0, :], t_b[:, 1, :]))
                own.wait()

                def low(v):
                    dve.wait_ge(yhi_ready, VT * i + v + 1)
                    nc.vector.tensor_tensor(y_lo[:, v, :], sg[:, v, :], y_hi[:, v, :].bitcast(F32),
                                            ALU.subtract).then_inc(y_ready, 1)
                for v in range(VT):
                    nc.vector.scalar_tensor_tensor(sg[:, v, :], sg[:, v, :], gn[:, v:v + 1], t_b[:, 0, :],
                                                   ALU.mult, ALU.mult).then_inc(y_val, 1)
                    if v >= 1:
                        low(v - 1)
                low(VT - 1)

            def add_to_h(k, bank, unit):
                nc.vector.tensor_tensor(h[:, k, :], h[:, k, :], ps[:, bank, :], ALU.add).then_inc(bank_read, 1)

            def ret_head(i, n, j, per, unit, uper):
                first = per == 0
                n, unit = n + per * j, unit + uper * j
                if first:
                    norm_scale(MIX0)
                    for c in range(2):
                        own.mark(nc.vector.tensor_tensor(rope_t[:, c, :], rope_t[:, c, :], rstd[:], ALU.mult))
                    own.wait()
                else:
                    ret_y(i - 1)
                dve.wait_ge(slot_used, n + 2)
                if not first:
                    dve.wait_ge(y_ready, VT * i)
                rotate(i, 0, unit)
                dve.wait_ge(slot_used, n + 4)
                rotate(i, 2, unit + 2)
                n, unit = n + 4, unit + 4
                if not first:
                    for k in range(KT):
                        dve.wait_ge(slot_used, n + k // 2 + 1)
                        add_to_h(k, k % UB, unit + k)
                    n, unit = n + 4, unit + KT
                n = n + 4
                dve.wait_ge(slot_used, n)
                for t in range(TT):
                    dve.wait_ge(vhi_ready, TT * i + t + 1)
                    nc.vector.scalar_tensor_tensor(v_lo[:, t, :], ps[:, t, :], rstd_tok[:, t:t + 1],
                                                   v_hi[:, t, :].bitcast(F32), ALU.mult, ALU.subtract
                                                   ).then_inc(bank_read, 1)
                unit = unit + TT

                def low(kt):
                    dve.wait_ge(shi_ready, TT * i + kt + 1)
                    nc.vector.tensor_tensor(s_lo[:, kt, kt * P:T], tmp[:, kt, kt * P:T],
                                            s_hi[:, kt, kt * P:T].bitcast(F32), ALU.subtract).then_inc(s_ready, 1)
                for kt in range(TT):
                    w = T - kt * P
                    table = (decay[:, i, 0:w] if isinstance(i, int)
                             else decay[:, bass.ds(i, 1), 0:w].rearrange("p a t -> p (a t)"))
                    dve.wait_ge(s_done, TT * i + kt + 1)
                    nc.vector.tensor_tensor(tmp[:, kt, kt * P:T], ps[:, 4 + kt, 0:w], table,
                                            ALU.mult).then_inc(s_mul, 1)
                    if kt >= 1:
                        low(kt - 1)
                low(TT - 1)

                def silu(v):
                    dve.wait_ge(sig_ready, VT * i + v + 1)
                    own.mark(nc.vector.tensor_tensor(sg[:, v, :], t_a[:, v % 2, :], t_b[:, v % 2, :], ALU.mult))
                dve.wait_ge(s_ready, TT * (i + 1))
                for v in range(VT):
                    dve.wait_ge(slot_used, n + v + 1)
                    if v >= 2:
                        own.wait()
                    nc.vector.tensor_tensor(t_a[:, v % 2, :], ps[:, v, :], rstd[:], ALU.mult).then_inc(bank_read, 1)
                    if v >= 1:
                        silu(v - 1)
                dve.wait_ge(bank_read, unit + VT)
                silu(VT - 1)
                own.wait()
                ret_output(i)

            ret_head(0, 0, 0, 0, 0, 0)
            with dve.Fori(1, HEADS) as i:
                own.enter(i - 1, RET_MARKS)
                ret_head(i, RET_FIRST, i - 1, RET_HEAD, RET_FIRST_UNITS, RET_HEAD_UNITS)
            own.leave(RET_MARKS, HEADS - 1)
            ret_y(HEADS - 1)
            for k in range(KT):
                dve.wait_ge(slot_used, RET_SLOTS - 4 + k // 2 + 1)
                add_to_h(k, k % UB, RET_UNITS - KT + k)
                if k >= 2:
                    finish(MLP0, k - 2)
            finish(MLP0, KT - 2)
            finish(MLP0, KT - 1)

            def mlp_quarter(L, q, norm=None):
                n, unit = MLP_BASE[L] + 2 * KT * q, MLP_UNIT[L] + 2 * KT * q

                def low(m):
                    dve.wait_ge(hidhi_ready, KT * QUARTERS * L + KT * q + m + 1)
                    nc.vector.tensor_tensor(hid_lo[:, m, :], t_b[:, m % 2, :], hid_hi[:, m, :].bitcast(F32),
                                            ALU.subtract).then_inc(hid_ready, 1)
                for m in range(KT):
                    dve.wait_ge(slot_used, n + m + 1)
                    nc.vector.scalar_tensor_tensor(t_a[:, m % 2, :], ps[:, m % UB, :], 0.0, rstd[:],
                                                   ALU.max, ALU.mult).then_inc(bank_read, 1)
                    if m >= 1:
                        low(m - 1)
                low(KT - 1)
                for m in range(KT):
                    dve.wait_ge(slot_used, n + KT + m + 1)
                    add_to_h(m, m % UB, unit + KT + m)
                    if norm is not None and m >= 1:
                        finish(norm, m - 1)
                if norm is not None:
                    finish(norm, KT - 1)

            def ple(L, norm, next_norm):
                for f in range(PF):
                    dve.wait_ge(phi_ready, PF * L + f + 1)
                    nc.vector.tensor_tensor(p_lo[:, f, :], p_raw[:, f, :], p_hi[:, f, :].bitcast(F32),
                                            ALU.subtract).then_inc(p_ready, 1)
                norm_scale(norm)

                def mix(m):
                    dve.wait_ge(slot_used, PLE_BASE[L] + PLE_PROJ[m // 4] + 1)
                    dve.wait_ge(psig_ready, KT * L + m + 1)
                    if m >= 2:
                        dve.wait_ge(h_ready, KT * L + m - 1)
                    own.mark(nc.vector.tensor_tensor(proj[:, m % 2, :], t_b[:, m % 2, :], ps[:, 4 + m % 4, :],
                                                     ALU.mult))
                    own.wait()
                    nc.vector.tensor_tensor(h[:, m, :], h[:, m, :], proj[:, m % 2, :], ALU.add).then_inc(h_ready, 1)
                    if next_norm is not None:
                        finish(next_norm, m)
                for m in range(KT):
                    dve.wait_ge(slot_used, PLE_BASE[L] + PLE_GATE[m] + 1)
                    nc.vector.tensor_tensor(t_a[:, m % 2, :], ps[:, m % UB, :], rstd[:],
                                            ALU.mult).then_inc(bank_read, 1)
                    if m >= 1:
                        mix(m - 1)
                mix(KT - 1)

            def mlp_ple(L, mlp_norm, ple_norm, next_norm):
                norm_scale(mlp_norm)
                with dve.Fori(0, QUARTERS - 1) as q:
                    mlp_quarter(L, q)
                mlp_quarter(L, QUARTERS - 1, ple_norm)
                ple(L, ple_norm, next_norm)

            mlp_ple(0, MLP0, PLE0, MIX1)

            C = QR + KVR + ROPE
            norm_scale(MIX1)
            dve.wait_ge(tok_ready, 2)
            for t in range(TT):
                dve.wait_ge(slot_used, MLA_BASE + 4)
                nc.vector.tensor_scalar(c_tok[:, t, 0:QR], ps[:, t, 0:QR], rstd_tok[:, t:t + 1], None,
                                        ALU.mult).then_inc(bank_read, 1)
            for t in range(TT):
                dve.wait_ge(slot_used, MLA_BASE + 8)
                nc.vector.tensor_scalar(c_tok[:, t, QR:C], ps[:, t, 0:KVR + ROPE], rstd_tok[:, t:t + 1], None,
                                        ALU.mult).then_inc(bank_read, 1)

            def pairs(x, parts):
                return x.rearrange("p t (h c) -> p t h c", h=parts)

            def rotate_tokens(dst, src, parts):
                half = ROPE // 2
                cos = mrope[:, 0, :, :].unsqueeze(2).to_broadcast([P, TT, parts, half])
                sin = mrope[:, 1, :, :].unsqueeze(2).to_broadcast([P, TT, parts, half])
                x1, x2 = src[:, :, :, 0:half], src[:, :, :, half:ROPE]
                m = tmp[:, 2, 0:TT * parts * half].rearrange("p (t h c) -> p t h c", t=TT, h=parts)
                m2 = tmp[:, 3, 0:TT * parts * half].rearrange("p (t h c) -> p t h c", t=TT, h=parts)
                own.mark(nc.vector.tensor_tensor(dst[:, :, :, 0:half], x1, cos, ALU.mult))
                own.mark(nc.vector.tensor_tensor(m, x2, sin, ALU.mult))
                own.mark(nc.vector.tensor_tensor(dst[:, :, :, half:ROPE], x2, cos, ALU.mult))
                own.mark(nc.vector.tensor_tensor(m2, x1, sin, ALU.mult))
                own.wait()
                own.mark(nc.vector.tensor_tensor(dst[:, :, :, 0:half], dst[:, :, :, 0:half], m, ALU.subtract))
                return nc.vector.tensor_tensor(dst[:, :, :, half:ROPE], dst[:, :, :, half:ROPE], m2, ALU.add)

            dve.wait_ge(mla_loaded, 32)
            dve.wait_ge(bank_read, MLA_UNIT + MLA_IN_UNITS)
            kr = c_tok[:, :, QR + KVR:C]
            own.mark(nc.vector.tensor_tensor(r_mul[:, :, 0, :], kr, kr, ALU.mult))
            own.wait()
            own.mark(nc.vector.tensor_reduce(small[:, 56:60], r_mul[:, :, 0, :], AX.X, ALU.add))
            own.mark(nc.vector.tensor_tensor(r_mul[:, :, 1, :], kr,
                                             rgain[:, 1:2, :].to_broadcast([P, TT, ROPE]), ALU.mult))
            own.wait()
            own.mark(rotate_tokens(kr_tok[:].unsqueeze(2), r_mul[:, :, 1:2, :], 1))
            dve.wait_ge(css_ready, 8)
            for j, width in enumerate((QR, KVR)):
                nc.vector.tensor_scalar(small[:, 8 + 4 * j:12 + 4 * j], small[:, 4 * j:4 * j + 4], 1.0 / width, EPS,
                                        ALU.mult, ALU.add).then_inc(cms_ready, 1)
            dve.wait_ge(croot_ready, 1)
            own.mark(nc.vector.reciprocal(small[:, 0:8], small[:, 16:24]))
            own.wait()
            for j, (lo, hi) in enumerate(((0, QR), (QR, QR + KVR))):
                for t in range(TT):
                    nc.vector.tensor_scalar(c_tok[:, t, lo:hi], c_tok[:, t, lo:hi], small[:, 4 * j + t:4 * j + t + 1],
                                            None, ALU.mult).then_inc(cn_ready, 1)
            for f in range(QF + KVF):
                dve.wait_ge(chi_ready, f + 1)
                nc.vector.scalar_tensor_tensor(c_lo[:, f, :], ps[:, 4 + f % 4, :], gains[:, G_QA + f:G_QA + f + 1],
                                               c_hi[:, f, :].bitcast(F32), ALU.mult, ALU.subtract
                                               ).then_inc(c_ready, 1)

            def by_head(x, width):
                return x.rearrange("p (t h) -> p t h", t=TT).unsqueeze(3).to_broadcast([P, TT, GH, width])

            def qk_transposed(g, which):
                for x in range(GH + 1):
                    dve.wait_ge(qkThi_ready, 6 * g + 3 * which + x + 1)
                    hi, lo, gain = (qT_hi, qT_lo, G_QN) if which == 0 else (kT_hi, kT_lo, G_KN)
                    bank = ps[:, 4 * which + x, :]
                    if x < GH:
                        last = nc.vector.scalar_tensor_tensor(lo[:, x, :], bank, gains[:, gain:gain + 1],
                                                              hi[:, x, :].bitcast(F32), ALU.mult, ALU.subtract)
                    else:
                        last = nc.vector.tensor_tensor(lo[:, x, :], bank, hi[:, x, :].bitcast(F32), ALU.subtract)
                    last.then_inc(qkT_ready, 1)

            def mla_group(g):
                dve.wait_ge(qtok_ready, TT * (g + 1))
                q4 = q_tok.rearrange("p t (h c) -> p t h c", h=GH)
                sq4 = tmp[:, :, 0:GH * QKD]
                own.mark(nc.vector.tensor_tensor(sq4, q_tok, q_tok, ALU.mult))
                own.wait()
                own.mark(nc.vector.tensor_reduce(small[:, 24:32].rearrange("p (t h) -> p t h", t=TT),
                                                 sq4.rearrange("p t (h c) -> p t h c", h=GH), AX.X, ALU.add))
                own.wait()
                nc.vector.tensor_scalar(small[:, 24:32], small[:, 24:32], 1.0 / QKD, EPS, ALU.mult,
                                        ALU.add).then_inc(qkms_ready, 1)
                own.mark(nc.vector.tensor_tensor(
                    r_mul[:], q4[:, :, :, NOPE:QKD],
                    rgain[:, 0:1, :].unsqueeze(1).to_broadcast([P, TT, GH, ROPE]), ALU.mult))
                own.wait()
                rotate_tokens(pairs(r_tok[:], GH), r_mul[:], GH).then_inc(qkn_ready, 1)
                dve.wait_ge(qkroot_ready, 2 * g + 1)
                own.mark(nc.vector.reciprocal(qscale[:], small[:, 32:40]))
                own.wait()
                own.mark(nc.vector.tensor_scalar(qscale[:], qscale[:], QKD ** -0.5, None, ALU.mult))
                for t in range(TT):
                    dve.wait_ge(mvhi_ready, TT * g + t + 1)
                    kv = ps[:, 4 + t, :].rearrange("p (h c) -> p h c", h=GH)
                    nc.vector.tensor_tensor(mv_lo[:, t, :].rearrange("p (h c) -> p h c", h=GH),
                                            kv[:, :, NOPE:NOPE + VD],
                                            mv_hi[:, t, :].bitcast(F32).rearrange("p (h c) -> p h c", h=GH),
                                            ALU.subtract).then_inc(mv_ready, 1)
                dve.wait_ge(ktok_ready, TT * (g + 1))
                dve.wait_ge(qkn_ready, 2 * g + 1)
                sk = tmp[:, :, 0:GH * NOPE]
                own.mark(nc.vector.tensor_tensor(sk, k_tok[:], k_tok[:], ALU.mult))
                own.wait()
                own.mark(nc.vector.tensor_reduce(small[:, 40:48].rearrange("p (t h) -> p t h", t=TT),
                                                 sk.rearrange("p t (h c) -> p t h c", h=GH), AX.X, ALU.add))
                own.wait()
                own.mark(nc.vector.tensor_tensor(
                    small[:, 40:48].rearrange("p (t h) -> p t h", t=TT),
                    small[:, 40:48].rearrange("p (t h) -> p t h", t=TT),
                    small[:, 56:60].unsqueeze(2).to_broadcast([P, TT, GH]), ALU.add))
                own.wait()
                nc.vector.tensor_scalar(small[:, 40:48], small[:, 40:48], 1.0 / QKD, EPS, ALU.mult,
                                        ALU.add).then_inc(qkms_ready, 1)
                qk_transposed(g, 0)
                dve.wait_ge(qkroot_ready, 2 * g + 2)
                own.mark(nc.vector.reciprocal(small[:, 48:56], small[:, 48:56]))
                own.wait()
                k4 = k_tok[:].rearrange("p t (h c) -> p t h c", h=GH)
                own.mark(nc.vector.tensor_tensor(k4, k4, by_head(small[:, 48:56], NOPE), ALU.mult))
                nc.vector.tensor_tensor(pairs(r_tok[:], GH),
                                        kr_tok[:].unsqueeze(2).to_broadcast([P, TT, GH, ROPE]),
                                        by_head(small[:, 48:56], ROPE), ALU.mult).then_inc(qkn_ready, 1)
                qk_transposed(g, 1)

                def maximum(u):
                    b = u % TT
                    kend = (b + 1) * P
                    bank = ps[:, 4 + u % 2, :]
                    dve.wait_ge(sc_done, 8 * g + u + 1)
                    own.mark(nc.vector.memset(bank[0:CHUNK, kend - CHUNK:kend], -1e30))
                    own.wait()
                    own.mark(nc.vector.reduce_max(att[:, u:u + 1], bank[:, 0:kend], AX.X))
                    own.wait()
                    col = b * GH + u // TT
                    nc.vector.tensor_scalar(att[:, 8 + u:9 + u], att[:, u:u + 1], qscale[:, col:col + 1], -1.0,
                                            ALU.mult, ALU.mult).then_inc(nmax_ready, 1)

                def normalize(u):
                    kend = (u % TT + 1) * P
                    dve.wait_ge(exp_ready, 8 * g + u + 1)
                    own.mark(nc.vector.reciprocal(att[:, 24 + u:25 + u], att[:, 16 + u:17 + u]))
                    own.wait()
                    nc.vector.tensor_scalar(pr[:, u % 2, 0:kend], pr[:, u % 2, 0:kend], att[:, 24 + u:25 + u], None,
                                            ALU.mult).then_inc(pr_ready, 1)

                def transposed(u):
                    b = u % TT
                    dve.wait_ge(pThi_ready, 8 * g + u + 1)
                    blocks = slice(b * P, (b + 1) * P)
                    nc.vector.tensor_tensor(pT_lo[:, 0:b + 1, blocks],
                                            ps[:, 6, 0:(b + 1) * P].rearrange("p (k q) -> p k q", k=b + 1),
                                            pT_hi[:, 0:b + 1, blocks].bitcast(F32), ALU.subtract
                                            ).then_inc(pT_ready, 1)

                def output(hh):
                    head = GH * g + hh
                    dve.wait_ge(ohi_ready, head + 1)
                    at = (lambda x: x[:, bass.ds(head, 1), :].rearrange("p a t -> p (a t)"))
                    nc.vector.tensor_tensor(at(x_lo), ps[:, 7, :], at(x_hi).bitcast(F32), ALU.subtract
                                            ).then_inc(o_ready, 1)

                for u in range(GH * TT):
                    maximum(u)
                    if u >= 1:
                        normalize(u - 1)
                    if u == TT + 2:
                        output(0)
                    if u >= 2:
                        transposed(u - 2)
                normalize(GH * TT - 1)
                transposed(GH * TT - 2)
                transposed(GH * TT - 1)
                output(1)

            with dve.Fori(0, GROUPS) as g:
                own.enter(g, MLA_MARKS)
                mla_group(g)
            own.leave(MLA_MARKS, GROUPS)
            for k in range(KT):
                dve.wait_ge(slot_used, MLA_OUT_BASE + k + 1)
                add_to_h(k, k % UB, MLA_OUT_UNIT + k)
                if k >= 1:
                    finish(MLP1, k - 1)
            finish(MLP1, KT - 1)

            mlp_ple(1, MLP1, PLE1, None)

        @block.tensor
        def _(pe):
            def product(out, st, mv, start, stop):
                nc.tensor.matmul(out, st[0], mv[1], start=start, stop=False)
                nc.tensor.matmul(out, st[1], mv[0], start=False, stop=False)
                return nc.tensor.matmul(out, st[0], mv[0], start=False, stop=stop)

            def weights(n, lo, hi):
                return w_hi[:, n % RING, lo:hi], w_lo[:, n % RING, lo:hi]

            def arrived(n):
                pe.wait_ge(lo_done, n + 1)

            def bank_free(unit):
                if not isinstance(unit, int) or unit >= UB:
                    pe.wait_ge(bank_read, unit - (UB - 1))

            def both(hi, lo, k, cols=slice(0, T)):
                return hi[:, k, cols], lo[:, k, cols]

            def tile_of(n, bank, operand, k, width=P, base=0, last=KT - 1):
                return product(ps[:, bank, :], weights(n, base + k * width, base + (k + 1) * width),
                               both(*operand, k), k == 0, k == last)

            def linear(n, i, per, unit, uper, count, operand, ready=None, mid=None):
                off, uoff = per * i, uper * i
                for m in range(2):
                    arrived(n + m + off)
                    bank_free(unit + m + uoff)
                    for k in range(KT - 1):
                        if m == 0 and ready:
                            ready(k)
                        tile_of(n + m, (unit + m) % UB, operand, k)
                if ready:
                    ready(KT - 1)
                for m in range(2):
                    tile_of(n + m, (unit + m) % UB, operand, KT - 1).then_inc(slot_used, 1)
                if mid:
                    mid()
                for m in range(2, count):
                    arrived(n + m + off)
                    bank_free(unit + m + uoff)
                    for k in range(KT):
                        last = tile_of(n + m, (unit + m) % UB, operand, k)
                    last.then_inc(slot_used, 1)

            def square_sum(norm):
                pe.wait_ge(sq_added, KT * (norm + 1))
                nc.tensor.matmul(ps[:, NORM_BANK, :], ones[:], sq_sum[:], start=True, stop=True).then_inc(ss_done, 1)

            def turn_rstd(norm):
                pe.wait_ge(rstd_ready, norm + 1)
                for t in range(TT):
                    last = nc.tensor.matmul(ps[:, NORM_BANK, t:t + 1], rstd[0:1, t * P:(t + 1) * P],
                                            ones[0:1, 0:1], start=True, stop=True)
                last.then_inc(tok_done, 1)

            def x_tile(norm):
                return lambda k: pe.wait_ge(x_ready, KT * norm + k + 1)

            pe.wait_ge(ones_set, 1)

            def head_square_sum(i):
                pe.wait_ge(osq_added, VT * (i + 1))
                nc.tensor.matmul(ps[:, NORM_BANK, :], ones[:], sq_sum[:], start=True, stop=True).then_inc(hss_done, 1)

            def ret_out(i, n, off, unit, uoff):
                for m in range(KT):
                    if m % 2 == 0:
                        arrived(n + m // 2 + off)
                    bank_free(unit + m + uoff)
                    for k in range(VT):
                        if m == 0:
                            pe.wait_ge(y_ready, VT * i + k + 1)
                        last = tile_of(n + m // 2, (unit + m) % UB, (y_hi, y_lo), k, base=(m % 2) * VT * P,
                                       last=VT - 1)
                    if m % 2:
                        last.then_inc(slot_used, 1)

            def ret_head(i, n, j, per, unit, uper):
                first = per == 0
                off, uoff = per * j, uper * j

                def norms():
                    if first:
                        square_sum(MIX0)
                    else:
                        head_square_sum(i - 1)
                linear(n, j, per, unit, uper, 4, operand[MIX0], x_tile(MIX0), norms)
                n, unit = n + 4, unit + 4
                if first:
                    turn_rstd(MIX0)
                else:
                    ret_out(i - 1, n, off, unit, uoff)
                    n, unit = n + 4, unit + KT
                for t in range(TT):
                    bank_free(unit + t + uoff)
                for s in range(4):
                    arrived(n + s + off)
                    for kk in range(2):
                        k = 2 * s + kk
                        for t in range(TT):
                            last = product(ps[:, t, :], both(x_hi, x_lo, k, slice(t * P, (t + 1) * P)),
                                           weights(n + s, kk * DV, (kk + 1) * DV), k == 0, k == KT - 1)
                    last.then_inc(slot_used, 1)
                n, unit = n + 4, unit + 4
                pe.wait_ge(qk_ready, 4 * (i + 1))
                if first:
                    pe.wait_ge(tok_ready, 1)
                else:
                    pe.wait_ge(osq_added, VT * i)
                    pe.wait_ge(hms_ready, i)
                for kt in range(TT):
                    for c in range(2):
                        last = product(ps[:, 4 + kt, 0:T - kt * P],
                                       both(qk_hi, qk_lo, 2 + c, slice(kt * P, (kt + 1) * P)),
                                       both(qk_hi, qk_lo, c, slice(kt * P, T)), c == 0, c == 1)
                    last.then_inc(s_done, 1)
                for v in range(VT):
                    arrived(n + v + off)
                    bank_free(unit + v + uoff)
                    for k in range(KT):
                        last = tile_of(n + v, (unit + v) % UB, operand[MIX0], k)
                    last.then_inc(slot_used, 1)
                pe.wait_ge(s_ready, TT * (i + 1))
                for v in range(VT):
                    for kt in range(TT):
                        last = product(ps[:, 4 + v, kt * P:T],
                                       both(v_hi, v_lo, kt, slice(v * P, (v + 1) * P)),
                                       both(s_hi, s_lo, kt, slice(kt * P, T)), kt == 0, kt == TT - 1)
                    last.then_inc(pv_done, 1)

            ret_head(0, 0, 0, 0, 0, 0)
            with pe.Fori(1, HEADS) as i:
                ret_head(i, RET_FIRST, i - 1, RET_HEAD, RET_FIRST_UNITS, RET_HEAD_UNITS)
            head_square_sum(HEADS - 1)
            ret_out(HEADS - 1, RET_SLOTS - 4, 0, RET_UNITS - KT, 0)

            def mlp_quarter(L, norm, q, mid=None):
                linear(MLP_BASE[L], q, 2 * KT, MLP_UNIT[L], 2 * KT, KT, operand[norm],
                       x_tile(norm), mid)
                linear(MLP_BASE[L] + KT, q, 2 * KT, MLP_UNIT[L] + KT, 2 * KT, KT, (hid_hi, hid_lo),
                       lambda k: pe.wait_ge(hid_ready, KT * QUARTERS * L + KT * q + k + 1))

            def ple(L, norm):
                for pos in range(PLE_SLOTS):
                    n = PLE_BASE[L] + pos
                    if pos == 0:
                        linear(n, 0, 0, PLE_UNIT[L], 0, 2, operand[norm], x_tile(norm),
                               lambda: square_sum(norm))
                    elif pos in PLE_PROJ:
                        half = PLE_PROJ.index(pos)
                        arrived(n)
                        if half == 0:
                            pe.wait_ge(p_ready, PF * (L + 1))
                            pe.wait_ge(rstd_ready, norm + 1)
                        for m in range(4):
                            if half:
                                pe.wait_ge(h_ready, KT * L + m + 1)
                            for k in range(PF):
                                last = tile_of(n, 4 + m, (p_hi, p_lo), k, base=m * PF * P, last=PF - 1)
                        last.then_inc(slot_used, 1)
                    elif pos >= 2:
                        unit = PLE_UNIT[L] + PLE_GATE.index(pos)
                        arrived(n)
                        bank_free(unit)
                        for k in range(KT):
                            last = tile_of(n, unit % UB, operand[norm], k)
                        last.then_inc(slot_used, 1)

            def mlp_ple(L, mlp_norm, ple_norm):
                mlp_quarter(L, mlp_norm, 0, lambda: square_sum(mlp_norm))
                with pe.Fori(1, QUARTERS) as q:
                    mlp_quarter(L, mlp_norm, q)
                ple(L, ple_norm)

            mlp_ple(0, MLP0, PLE0)

            for part, width in enumerate((QR, KVR + ROPE)):
                for t in range(TT):
                    bank_free(MLA_UNIT + 4 * part + t)
                for s in range(4):
                    n = MLA_BASE + 4 * part + s
                    arrived(n)
                    for kk in range(2):
                        k = 2 * s + kk
                        if part == 0:
                            pe.wait_ge(x_ready, KT * MIX1 + k + 1)
                        for t in range(TT):
                            last = product(ps[:, t, 0:width], both(*operand[MIX1], k, slice(t * P, (t + 1) * P)),
                                           weights(n, kk * width, (kk + 1) * width), k == 0, k == KT - 1)
                    last.then_inc(slot_used, 1)
                if part == 0:
                    square_sum(MIX1)
                    turn_rstd(MIX1)
            pe.wait_ge(cn_ready, 8)
            pe.wait_ge(tok_ready, 2)
            for f in range(QF + KVF):
                if f >= 4:
                    pe.wait_ge(c_ready, f - 3)
                for t in range(TT):
                    last = nc.tensor.transpose(ps[:, 4 + f % 4, t * P:(t + 1) * P], c_tok[:, t, f * P:(f + 1) * P],
                                               ident[:])
                last.then_inc(cT_done, 1)
            pe.wait_ge(c_ready, QF + KVF)

            def mla_group(g):
                n = MLA_GROUP_BASE
                off = MLA_GROUP_SLOTS * g
                for f in range(QF):
                    arrived(n + f + off)
                    for t in range(TT):
                        last = product(ps[:, t, 0:GH * QKD], both(c_hi, c_lo, f, slice(t * P, (t + 1) * P)),
                                       weights(n + f, 0, GH * QKD), f == 0, f == QF - 1)
                    last.then_inc(slot_used, 1)
                arrived(n + QF + off)
                for f in range(KVF):
                    for t in range(TT):
                        last = product(ps[:, 4 + t, :], both(c_hi, c_lo, QF + f, slice(t * P, (t + 1) * P)),
                                       weights(n + QF, f * T, (f + 1) * T), f == 0, f == KVF - 1)
                last.then_inc(slot_used, 1)
                pe.wait_ge(qtok_ready, TT * (g + 1))
                for which in range(2):
                    pe.wait_ge(qkn_ready, 2 * g + which + 1)
                    if which:
                        pe.wait_ge(mv_ready, TT * (g + 1))
                    for xx in range(GH + 1):
                        for t in range(TT):
                            if xx == GH:
                                src = r_tok[:, t, :]
                            elif which == 0:
                                src = q_tok[:, t, xx * QKD:xx * QKD + NOPE]
                            else:
                                src = k_tok[:, t, xx * NOPE:(xx + 1) * NOPE]
                            last = nc.tensor.transpose(ps[:, 4 * which + xx, t * P:(t + 1) * P], src, ident[:])
                        last.then_inc(qkT_done, 1)
                pe.wait_ge(qkT_ready, 6 * (g + 1))

                def scores(u):
                    hh, b = divmod(u, TT)
                    kend = (b + 1) * P
                    if u >= 2:
                        pe.wait_ge(exp_ready, 8 * g + u - 1)
                    rows, cols = slice(hh * ROPE, (hh + 1) * ROPE), slice(b * P, (b + 1) * P)
                    product(ps[:, 4 + u % 2, 0:kend], both(qT_hi, qT_lo, hh, cols),
                            both(kT_hi, kT_lo, hh, slice(0, kend)), True, False)
                    product(ps[:, 4 + u % 2, 0:kend],
                            (qT_hi[rows, GH, cols], qT_lo[rows, GH, cols]),
                            (kT_hi[rows, GH, 0:kend], kT_lo[rows, GH, 0:kend]), False, True).then_inc(sc_done, 1)

                def transpose_probs(u):
                    pe.wait_ge(pr_ready, 8 * g + u + 1)
                    if u >= 1:
                        pe.wait_ge(pT_ready, 8 * g + u)
                    for kt in range(u % TT + 1):
                        last = nc.tensor.transpose(ps[:, 6, kt * P:(kt + 1) * P], pr[:, u % 2, kt * P:(kt + 1) * P],
                                                   ident[:])
                    last.then_inc(pT_done, 1)

                def output(hh):
                    pe.wait_ge(pT_ready, 8 * g + TT * (hh + 1))
                    if hh:
                        pe.wait_ge(o_ready, GH * g + hh)
                    for kt in range(TT):
                        last = product(ps[:, 7, kt * P:T], both(mv_hi, mv_lo, kt, slice(hh * VD, (hh + 1) * VD)),
                                       both(pT_hi, pT_lo, kt, slice(kt * P, T)), kt == 0, kt == TT - 1)
                    last.then_inc(o_done, 1)

                for u in range(GH * TT):
                    scores(u)
                    if u >= 1:
                        transpose_probs(u - 1)
                    if u == TT + 1:
                        output(0)
                transpose_probs(GH * TT - 1)
                output(1)
                pe.wait_ge(o_ready, GH * (g + 1))

            with pe.Fori(0, GROUPS) as g:
                mla_group(g)
            linear(MLA_OUT_BASE, 0, 0, MLA_OUT_UNIT, 0, KT, (x_hi, x_lo))

            mlp_ple(1, MLP1, PLE1)


def rotary(seq, dim):
    inv = np.float32(1.0) / (np.float32(10000.0) ** (np.arange(0, dim, 2, dtype=np.float32) / np.float32(dim)))
    angle = np.arange(seq, dtype=np.float32)[:, None] * inv[None, :]
    return np.cos(angle), np.sin(angle)


def decay_tables():
    gamma_log = np.log(1.0 - 2.0 ** (-5.0 - np.arange(HEADS)))
    p, x = np.arange(P)[:, None], np.arange(T)[None, :]
    seen = x // CHUNK >= p // CHUNK
    table = np.exp(gamma_log[None, :, None] * np.abs(x - p)[:, None, :]) * seen[:, None, :]
    return (table * DK ** -0.5).astype(np.float32)


def std_slots(w):
    k, m = w.shape
    return w.reshape(k // P, P, m // P, P).transpose(2, 1, 0, 3).reshape(m // P, P, k)


def wide_slots(w, rows):
    k, m = w.shape
    return w.reshape(k // P // rows, rows, P, m).transpose(0, 2, 1, 3).reshape(-1, P, rows * m)


def columns(v):
    return v.reshape(-1, P).T


def lay_out(inputs):
    def tiles(x):
        return x.T.reshape(-1, P, x.shape[0]).transpose(1, 0, 2)

    w = {k: np.asarray(v) for k, v in inputs.items()}
    w_in, w_out = w["ret_w_in"][0], w["ret_w_out"][0]
    q, k, v, gate = np.split(w_in, [D, 2 * D, 2 * D + HEADS * DV], axis=1)

    def head_out(i):
        return w_out[i * DV:(i + 1) * DV].reshape(VT, P, KT // 2, 2, P).transpose(2, 1, 3, 0, 4).reshape(-1, P, SLOT)

    def mlp_ple(L):
        parts = []
        w1, w2 = w["mlp_w1"][L], w["mlp_w2"][L]
        for c in range(QUARTERS):
            parts += [std_slots(w1[:, c * D:(c + 1) * D]), std_slots(w2[c * D:(c + 1) * D])]
        gates = std_slots(w["ple_gate_w"][L])
        pp = w["ple_proj_w"][L].reshape(PF, P, 2, 4, P).transpose(2, 1, 3, 0, 4).reshape(2, P, SLOT)
        for pos in range(PLE_SLOTS):
            parts.append(pp[PLE_PROJ.index(pos)][None] if pos in PLE_PROJ else gates[PLE_GATE.index(pos)][None])
        return parts

    parts = []
    for i in range(HEADS):
        dk, dv = slice(i * DK, (i + 1) * DK), slice(i * DV, (i + 1) * DV)
        parts += [std_slots(q[:, dk]), std_slots(k[:, dk])]
        if i:
            parts.append(head_out(i - 1))
        parts += [wide_slots(v[:, dv], 2), std_slots(gate[:, dv])]
    parts.append(head_out(HEADS - 1))
    mla_in, uq, ukv = w["mla_w_in"][0], w["mla_w_uq"][0], w["mla_w_ukv"][0]
    gq, gkv = GH * QKD, GH * (NOPE + VD)
    qn, kn = w["mla_q_norm"][0], w["mla_k_norm"][0]
    gains = [w[name][L] for L in range(2) for name in ("mix_norm", "mlp_norm", "ple_norm")]
    gains += [w["ret_gn"][0].reshape(-1), w["mla_q_a_norm"][0], w["mla_kv_a_norm"][0], qn[:NOPE], kn[:NOPE]]
    cos, sin = rotary(T, DK)
    mcos, msin = rotary(T, ROPE)
    mrope = np.stack([mcos, msin]).reshape(2, TT, P, ROPE // 2).transpose(2, 0, 1, 3)
    out = {
        "x": tiles(w["x"][0]),
        "p": np.stack([tiles(w["p"][L, 0]) for L in range(2)]),
        "gains": np.concatenate([columns(g) for g in gains], axis=1),
        "rope": np.stack([cos.T, sin.T], axis=1),
        "decay": decay_tables(),
        "ident": np.eye(P, dtype=np.float32),
        "mrope": mrope,
        "rgain": np.broadcast_to(np.stack([qn[NOPE:], kn[NOPE:]])[None], (P, 2, ROPE)),
        "weights0": np.concatenate(parts + mlp_ple(0)),
        "weights1": np.concatenate(mlp_ple(1)),
        "mla_in_q": wide_slots(mla_in[:, :QR], 2),
        "mla_in_kv": wide_slots(mla_in[:, QR:], 2),
        "mla_uq": np.concatenate([wide_slots(uq[:, c * gq:(c + 1) * gq], 1) for c in range(GROUPS)]),
        "mla_ukv": np.concatenate([wide_slots(ukv[:, c * gkv:(c + 1) * gkv], 2) for c in range(GROUPS)]),
        "mla_out": std_slots(w["mla_w_out"][0]),
    }
    return {name: np.ascontiguousarray(v) for name, v in out.items()}


def kernel(**inputs):
    import concourse.bacc as bacc
    from concourse.bass_utils import run_bass_kernel_spmd

    nc = bacc.Bacc("TRN2", target_bir_lowering=False, num_devices=1)
    arrays = lay_out(inputs)
    aps = {name: nc.dram_tensor("in_" + name, v.shape, F32, kind="ExternalInput").ap() for name, v in arrays.items()}
    aps["out"] = nc.dram_tensor("out", (P, KT, T), F32, kind="ExternalOutput").ap()
    build(nc, aps)
    got = run_bass_kernel_spmd(nc, [{"in_" + name: v for name, v in arrays.items()}], core_ids=[0]).results[0]["out"]
    return got.transpose(2, 1, 0).reshape(1, T, D)
```

```python
from contextlib import ExitStack

import numpy as np

import concourse.bass as bass
from concourse import mybir
from concourse.alu_op_type import AluOpType as ALU

F32 = mybir.dt.float32
F32R = mybir.dt.float32r
ACT = mybir.ActivationFunctionType
AX = mybir.AxisListType

P = 128
D = 1024
T = 512
KT = D // P
TT = T // P
CHUNK = 64
EPS = 1e-6
RING = 4
AHEAD = 3
SLOT = 1024

HEADS = 4
DK = D // HEADS
DV = 2 * DK
VT = DV // P

MH = 8
NOPE, ROPE, VD = 128, 64, 128
QKD = NOPE + ROPE
QR, KVR = 384, 256
QF, KVF = QR // P, KVR // P
PLE = 256
PF = PLE // P
QUARTERS = 4

RET_FIRST = 12
RET_HEAD = 16
RET_SLOTS = RET_FIRST + (HEADS - 1) * RET_HEAD + 4
MLP_SLOTS = QUARTERS * 2 * KT
PLE_SLOTS = KT + 2
LAYER0_SLOTS = RET_SLOTS + MLP_SLOTS + PLE_SLOTS
MLA_IN_SLOTS = 8
MLA_HEAD_SLOTS = 2
MLA_SLOTS = MLA_IN_SLOTS + MH * MLA_HEAD_SLOTS + KT
LAYER1_SLOTS = MLP_SLOTS + PLE_SLOTS
MLA_BASE = LAYER0_SLOTS
MLA_HEAD_BASE = MLA_BASE + MLA_IN_SLOTS
MLA_OUT_BASE = MLA_HEAD_BASE + MH * MLA_HEAD_SLOTS
MLP_BASE = (RET_SLOTS, MLA_BASE + MLA_SLOTS)
PLE_BASE = (MLP_BASE[0] + MLP_SLOTS, MLP_BASE[1] + MLP_SLOTS)
SLOTS = PLE_BASE[1] + PLE_SLOTS
assert SLOTS == LAYER0_SLOTS + MLA_SLOTS + LAYER1_SLOTS

RET_FIRST_UNITS = 12
RET_HEAD_UNITS = 20
RET_UNITS = RET_FIRST_UNITS + (HEADS - 1) * RET_HEAD_UNITS + KT
MLP_UNITS = MLP_SLOTS
PLE_UNITS = KT
MLA_IN_UNITS = 8
MLP_UNIT = (RET_UNITS, RET_UNITS + MLP_UNITS + PLE_UNITS + MLA_IN_UNITS + KT)
PLE_UNIT = (MLP_UNIT[0] + MLP_UNITS, MLP_UNIT[1] + MLP_UNITS)
MLA_UNIT = PLE_UNIT[0] + PLE_UNITS
MLA_OUT_UNIT = MLA_UNIT + MLA_IN_UNITS
UB = 4
NORM_BANK = 7

MIX0, MLP0, PLE0, MIX1, MLP1, PLE1 = range(6)
G_GN = 6 * KT
G_QA = G_GN + HEADS * VT
G_KVA = G_QA + QF
G_QN = G_KVA + KVF
G_KN = G_QN + 1
GAINS = G_KN + 1


PLE_PROJ = (2, 7)
PLE_GATE = tuple(s for s in range(KT + 2) if s not in PLE_PROJ)


def gate_unit(v, j, per):
    return RET_FIRST_UNITS - VT + v + (RET_HEAD_UNITS * (j + 1) if per else 0)


def slot_width(n):
    if MLA_BASE <= n < MLA_HEAD_BASE:
        return 2 * QR if n < MLA_BASE + 4 else 2 * (KVR + ROPE)
    if MLA_HEAD_BASE <= n < MLA_OUT_BASE:
        return KVF * (NOPE + VD) if (n - MLA_HEAD_BASE) % MLA_HEAD_SLOTS else QF * QKD
    return SLOT


RET_MARKS = 14
ATT_MARKS = 12
POOL_MARKS = 9


class Chain:

    def __init__(self, engine, sem):
        self.engine, self.sem, self.base, self.local = engine, sem, 0, 0

    def mark(self, ins):
        ins.then_inc(self.sem, 1)
        self.local += 1

    def wait(self):
        self.engine.wait_ge(self.sem, self.base + self.local)

    def enter(self, i, per):
        self.outer = self.base + self.local
        self.base, self.local = self.outer + per * i, 0

    def leave(self, per, turns):
        assert self.local == per, self.local
        self.base, self.local = self.outer + per * turns, 0


def build(nc, a):
    with ExitStack() as ctx:
        def sb(name, shape, dt=F32, scope=ctx):
            return scope.enter_context(nc.sbuf_tensor(name, shape, dt))

        def sem(name):
            return ctx.enter_context(nc.semaphore(name))

        h = sb("h", [P, KT, T])
        x_hi = sb("x_hi", [P, KT, T], F32R)
        x_lo = sb("x_lo", [P, KT, T], F32R)
        w_raw = sb("w_raw", [P, RING, SLOT])
        w_hi = sb("w_hi", [P, RING, SLOT], F32R)
        w_lo = sb("w_lo", [P, RING, SLOT], F32R)
        gains = sb("gains", [P, GAINS])
        ident = sb("ident", [P, P])
        ones = sb("ones", [P, P])
        sq = sb("sq", [P, 2, T])
        sq_sum = sb("sq_sum", [P, T])
        rstd = sb("rstd", [P, T])
        rstd_tok = sb("rstd_tok", [P, TT])
        tmp = sb("tmp", [P, 4, T])
        t_a, t_b = tmp[:, 0:2, :], tmp[:, 2:4, :]

        with ExitStack() as ret:
            qk_hi = sb("qk_hi", [P, 4, T], F32R, ret)
            qk_lo = sb("qk_lo", [P, 4, T], F32R, ret)
            s_hi = sb("s_hi", [P, TT, T], F32R, ret)
            s_lo = sb("s_lo", [P, TT, T], F32R, ret)
            v_hi = sb("v_hi", [P, TT, DV], F32R, ret)
            v_lo = sb("v_lo", [P, TT, DV], F32R, ret)
            y_hi = sb("y_hi", [P, VT, T], F32R, ret)
            y_lo = sb("y_lo", [P, VT, T], F32R, ret)
            sg = sb("sg", [P, VT, T], F32, ret)
            decay = sb("decay", [P, HEADS, T], F32, ret)
            rope_t = sb("rope_t", [P, 2, T], F32, ret)
            gn = sb("gn", [P, VT], F32, ret)
        with ExitStack() as mlp:
            x2_hi = sb("x2_hi", [P, KT, T], F32R, mlp)
            x2_lo = sb("x2_lo", [P, KT, T], F32R, mlp)
            hid_hi = sb("hid_hi", [P, KT, T], F32R, mlp)
            hid_lo = sb("hid_lo", [P, KT, T], F32R, mlp)
            p_raw = sb("p_raw", [P, PF, T], F32, mlp)
            p_hi = sb("p_hi", [P, PF, T], F32R, mlp)
            p_lo = sb("p_lo", [P, PF, T], F32R, mlp)
            proj = sb("proj", [P, 2, T], F32, mlp)
        with ExitStack() as mla:
            qT_hi = sb("qT_hi", [P, 3, T], F32R, mla)
            qT_lo = sb("qT_lo", [P, 3, T], F32R, mla)
            kT_hi = sb("kT_hi", [P, 3, T], F32R, mla)
            kT_lo = sb("kT_lo", [P, 3, T], F32R, mla)
            mv_hi = sb("mv_hi", [P, 2, TT, VD], F32R, mla)
            mv_lo = sb("mv_lo", [P, 2, TT, VD], F32R, mla)
            pT_hi = sb("pT_hi", [P, TT, T], F32R, mla)
            pT_lo = sb("pT_lo", [P, TT, T], F32R, mla)
            c_hi = sb("c_hi", [P, QF + KVF, T], F32R, mla)
            c_lo = sb("c_lo", [P, QF + KVF, T], F32R, mla)
            c_tok = sb("c_tok", [P, TT, QR + KVR + ROPE], F32, mla)
            q_tok = c_tok[:, :, 0:QKD]
            k_tok = sb("k_tok", [P, TT, NOPE], F32, mla)
            rq_tok = sb("rq_tok", [P, TT, 2 * ROPE], F32, mla)
            rk_tok = sb("rk_tok", [P, TT, 2 * ROPE], F32, mla)
            kr_tok = sb("kr_tok", [P, TT, ROPE], F32, mla)
            qg_tok = sb("qg_tok", [P, TT, ROPE], F32, mla)
            mrope = sb("mrope", [P, 2, TT, ROPE // 2], F32, mla)
            rgain = sb("rgain", [P, 2, ROPE], F32, mla)
            half_neg = sb("half_neg", [P, TT], F32, mla)
            eps_sum = sb("eps_sum", [P, TT], F32, mla)
            per_qkd = sb("per_qkd", [P, TT], F32, mla)
            small = sb("small", [P, 32], F32, mla)
            q_ss = sb("q_ss", [P, TT], F32, mla)
            k_ss = sb("k_ss", [P, TT], F32, mla)
            kr_ss = sb("kr_ss", [P, TT], F32, mla)
            q_ms = sb("q_ms", [P, TT], F32, mla)
            k_ms = sb("k_ms", [P, TT], F32, mla)
            k_rs = sb("k_rs", [P, TT], F32, mla)
            qscale = sb("qscale", [P, 2, TT], F32, mla)
            att = sb("att", [P, 4, 8], F32, mla)
            pr = sb("pr", [P, 2, T], F32, mla)

        ps = ctx.enter_context(nc.psum_tensor("ps", [P, 8, 512], F32))

        operand = {n: (x2_hi, x2_lo) if n in (MIX1, MLP1) else (x_hi, x_lo) for n in range(6)}

        raw_loaded = [sem(f"raw_loaded{r}") for r in range(RING)]
        hi_done = sem("hi_done")
        lo_done = sem("lo_done")
        slot_used = sem("slot_used")
        bank_read = sem("bank_read")
        ones_set = sem("ones_set")
        x_loaded = [sem(f"x_loaded{k}") for k in range(KT)]
        tables_loaded = sem("tables_loaded")
        sq_ready = sem("sq_ready")
        sq_added = sem("sq_added")
        xhi_ready = sem("xhi_ready")
        x_ready = sem("x_ready")
        ss_done = sem("ss_done")
        ms_ready = sem("ms_ready")
        root_ready = sem("root_ready")
        rstd_ready = sem("rstd_ready")
        tok_done = sem("tok_done")
        tok_ready = sem("tok_ready")
        h_ready = sem("h_ready")
        chain = sem("chain")
        out_stored = sem("out_stored")
        qk_rot = sem("qk_rot")
        qkhi_ready = sem("qkhi_ready")
        qk_ready = sem("qk_ready")
        vhi_ready = sem("vhi_ready")
        s_done = sem("s_done")
        s_mul = sem("s_mul")
        shi_ready = sem("shi_ready")
        s_ready = sem("s_ready")
        sig_ready = sem("sig_ready")
        pv_done = sem("pv_done")
        osq_ready = sem("osq_ready")
        osq_added = sem("osq_added")
        hss_done = sem("hss_done")
        hms_ready = sem("hms_ready")
        hroot_ready = sem("hroot_ready")
        y_val = sem("y_val")
        yhi_ready = sem("yhi_ready")
        y_ready = sem("y_ready")
        sqr_ready = sem("sqr_ready")
        hidhi_ready = sem("hidhi_ready")
        hid_ready = sem("hid_ready")
        p_loaded = [sem(f"p_loaded{l}") for l in range(2)]
        phi_ready = sem("phi_ready")
        p_ready = sem("p_ready")
        psig_ready = sem("psig_ready")
        mla_loaded = sem("mla_loaded")
        css_ready = sem("css_ready")
        cms_ready = sem("cms_ready")
        croot_ready = sem("croot_ready")
        cn_ready = sem("cn_ready")
        cT_done = sem("cT_done")
        chi_ready = sem("chi_ready")
        c_ready = sem("c_ready")
        kr_ready = sem("kr_ready")
        qtok_ready = sem("qtok_ready")
        ktok_ready = sem("ktok_ready")
        mvhi_ready = sem("mvhi_ready")
        mv_ready = sem("mv_ready")
        pool_chain = sem("pool_chain")
        qscale_ready = sem("qscale_ready")
        qkn_ready = sem("qkn_ready")
        qkT_done = sem("qkT_done")
        qkThi_ready = sem("qkThi_ready")
        qkT_ready = sem("qkT_ready")
        sc_done = sem("sc_done")
        nmax_ready = sem("nmax_ready")
        exp_ready = sem("exp_ready")
        pr_ready = sem("pr_ready")
        pT_done = sem("pT_done")
        pThi_ready = sem("pThi_ready")
        pT_ready = sem("pT_ready")
        o_done = sem("o_done")
        ohi_ready = sem("ohi_ready")
        o_ready = sem("o_ready")

        block = ctx.enter_context(nc.Block())

        def mla_source(n):
            s = n - MLA_BASE
            if s < 4:
                return a["mla_in_q"][s]
            if s < MLA_IN_SLOTS:
                return a["mla_in_kv"][s - 4]
            s = n - MLA_HEAD_BASE
            if s < MH * MLA_HEAD_SLOTS:
                return a["mla_ukv"][s // 2] if s % 2 else a["mla_uq"][s // 2]
            return a["mla_out"][n - MLA_OUT_BASE]

        def walk(engine, one, w, first, count):
            head = RING if first == 0 else -first % RING
            for j in range(head):
                one(first + j, (first + j) % RING, w[j], (first + j) // RING)
            turns = (count - head) // RING
            with engine.Fori(0, turns) as i:
                for r in range(RING):
                    one(first + head + r + RING * i, r,
                        w[bass.ds(head + r + RING * i, 1)].rearrange("a p n -> (a p) n"),
                        (first + head) // RING + i)
            for j in range(head + turns * RING, count):
                one(first + j, (first + j) % RING, w[j], (first + j) // RING)

        @block.sync
        def _(sp):
            def load(n, r, source, turn):
                width = slot_width(n) if isinstance(n, int) else SLOT
                if not isinstance(n, int) or n >= RING:
                    sp.wait_ge(lo_done, n - (RING - 1))
                sp.dma_start(w_raw[:, r, 0:width], source).then_inc(raw_loaded[r], 16)
            walk(sp, load, a["weights0"], 0, LAYER0_SLOTS)
            for n in range(MLA_BASE, MLP_BASE[1]):
                load(n, n % RING, mla_source(n), n // RING)
            walk(sp, load, a["weights1"], MLP_BASE[1], LAYER1_SLOTS)
            for k in range(KT):
                sp.wait_ge(h_ready, KT + k + 1)
                sp.dma_start(a["out"][:, k, :], h[:, k, :]).then_inc(out_stored, 16)
            sp.wait_ge(out_stored, 16 * KT)

        @block.gpsimd
        def _(pool):
            nc.gpsimd.memset(ones[:], 1.0).then_inc(ones_set, 1)

            def low(n, r, source, turn):
                width = slot_width(n) if isinstance(n, int) else SLOT
                pool.wait_ge(hi_done, n + 1)
                nc.gpsimd.tensor_tensor(w_lo[:, r, 0:width], w_raw[:, r, 0:width],
                                        w_hi[:, r, 0:width].bitcast(F32), ALU.subtract).then_inc(lo_done, 1)
            walk(pool, low, a["weights0"], 0, LAYER0_SLOTS)

            own = Chain(pool, pool_chain)

            def low_at(c, i=0, per=0):
                width, r = slot_width(c), c % RING
                pool.wait_ge(hi_done, c + 1 + per * i)
                nc.gpsimd.tensor_tensor(w_lo[:, r, 0:width], w_raw[:, r, 0:width],
                                        w_hi[:, r, 0:width].bitcast(F32), ALU.subtract).then_inc(lo_done, 1)

            for n in range(MLA_BASE, MLA_HEAD_BASE):
                low_at(n)
            pool.wait_ge(tok_ready, 2)
            own.mark(nc.gpsimd.memset(rq_tok[:], 0.0))
            own.mark(nc.gpsimd.memset(rk_tok[:], 0.0))
            own.mark(nc.gpsimd.memset(half_neg[:], -0.5))
            own.mark(nc.gpsimd.memset(eps_sum[:], QKD * EPS))
            own.mark(nc.gpsimd.memset(per_qkd[:], 1.0 / QKD))
            for n in range(MLA_HEAD_BASE, MLA_HEAD_BASE + AHEAD):
                low_at(n)
            pool.wait_ge(mla_loaded, 32)
            pool.wait_ge(kr_ready, 1)

            def by_token(x, width):
                return x.unsqueeze(2).to_broadcast([P, TT, width])

            def project(y, par, c, i=0, per=0):
                half = ROPE // 2
                cos, sin = mrope[:, 0, :, :], mrope[:, 1, :, :]
                mine = slice(par * ROPE, (par + 1) * ROPE)
                first, second = (slice(par * ROPE + o, par * ROPE + o + half) for o in (0, half))
                m1 = tmp[:, 2, 0:TT * half].rearrange("p (t c) -> p t c", t=TT)
                m2 = tmp[:, 3, 0:TT * half].rearrange("p (t c) -> p t c", t=TT)
                low_at(c + AHEAD, i, per)
                pool.wait_ge(qtok_ready, 6 * (y + 1))
                own.mark(nc.gpsimd.tensor_tensor(q_ms[:], q_ss[:], eps_sum[:], ALU.add))
                own.mark(nc.gpsimd.tensor_tensor(qg_tok[:], q_tok[:, :, NOPE:QKD],
                                                 rgain[:, 0:1, :].to_broadcast([P, TT, ROPE]), ALU.mult))
                own.wait()
                nc.gpsimd.tensor_tensor(qscale[:, par, :], q_ms[:], half_neg[:], ALU.pow).then_inc(qscale_ready, 1)
                x1, x2 = qg_tok[:, :, 0:half], qg_tok[:, :, half:ROPE]
                own.mark(nc.gpsimd.tensor_tensor(rq_tok[:, :, first], x1, cos, ALU.mult))
                own.mark(nc.gpsimd.tensor_tensor(m1, x2, sin, ALU.mult))
                own.mark(nc.gpsimd.tensor_tensor(rq_tok[:, :, second], x2, cos, ALU.mult))
                own.mark(nc.gpsimd.tensor_tensor(m2, x1, sin, ALU.mult))
                own.wait()
                nc.gpsimd.tensor_tensor(rq_tok[:, :, first], rq_tok[:, :, first], m1,
                                        ALU.subtract).then_inc(qkn_ready, 1)
                nc.gpsimd.tensor_tensor(rq_tok[:, :, second], rq_tok[:, :, second], m2,
                                        ALU.add).then_inc(qkn_ready, 1)
                low_at(c + 1 + AHEAD, i, per)
                pool.wait_ge(ktok_ready, 6 * (y + 1))
                own.mark(nc.gpsimd.tensor_tensor(k_ms[:], k_ss[:], kr_ss[:], ALU.add))
                own.wait()
                own.mark(nc.gpsimd.tensor_tensor(k_ms[:], k_ms[:], per_qkd[:], ALU.mult))
                own.wait()
                own.mark(nc.gpsimd.tensor_tensor(k_rs[:], k_ms[:], half_neg[:], ALU.pow))
                own.wait()
                nc.gpsimd.tensor_tensor(rk_tok[:, :, mine], kr_tok[:], by_token(k_rs[:], ROPE),
                                        ALU.mult).then_inc(qkn_ready, 1)
                nc.gpsimd.tensor_tensor(k_tok[:], k_tok[:], by_token(k_rs[:], NOPE),
                                        ALU.mult).then_inc(qkn_ready, 1)

            for y in (0, 1):
                project(y, y, MLA_HEAD_BASE + 2 * y)
            with pool.Fori(0, 2) as i:
                own.enter(i, 2 * POOL_MARKS)
                for j in (0, 1):
                    project(2 + j + 2 * i, j, MLA_HEAD_BASE + 4 + 2 * j, i, 4)
            own.leave(2 * POOL_MARKS, 2)
            for y in (6, 7):
                project(y, y % 2, MLA_HEAD_BASE + 2 * y)
            for n in range(MLA_OUT_BASE + AHEAD, MLP_BASE[1]):
                low_at(n)
            walk(pool, low, a["weights1"], MLP_BASE[1], LAYER1_SLOTS)

        @block.scalar
        def _(act):
            def w_high(c, i=0, per=0):
                if c >= SLOTS:
                    return
                width, r = slot_width(c), c % RING
                if c >= RING:
                    act.wait_ge(slot_used, c - (RING - 1) + per * i)
                act.wait_ge(raw_loaded[r], 16 * (c // RING + 1 + (per // RING) * i))
                nc.scalar.activation(w_hi[:, r, 0:width], w_raw[:, r, 0:width], ACT.Copy).then_inc(hi_done, 1)

            def step(n, i=0, per=0):
                w_high(n + AHEAD, i, per)

            def finish(norm, k):
                n = norm * KT + k
                if n >= 2:
                    act.wait_ge(sq_added, n - 1)
                nc.scalar.activation(sq[:, k % 2, :], h[:, k, :], ACT.Square).then_inc(sq_ready, 1)
                nc.scalar.activation(operand[norm][0][:, k, :], h[:, k, :], ACT.Copy,
                                     scale=gains[:, n:n + 1]).then_inc(xhi_ready, 1)

            def root(norm):
                act.wait_ge(ms_ready, norm + 1)
                nc.scalar.activation(t_b[:, 1, :], t_b[:, 0, :], ACT.Sqrt).then_inc(root_ready, 1)

            act.dma_start(gains[:], a["gains"]).then_inc(tables_loaded, 16)
            for k in range(KT):
                act.dma_start(h[:, k, :], a["x"][:, k, :]).then_inc(x_loaded[k], 16)
            act.dma_start(rope_t[:], a["rope"]).then_inc(tables_loaded, 16)
            act.dma_start(ident[:], a["ident"]).then_inc(tables_loaded, 16)
            act.dma_start(decay[:], a["decay"]).then_inc(tables_loaded, 16)
            act.wait_ge(tables_loaded, 64)
            for k in range(KT):
                act.wait_ge(x_loaded[k], 16)
                finish(MIX0, k)
                if k < AHEAD:
                    w_high(k)

            def ret_output(i):
                for v in range(VT):
                    act.wait_ge(pv_done, VT * i + v + 1)
                    if v >= 2:
                        act.wait_ge(osq_added, VT * i + v - 1)
                    nc.scalar.activation(sq[:, v % 2, :], ps[:, 4 + v, :], ACT.Square).then_inc(osq_ready, 1)

            def ret_y(i):
                act.wait_ge(hms_ready, i + 1)
                nc.scalar.activation(t_b[:, 1, :], t_b[:, 0, :], ACT.Sqrt).then_inc(hroot_ready, 1)
                for v in range(VT):
                    act.wait_ge(y_val, VT * i + v + 1)
                    nc.scalar.activation(y_hi[:, v, :], sg[:, v, :], ACT.Copy).then_inc(yhi_ready, 1)

            def ret_rotated(i, first):
                for j in range(2):
                    act.wait_ge(qk_rot, 4 * i + first + j + 1)
                    nc.scalar.activation(qk_hi[:, first + j, :], t_a[:, j, :], ACT.Copy).then_inc(qkhi_ready, 1)

            def ret_head(i, n, j, per):
                first = per == 0
                step(n, j, per)
                if first:
                    root(MIX0)
                step(n + 1, j, per)
                if not first:
                    ret_y(i - 1)
                step(n + 2, j, per)
                ret_rotated(i, 0)
                step(n + 3, j, per)
                n += 4
                if not first:
                    step(n, j, per)
                ret_rotated(i, 2)
                if not first:
                    for m in range(1, 4):
                        step(n + m, j, per)
                    n += 4
                for m in range(4):
                    step(n + m, j, per)
                n += 4
                step(n, j, per)
                act.wait_ge(tok_ready, 1)
                for t in range(TT):
                    nc.scalar.activation(v_hi[:, t, :], ps[:, t, :], ACT.Copy,
                                         scale=rstd_tok[:, t:t + 1]).then_inc(vhi_ready, 1)
                for kt in range(TT):
                    act.wait_ge(s_mul, TT * i + kt + 1)
                    nc.scalar.activation(s_hi[:, kt, kt * P:T], tmp[:, kt, kt * P:T],
                                         ACT.Copy).then_inc(shi_ready, 1)
                for v in range(VT):
                    if v + 1 < VT:
                        step(n + v + 1, j, per)
                    act.wait_ge(bank_read, gate_unit(v, j, per) + 1)
                    nc.scalar.activation(t_b[:, v % 2, :], t_a[:, v % 2, :], ACT.Sigmoid).then_inc(sig_ready, 1)
                ret_output(i)

            ret_head(0, 0, 0, 0)
            with act.Fori(1, HEADS) as i:
                ret_head(i, RET_FIRST, i - 1, RET_HEAD)
            n = RET_SLOTS - 4
            for m in range(5):
                if m < 4:
                    step(n + m)
                if m == 0:
                    ret_y(HEADS - 1)
                else:
                    for k in (2 * m - 2, 2 * m - 1):
                        act.wait_ge(bank_read, RET_UNITS - KT + k + 1)
                        finish(MLP0, k)

            def hidden(L, q, m):
                act.wait_ge(bank_read, MLP_UNIT[L] + 2 * KT * q + m + 1)
                done = KT * QUARTERS * L + KT * q + m + 1
                nc.scalar.activation(t_b[:, m % 2, :], t_a[:, m % 2, :], ACT.Square).then_inc(sqr_ready, 1)
                act.wait_ge(sqr_ready, done)
                nc.scalar.activation(hid_hi[:, m, :], t_b[:, m % 2, :], ACT.Copy).then_inc(hidhi_ready, 1)

            def mlp_quarter(L, q, looped, start=None, norm=None):
                for s in range(2 * KT):
                    if looped:
                        step(MLP_BASE[L] + s, q, 2 * KT)
                    else:
                        step(MLP_BASE[L] + 2 * KT * q + s)
                    if start is not None and s == 0:
                        start()
                    if 1 <= s <= KT:
                        hidden(L, q, s - 1)
                    if norm is not None and s > KT:
                        act.wait_ge(bank_read, MLP_UNIT[L] + 2 * KT * q + s)
                        finish(norm, s - KT - 1)
                if norm is not None:
                    act.wait_ge(bank_read, MLP_UNIT[L] + MLP_UNITS)
                    finish(norm, KT - 1)

            def mlp_act(L, mlp_norm, ple_norm, before):
                def start():
                    before()
                    root(mlp_norm)
                mlp_quarter(L, 0, False, start)
                with act.Fori(1, QUARTERS - 1) as q:
                    mlp_quarter(L, q, True)
                mlp_quarter(L, QUARTERS - 1, False, None, ple_norm)

            def ple_act(L, norm, next_norm):
                act.wait_ge(p_loaded[L], 16)
                for f in range(PF):
                    nc.scalar.activation(p_hi[:, f, :], p_raw[:, f, :], ACT.Copy).then_inc(phi_ready, 1)
                m = 0
                for s in range(PLE_SLOTS):
                    step(PLE_BASE[L] + s)
                    if s == 0:
                        root(norm)
                    if s > 0 and s - 1 not in PLE_PROJ:
                        ple_gate(L, m, next_norm)
                        m += 1
                ple_gate(L, m, next_norm)
                if next_norm is not None:
                    act.wait_ge(h_ready, KT * L + KT)
                    finish(next_norm, KT - 1)

            def ple_gate(L, m, next_norm):
                act.wait_ge(bank_read, PLE_UNIT[L] + m + 1)
                nc.scalar.activation(t_b[:, m % 2, :], t_a[:, m % 2, :], ACT.Sigmoid).then_inc(psig_ready, 1)
                if next_norm is not None and m >= 1:
                    act.wait_ge(h_ready, KT * L + m)
                    finish(next_norm, m - 1)

            def load_p(L, slots):
                def go():
                    act.wait_ge(slot_used, slots)
                    act.dma_start(p_raw[:], a["p"][L]).then_inc(p_loaded[L], 16)
                return go

            mlp_act(0, MLP0, PLE0, load_p(0, RET_SLOTS))
            ple_act(0, PLE0, MIX1)

            act.wait_ge(slot_used, MLA_BASE)
            act.dma_start(mrope[:], a["mrope"]).then_inc(mla_loaded, 16)
            act.dma_start(rgain[:], a["rgain"]).then_inc(mla_loaded, 16)
            for s in range(4):
                step(MLA_BASE + s)
            step(MLA_BASE + 4)
            root(MIX1)
            for s in range(5, MLA_IN_SLOTS):
                step(MLA_BASE + s)
            act.wait_ge(bank_read, MLA_UNIT + MLA_IN_UNITS)
            for j, (lo, hi) in enumerate(((0, QR), (QR, QR + KVR))):
                for t in range(TT):
                    if j or t:
                        act.wait_ge(css_ready, 4 * j + t)
                    nc.scalar.activation(sq[:, 0, 0:hi - lo], c_tok[:, t, lo:hi], ACT.Square,
                                         accum_out=small[:, 4 * j + t:4 * j + t + 1]).then_inc(css_ready, 1)
            act.wait_ge(cms_ready, 2)
            nc.scalar.activation(small[:, 16:24], small[:, 8:16], ACT.Sqrt).then_inc(croot_ready, 1)
            for f in range(QF + KVF):
                act.wait_ge(cT_done, f + 1)
                nc.scalar.activation(c_hi[:, f, :], ps[:, 4 + f % 4, :], ACT.Copy,
                                     scale=gains[:, G_QA + f:G_QA + f + 1]).then_inc(chi_ready, 1)

            def project_q(y, c, i, per):
                step(c, i, per)
                act.wait_ge(slot_used, c + 1 + per * i)
                junk = sq[:].rearrange("p a t -> p (a t)")
                for t in range(TT):
                    lo = t % 2 * QKD
                    nc.scalar.activation(junk[:, t * QKD:(t + 1) * QKD], ps[:, t // 2, lo:lo + QKD], ACT.Square,
                                         accum_out=q_ss[:, t:t + 1]).then_inc(qtok_ready, 1)
                for b in range(2):
                    nc.scalar.activation(q_tok[:, 2 * b:2 * b + 2, :],
                                         ps[:, b, 0:2 * QKD].rearrange("p (t c) -> p t c", t=2),
                                         ACT.Copy).then_inc(qtok_ready, 1)

            def project_kv(y, par, c, i, per):
                step(c + 1, i, per)
                act.wait_ge(slot_used, c + 2 + per * i)
                kv = NOPE + VD
                for t in range(TT):
                    lo = t % 2 * kv
                    nc.scalar.activation(tmp[:, 0, t * NOPE:(t + 1) * NOPE], ps[:, 2 + t // 2, lo:lo + NOPE],
                                         ACT.Square, accum_out=k_ss[:, t:t + 1]).then_inc(ktok_ready, 1)
                for b in range(2):
                    bank = ps[:, 2 + b, :].rearrange("p (t c) -> p t c", t=2)
                    nc.scalar.activation(k_tok[:, 2 * b:2 * b + 2, :], bank[:, :, 0:NOPE],
                                         ACT.Copy).then_inc(ktok_ready, 1)
                    nc.scalar.activation(mv_hi[:, par, 2 * b:2 * b + 2, :], bank[:, :, NOPE:kv],
                                         ACT.Copy).then_inc(mvhi_ready, 1)

            def transposed_qk(y, par, which):
                dst, gain = (qT_hi, G_QN) if which == 0 else (kT_hi, G_KN)
                act.wait_ge(qkT_done, 4 * y + 2 * which + 1)
                nc.scalar.activation(dst[:, par, :], ps[:, 2 * which, :], ACT.Copy,
                                     scale=gains[:, gain:gain + 1]).then_inc(qkThi_ready, 1)
                rows = slice(par * ROPE, (par + 1) * ROPE)
                act.wait_ge(qkT_done, 4 * y + 2 * which + 2)
                nc.scalar.activation(dst[rows, 2, :], ps[rows, 2 * which + 1, :], ACT.Copy).then_inc(qkThi_ready, 1)

            def exponent(x, par, b):
                kend, u = (b + 1) * P, 4 * par + b
                act.wait_ge(nmax_ready, 4 * x + b + 1)
                if b >= 2:
                    act.wait_ge(pT_done, 4 * x + b - 1)
                nc.scalar.activation(pr[:, b % 2, 0:kend], ps[:, 4 + b % 2, 0:kend], ACT.Exp,
                                     bias=att[:, 1, u:u + 1], scale=qscale[:, par, b:b + 1],
                                     accum_out=att[:, 2, u:u + 1]).then_inc(exp_ready, 1)

            def transposed_p(x, b):
                act.wait_ge(pT_done, 4 * x + b + 1)
                nc.scalar.activation(pT_hi[:, 0:b + 1, b * P:(b + 1) * P],
                                     ps[:, 6, 0:(b + 1) * P].rearrange("p (k q) -> p k q", k=b + 1),
                                     ACT.Copy).then_inc(pThi_ready, 1)

            def output(x):
                act.wait_ge(o_done, x + 1)
                dst = x_hi[:, x, :] if isinstance(x, int) else x_hi[:, bass.ds(x, 1), :].rearrange("p a t -> p (a t)")
                nc.scalar.activation(dst, ps[:, 7, :], ACT.Copy).then_inc(ohi_ready, 1)

            def phase(x, par, c=None, i=0, per=0):
                first = isinstance(x, int) and x == 0
                exponent(x, par, 0)
                if not first:
                    output(x - 1)
                if c is not None:
                    project_q(x + 1, c, i, per)
                exponent(x, par, 1)
                transposed_p(x, 0)
                if c is not None:
                    project_kv(x + 1, 1 - par, c, i, per)
                exponent(x, par, 2)
                transposed_p(x, 1)
                if c is not None:
                    transposed_qk(x + 1, 1 - par, 0)
                exponent(x, par, 3)
                transposed_p(x, 2)
                if c is not None:
                    transposed_qk(x + 1, 1 - par, 1)
                transposed_p(x, 3)

            project_q(0, MLA_HEAD_BASE, 0, 0)
            project_kv(0, 0, MLA_HEAD_BASE, 0, 0)
            transposed_qk(0, 0, 0)
            transposed_qk(0, 0, 1)
            phase(0, 0, MLA_HEAD_BASE + 2)
            with act.Fori(0, 2) as i:
                for j in (1, 2):
                    phase(j + 2 * i, j % 2, MLA_HEAD_BASE + 2 * (j + 1), i, 4)
            for x in (5, 6):
                phase(x, x % 2, MLA_HEAD_BASE + 2 * (x + 1))
            phase(MH - 1, 1)
            output(MH - 1)
            for m in range(KT):
                step(MLA_OUT_BASE + m)
                if m >= 1:
                    act.wait_ge(bank_read, MLA_OUT_UNIT + m)
                    finish(MLP1, m - 1)
            act.wait_ge(bank_read, MLA_OUT_UNIT + KT)
            finish(MLP1, KT - 1)

            mlp_act(1, MLP1, PLE1, load_p(1, MLA_BASE + MLA_SLOTS))
            ple_act(1, PLE1, None)

        @block.vector
        def _(dve):
            own = Chain(dve, chain)

            def finish(norm, k):
                n = norm * KT + k
                dve.wait_ge(sq_ready, n + 1)
                if k == 0:
                    nc.vector.tensor_copy(sq_sum[:], sq[:, 0, :]).then_inc(sq_added, 1)
                else:
                    dve.wait_ge(sq_added, n)
                    nc.vector.tensor_tensor(sq_sum[:], sq_sum[:], sq[:, k % 2, :], ALU.add).then_inc(sq_added, 1)
                dve.wait_ge(xhi_ready, n + 1)
                hi, lo = operand[norm]
                nc.vector.scalar_tensor_tensor(lo[:, k, :], h[:, k, :], gains[:, n:n + 1],
                                               hi[:, k, :].bitcast(F32), ALU.mult, ALU.subtract
                                               ).then_inc(x_ready, 1)

            def norm_scale(norm):
                dve.wait_ge(ss_done, norm + 1)
                nc.vector.tensor_scalar(t_b[:, 0, :], ps[:, NORM_BANK, :], 1.0 / D, EPS, ALU.mult,
                                        ALU.add).then_inc(ms_ready, 1)
                dve.wait_ge(root_ready, norm + 1)
                nc.vector.reciprocal(rstd[:], t_b[:, 1, :]).then_inc(rstd_ready, 1)
                if norm in (MIX0, MIX1):
                    dve.wait_ge(tok_done, 1 + (norm == MIX1))
                    nc.vector.tensor_copy(rstd_tok[:], ps[:, NORM_BANK, 0:TT]).then_inc(tok_ready, 1)
                dve.wait_ge(rstd_ready, norm + 1)

            dve.wait_ge(tables_loaded, 64)
            for k in range(KT):
                dve.wait_ge(x_loaded[k], 16)
                finish(MIX0, k)

            def rotate(i, first, unit):
                one, two = ps[:, first, :], ps[:, first + 1, :]
                cos, sin = rope_t[:, 0, :], rope_t[:, 1, :]
                if first:
                    dve.wait_ge(qk_ready, 4 * i + 2)
                own.mark(nc.vector.tensor_tensor(t_a[:, 0, :], one, cos, ALU.mult))
                nc.vector.tensor_tensor(t_b[:, 1, :], one, sin, ALU.mult).then_inc(bank_read, 1)
                own.mark(nc.vector.tensor_tensor(t_b[:, 0, :], two, sin, ALU.mult))
                nc.vector.tensor_tensor(t_a[:, 1, :], two, cos, ALU.mult).then_inc(bank_read, 1)
                own.wait()
                nc.vector.tensor_tensor(t_a[:, 0, :], t_a[:, 0, :], t_b[:, 0, :], ALU.subtract).then_inc(qk_rot, 1)
                dve.wait_ge(bank_read, unit + 2)
                nc.vector.tensor_tensor(t_a[:, 1, :], t_a[:, 1, :], t_b[:, 1, :], ALU.add).then_inc(qk_rot, 1)
                for j in range(2):
                    dve.wait_ge(qkhi_ready, 4 * i + first + j + 1)
                    nc.vector.tensor_tensor(qk_lo[:, first + j, :], t_a[:, j, :],
                                            qk_hi[:, first + j, :].bitcast(F32), ALU.subtract).then_inc(qk_ready, 1)

            def ret_output(i):
                for v in range(VT):
                    dve.wait_ge(osq_ready, VT * i + v + 1)
                    own.mark(nc.vector.tensor_tensor(sg[:, v, :], sg[:, v, :], ps[:, 4 + v, :], ALU.mult))
                    if v == 0:
                        nc.vector.tensor_copy(sq_sum[:], sq[:, 0, :]).then_inc(osq_added, 1)
                    else:
                        dve.wait_ge(osq_added, VT * i + v)
                        nc.vector.tensor_tensor(sq_sum[:], sq_sum[:], sq[:, v % 2, :],
                                                ALU.add).then_inc(osq_added, 1)

            def ret_y(i):
                cols = (gains[:, G_GN + VT * i:G_GN + VT * (i + 1)] if isinstance(i, int)
                        else gains[:, bass.ds(G_GN + VT * i, VT)])
                own.mark(nc.vector.tensor_copy(gn[:], cols))
                dve.wait_ge(hss_done, i + 1)
                nc.vector.tensor_scalar(t_b[:, 0, :], ps[:, NORM_BANK, :], 1.0 / DV, EPS, ALU.mult,
                                        ALU.add).then_inc(hms_ready, 1)
                dve.wait_ge(hroot_ready, i + 1)
                own.mark(nc.vector.reciprocal(t_b[:, 0, :], t_b[:, 1, :]))
                own.wait()

                def low(v):
                    dve.wait_ge(yhi_ready, VT * i + v + 1)
                    nc.vector.tensor_tensor(y_lo[:, v, :], sg[:, v, :], y_hi[:, v, :].bitcast(F32),
                                            ALU.subtract).then_inc(y_ready, 1)
                for v in range(VT):
                    nc.vector.scalar_tensor_tensor(sg[:, v, :], sg[:, v, :], gn[:, v:v + 1], t_b[:, 0, :],
                                                   ALU.mult, ALU.mult).then_inc(y_val, 1)
                    if v >= 1:
                        low(v - 1)
                low(VT - 1)

            def add_to_h(k, bank, unit):
                nc.vector.tensor_tensor(h[:, k, :], h[:, k, :], ps[:, bank, :], ALU.add).then_inc(bank_read, 1)

            def ret_head(i, n, j, per, unit, uper):
                first = per == 0
                n, unit = n + per * j, unit + uper * j
                if first:
                    norm_scale(MIX0)
                    for c in range(2):
                        own.mark(nc.vector.tensor_tensor(rope_t[:, c, :], rope_t[:, c, :], rstd[:], ALU.mult))
                    own.wait()
                else:
                    ret_y(i - 1)
                dve.wait_ge(slot_used, n + 2)
                if not first:
                    dve.wait_ge(y_ready, VT * i)
                rotate(i, 0, unit)
                dve.wait_ge(slot_used, n + 4)
                rotate(i, 2, unit + 2)
                n, unit = n + 4, unit + 4
                if not first:
                    for k in range(KT):
                        dve.wait_ge(slot_used, n + k // 2 + 1)
                        add_to_h(k, k % UB, unit + k)
                    n, unit = n + 4, unit + KT
                n = n + 4
                dve.wait_ge(slot_used, n)
                for t in range(TT):
                    dve.wait_ge(vhi_ready, TT * i + t + 1)
                    nc.vector.scalar_tensor_tensor(v_lo[:, t, :], ps[:, t, :], rstd_tok[:, t:t + 1],
                                                   v_hi[:, t, :].bitcast(F32), ALU.mult, ALU.subtract
                                                   ).then_inc(bank_read, 1)
                unit = unit + TT

                def low(kt):
                    dve.wait_ge(shi_ready, TT * i + kt + 1)
                    nc.vector.tensor_tensor(s_lo[:, kt, kt * P:T], tmp[:, kt, kt * P:T],
                                            s_hi[:, kt, kt * P:T].bitcast(F32), ALU.subtract).then_inc(s_ready, 1)
                for kt in range(TT):
                    w = T - kt * P
                    table = (decay[:, i, 0:w] if isinstance(i, int)
                             else decay[:, bass.ds(i, 1), 0:w].rearrange("p a t -> p (a t)"))
                    dve.wait_ge(s_done, TT * i + kt + 1)
                    nc.vector.tensor_tensor(tmp[:, kt, kt * P:T], ps[:, 4 + kt, 0:w], table,
                                            ALU.mult).then_inc(s_mul, 1)
                    if kt >= 1:
                        low(kt - 1)
                low(TT - 1)

                def silu(v):
                    dve.wait_ge(sig_ready, VT * i + v + 1)
                    own.mark(nc.vector.tensor_tensor(sg[:, v, :], t_a[:, v % 2, :], t_b[:, v % 2, :], ALU.mult))
                dve.wait_ge(s_ready, TT * (i + 1))
                for v in range(VT):
                    dve.wait_ge(slot_used, n + v + 1)
                    if v >= 2:
                        own.wait()
                    nc.vector.tensor_tensor(t_a[:, v % 2, :], ps[:, v, :], rstd[:], ALU.mult).then_inc(bank_read, 1)
                    if v >= 1:
                        silu(v - 1)
                dve.wait_ge(bank_read, unit + VT)
                silu(VT - 1)
                own.wait()
                ret_output(i)

            ret_head(0, 0, 0, 0, 0, 0)
            with dve.Fori(1, HEADS) as i:
                own.enter(i - 1, RET_MARKS)
                ret_head(i, RET_FIRST, i - 1, RET_HEAD, RET_FIRST_UNITS, RET_HEAD_UNITS)
            own.leave(RET_MARKS, HEADS - 1)
            ret_y(HEADS - 1)
            for k in range(KT):
                dve.wait_ge(slot_used, RET_SLOTS - 4 + k // 2 + 1)
                add_to_h(k, k % UB, RET_UNITS - KT + k)
                if k >= 2:
                    finish(MLP0, k - 2)
            finish(MLP0, KT - 2)
            finish(MLP0, KT - 1)

            def mlp_quarter(L, q, norm=None):
                n, unit = MLP_BASE[L] + 2 * KT * q, MLP_UNIT[L] + 2 * KT * q

                def low(m):
                    dve.wait_ge(hidhi_ready, KT * QUARTERS * L + KT * q + m + 1)
                    nc.vector.tensor_tensor(hid_lo[:, m, :], t_b[:, m % 2, :], hid_hi[:, m, :].bitcast(F32),
                                            ALU.subtract).then_inc(hid_ready, 1)
                for m in range(KT):
                    dve.wait_ge(slot_used, n + m + 1)
                    nc.vector.scalar_tensor_tensor(t_a[:, m % 2, :], ps[:, m % UB, :], 0.0, rstd[:],
                                                   ALU.max, ALU.mult).then_inc(bank_read, 1)
                    if m >= 1:
                        low(m - 1)
                low(KT - 1)
                for m in range(KT):
                    dve.wait_ge(slot_used, n + KT + m + 1)
                    add_to_h(m, m % UB, unit + KT + m)
                    if norm is not None and m >= 1:
                        finish(norm, m - 1)
                if norm is not None:
                    finish(norm, KT - 1)

            def ple(L, norm, next_norm):
                for f in range(PF):
                    dve.wait_ge(phi_ready, PF * L + f + 1)
                    nc.vector.tensor_tensor(p_lo[:, f, :], p_raw[:, f, :], p_hi[:, f, :].bitcast(F32),
                                            ALU.subtract).then_inc(p_ready, 1)
                norm_scale(norm)

                def mix(m):
                    dve.wait_ge(slot_used, PLE_BASE[L] + PLE_PROJ[m // 4] + 1)
                    dve.wait_ge(psig_ready, KT * L + m + 1)
                    if m >= 2:
                        dve.wait_ge(h_ready, KT * L + m - 1)
                    own.mark(nc.vector.tensor_tensor(proj[:, m % 2, :], t_b[:, m % 2, :], ps[:, 4 + m % 4, :],
                                                     ALU.mult))
                    own.wait()
                    nc.vector.tensor_tensor(h[:, m, :], h[:, m, :], proj[:, m % 2, :], ALU.add).then_inc(h_ready, 1)
                    if next_norm is not None:
                        finish(next_norm, m)
                for m in range(KT):
                    dve.wait_ge(slot_used, PLE_BASE[L] + PLE_GATE[m] + 1)
                    nc.vector.tensor_tensor(t_a[:, m % 2, :], ps[:, m % UB, :], rstd[:],
                                            ALU.mult).then_inc(bank_read, 1)
                    if m >= 1:
                        mix(m - 1)
                mix(KT - 1)

            def mlp_ple(L, mlp_norm, ple_norm, next_norm):
                norm_scale(mlp_norm)
                with dve.Fori(0, QUARTERS - 1) as q:
                    mlp_quarter(L, q)
                mlp_quarter(L, QUARTERS - 1, ple_norm)
                ple(L, ple_norm, next_norm)

            mlp_ple(0, MLP0, PLE0, MIX1)

            C = QR + KVR + ROPE
            norm_scale(MIX1)
            dve.wait_ge(tok_ready, 2)
            for t in range(TT):
                dve.wait_ge(slot_used, MLA_BASE + 4)
                nc.vector.tensor_scalar(c_tok[:, t, 0:QR], ps[:, t, 0:QR], rstd_tok[:, t:t + 1], None,
                                        ALU.mult).then_inc(bank_read, 1)
            for t in range(TT):
                dve.wait_ge(slot_used, MLA_BASE + 8)
                nc.vector.tensor_scalar(c_tok[:, t, QR:C], ps[:, t, 0:KVR + ROPE], rstd_tok[:, t:t + 1], None,
                                        ALU.mult).then_inc(bank_read, 1)

            dve.wait_ge(mla_loaded, 32)
            dve.wait_ge(bank_read, MLA_UNIT + MLA_IN_UNITS)
            kr, half = c_tok[:, :, QR + KVR:C], ROPE // 2
            wide = [tmp[:, j, 0:TT * ROPE].rearrange("p (t c) -> p t c", t=TT) for j in (2, 3)]
            own.mark(nc.vector.tensor_tensor(wide[0], kr, kr, ALU.mult))
            own.mark(nc.vector.tensor_tensor(wide[1], kr, rgain[:, 1:2, :].to_broadcast([P, TT, ROPE]), ALU.mult))
            own.wait()
            own.mark(nc.vector.tensor_reduce(kr_ss[:], wide[0], AX.X, ALU.add))
            own.wait()
            own.mark(nc.vector.tensor_scalar(kr_ss[:], kr_ss[:], QKD * EPS, None, ALU.add))
            cos, sin = mrope[:, 0, :, :], mrope[:, 1, :, :]
            x1, x2 = wide[1][:, :, 0:half], wide[1][:, :, half:ROPE]
            m1, m2 = wide[0][:, :, 0:half], wide[0][:, :, half:ROPE]
            own.mark(nc.vector.tensor_tensor(kr_tok[:, :, 0:half], x1, cos, ALU.mult))
            own.mark(nc.vector.tensor_tensor(m1, x2, sin, ALU.mult))
            own.mark(nc.vector.tensor_tensor(kr_tok[:, :, half:ROPE], x2, cos, ALU.mult))
            own.mark(nc.vector.tensor_tensor(m2, x1, sin, ALU.mult))
            own.wait()
            own.mark(nc.vector.tensor_tensor(kr_tok[:, :, 0:half], kr_tok[:, :, 0:half], m1, ALU.subtract))
            nc.vector.tensor_tensor(kr_tok[:, :, half:ROPE], kr_tok[:, :, half:ROPE], m2,
                                    ALU.add).then_inc(kr_ready, 1)
            dve.wait_ge(css_ready, 8)
            for j, width in enumerate((QR, KVR)):
                nc.vector.tensor_scalar(small[:, 8 + 4 * j:12 + 4 * j], small[:, 4 * j:4 * j + 4], 1.0 / width, EPS,
                                        ALU.mult, ALU.add).then_inc(cms_ready, 1)
            dve.wait_ge(croot_ready, 1)
            own.mark(nc.vector.reciprocal(small[:, 0:8], small[:, 16:24]))
            own.wait()
            for j, (lo, hi) in enumerate(((0, QR), (QR, QR + KVR))):
                for t in range(TT):
                    nc.vector.tensor_scalar(c_tok[:, t, lo:hi], c_tok[:, t, lo:hi], small[:, 4 * j + t:4 * j + t + 1],
                                            None, ALU.mult).then_inc(cn_ready, 1)
            for f in range(QF + KVF):
                dve.wait_ge(chi_ready, f + 1)
                nc.vector.scalar_tensor_tensor(c_lo[:, f, :], ps[:, 4 + f % 4, :], gains[:, G_QA + f:G_QA + f + 1],
                                               c_hi[:, f, :].bitcast(F32), ALU.mult, ALU.subtract
                                               ).then_inc(c_ready, 1)

            def project_v(y, par):
                for b in range(2):
                    dve.wait_ge(mvhi_ready, 2 * y + b + 1)
                    v = ps[:, 2 + b, :].rearrange("p (t c) -> p t c", t=2)[:, :, NOPE:NOPE + VD]
                    nc.vector.tensor_tensor(mv_lo[:, par, 2 * b:2 * b + 2, :], v,
                                            mv_hi[:, par, 2 * b:2 * b + 2, :].bitcast(F32),
                                            ALU.subtract).then_inc(mv_ready, 1)

            def transposed_qk(y, par, which):
                hi, lo, gain = (qT_hi, qT_lo, G_QN) if which == 0 else (kT_hi, kT_lo, G_KN)
                dve.wait_ge(qkThi_ready, 4 * y + 2 * which + 1)
                nc.vector.scalar_tensor_tensor(lo[:, par, :], ps[:, 2 * which, :], gains[:, gain:gain + 1],
                                               hi[:, par, :].bitcast(F32), ALU.mult, ALU.subtract
                                               ).then_inc(qkT_ready, 1)
                rows = slice(par * ROPE, (par + 1) * ROPE)
                dve.wait_ge(qkThi_ready, 4 * y + 2 * which + 2)
                nc.vector.tensor_tensor(lo[rows, 2, :], ps[rows, 2 * which + 1, :], hi[rows, 2, :].bitcast(F32),
                                        ALU.subtract).then_inc(qkT_ready, 1)

            def maximum(x, par, b):
                kend, u = (b + 1) * P, 4 * par + b
                bank = ps[:, 4 + b % 2, :]
                if b == 0:
                    dve.wait_ge(qscale_ready, x + 1)
                dve.wait_ge(sc_done, 4 * x + b + 1)
                own.mark(nc.vector.memset(bank[0:CHUNK, kend - CHUNK:kend], -1e30))
                own.wait()
                own.mark(nc.vector.reduce_max(att[:, 0, u:u + 1], bank[:, 0:kend], AX.X))
                own.wait()
                nc.vector.tensor_scalar(att[:, 1, u:u + 1], att[:, 0, u:u + 1], qscale[:, par, b:b + 1], -1.0,
                                        ALU.mult, ALU.mult).then_inc(nmax_ready, 1)

            def normalize(x, par, b):
                kend, u = (b + 1) * P, 4 * par + b
                dve.wait_ge(exp_ready, 4 * x + b + 1)
                own.mark(nc.vector.reciprocal(att[:, 3, u:u + 1], att[:, 2, u:u + 1]))
                own.wait()
                nc.vector.tensor_scalar(pr[:, b % 2, 0:kend], pr[:, b % 2, 0:kend], att[:, 3, u:u + 1], None,
                                        ALU.mult).then_inc(pr_ready, 1)

            def transposed_p(x, b):
                dve.wait_ge(pThi_ready, 4 * x + b + 1)
                blocks = slice(b * P, (b + 1) * P)
                nc.vector.tensor_tensor(pT_lo[:, 0:b + 1, blocks],
                                        ps[:, 6, 0:(b + 1) * P].rearrange("p (k q) -> p k q", k=b + 1),
                                        pT_hi[:, 0:b + 1, blocks].bitcast(F32), ALU.subtract).then_inc(pT_ready, 1)

            def output(x):
                dve.wait_ge(ohi_ready, x + 1)

                def at(buffer):
                    return buffer[:, x, :] if isinstance(x, int) else \
                        buffer[:, bass.ds(x, 1), :].rearrange("p a t -> p (a t)")
                nc.vector.tensor_tensor(at(x_lo), ps[:, 7, :], at(x_hi).bitcast(F32),
                                        ALU.subtract).then_inc(o_ready, 1)

            def phase(x, par, project=True):
                maximum(x, par, 0)
                normalize(x, par, 0)
                if not (isinstance(x, int) and x == 0):
                    output(x - 1)
                maximum(x, par, 1)
                transposed_p(x, 0)
                normalize(x, par, 1)
                if project:
                    project_v(x + 1, 1 - par)
                maximum(x, par, 2)
                transposed_p(x, 1)
                normalize(x, par, 2)
                if project:
                    transposed_qk(x + 1, 1 - par, 0)
                maximum(x, par, 3)
                transposed_p(x, 2)
                normalize(x, par, 3)
                if project:
                    transposed_qk(x + 1, 1 - par, 1)
                transposed_p(x, 3)

            project_v(0, 0)
            transposed_qk(0, 0, 0)
            transposed_qk(0, 0, 1)
            phase(0, 0)
            with dve.Fori(0, 2) as i:
                own.enter(i, 2 * ATT_MARKS)
                for j in (1, 2):
                    phase(j + 2 * i, j % 2)
            own.leave(2 * ATT_MARKS, 2)
            for x in (5, 6):
                phase(x, x % 2)
            phase(MH - 1, 1, False)
            output(MH - 1)
            for k in range(KT):
                dve.wait_ge(slot_used, MLA_OUT_BASE + k + 1)
                add_to_h(k, k % UB, MLA_OUT_UNIT + k)
                if k >= 1:
                    finish(MLP1, k - 1)
            finish(MLP1, KT - 1)

            mlp_ple(1, MLP1, PLE1, None)

        @block.tensor
        def _(pe):
            def product(out, st, mv, start, stop):
                nc.tensor.matmul(out, st[0], mv[1], start=start, stop=False)
                nc.tensor.matmul(out, st[1], mv[0], start=False, stop=False)
                return nc.tensor.matmul(out, st[0], mv[0], start=False, stop=stop)

            def weights(n, lo, hi):
                return w_hi[:, n % RING, lo:hi], w_lo[:, n % RING, lo:hi]

            def arrived(n):
                pe.wait_ge(lo_done, n + 1)

            def bank_free(unit):
                if not isinstance(unit, int) or unit >= UB:
                    pe.wait_ge(bank_read, unit - (UB - 1))

            def both(hi, lo, k, cols=slice(0, T)):
                return hi[:, k, cols], lo[:, k, cols]

            def tile_of(n, bank, operand, k, width=P, base=0, last=KT - 1):
                return product(ps[:, bank, :], weights(n, base + k * width, base + (k + 1) * width),
                               both(*operand, k), k == 0, k == last)

            def linear(n, i, per, unit, uper, count, operand, ready=None, mid=None):
                off, uoff = per * i, uper * i
                for m in range(2):
                    arrived(n + m + off)
                    bank_free(unit + m + uoff)
                    for k in range(KT - 1):
                        if m == 0 and ready:
                            ready(k)
                        tile_of(n + m, (unit + m) % UB, operand, k)
                if ready:
                    ready(KT - 1)
                for m in range(2):
                    tile_of(n + m, (unit + m) % UB, operand, KT - 1).then_inc(slot_used, 1)
                if mid:
                    mid()
                for m in range(2, count):
                    arrived(n + m + off)
                    bank_free(unit + m + uoff)
                    for k in range(KT):
                        last = tile_of(n + m, (unit + m) % UB, operand, k)
                    last.then_inc(slot_used, 1)

            def square_sum(norm):
                pe.wait_ge(sq_added, KT * (norm + 1))
                nc.tensor.matmul(ps[:, NORM_BANK, :], ones[:], sq_sum[:], start=True, stop=True).then_inc(ss_done, 1)

            def turn_rstd(norm):
                pe.wait_ge(rstd_ready, norm + 1)
                for t in range(TT):
                    last = nc.tensor.matmul(ps[:, NORM_BANK, t:t + 1], rstd[0:1, t * P:(t + 1) * P],
                                            ones[0:1, 0:1], start=True, stop=True)
                last.then_inc(tok_done, 1)

            def x_tile(norm):
                return lambda k: pe.wait_ge(x_ready, KT * norm + k + 1)

            pe.wait_ge(ones_set, 1)

            def head_square_sum(i):
                pe.wait_ge(osq_added, VT * (i + 1))
                nc.tensor.matmul(ps[:, NORM_BANK, :], ones[:], sq_sum[:], start=True, stop=True).then_inc(hss_done, 1)

            def ret_out(i, n, off, unit, uoff):
                for m in range(KT):
                    if m % 2 == 0:
                        arrived(n + m // 2 + off)
                    bank_free(unit + m + uoff)
                    for k in range(VT):
                        if m == 0:
                            pe.wait_ge(y_ready, VT * i + k + 1)
                        last = tile_of(n + m // 2, (unit + m) % UB, (y_hi, y_lo), k, base=(m % 2) * VT * P,
                                       last=VT - 1)
                    if m % 2:
                        last.then_inc(slot_used, 1)

            def ret_head(i, n, j, per, unit, uper):
                first = per == 0
                off, uoff = per * j, uper * j

                def norms():
                    if first:
                        square_sum(MIX0)
                    else:
                        head_square_sum(i - 1)
                linear(n, j, per, unit, uper, 4, operand[MIX0], x_tile(MIX0), norms)
                n, unit = n + 4, unit + 4
                if first:
                    turn_rstd(MIX0)
                else:
                    ret_out(i - 1, n, off, unit, uoff)
                    n, unit = n + 4, unit + KT
                for t in range(TT):
                    bank_free(unit + t + uoff)
                for s in range(4):
                    arrived(n + s + off)
                    for kk in range(2):
                        k = 2 * s + kk
                        for t in range(TT):
                            last = product(ps[:, t, :], both(x_hi, x_lo, k, slice(t * P, (t + 1) * P)),
                                           weights(n + s, kk * DV, (kk + 1) * DV), k == 0, k == KT - 1)
                    last.then_inc(slot_used, 1)
                n, unit = n + 4, unit + 4
                pe.wait_ge(qk_ready, 4 * (i + 1))
                if first:
                    pe.wait_ge(tok_ready, 1)
                else:
                    pe.wait_ge(osq_added, VT * i)
                    pe.wait_ge(hms_ready, i)
                for kt in range(TT):
                    for c in range(2):
                        last = product(ps[:, 4 + kt, 0:T - kt * P],
                                       both(qk_hi, qk_lo, 2 + c, slice(kt * P, (kt + 1) * P)),
                                       both(qk_hi, qk_lo, c, slice(kt * P, T)), c == 0, c == 1)
                    last.then_inc(s_done, 1)
                for v in range(VT):
                    arrived(n + v + off)
                    bank_free(unit + v + uoff)
                    for k in range(KT):
                        last = tile_of(n + v, (unit + v) % UB, operand[MIX0], k)
                    last.then_inc(slot_used, 1)
                pe.wait_ge(s_ready, TT * (i + 1))
                for v in range(VT):
                    for kt in range(TT):
                        last = product(ps[:, 4 + v, kt * P:T],
                                       both(v_hi, v_lo, kt, slice(v * P, (v + 1) * P)),
                                       both(s_hi, s_lo, kt, slice(kt * P, T)), kt == 0, kt == TT - 1)
                    last.then_inc(pv_done, 1)

            ret_head(0, 0, 0, 0, 0, 0)
            with pe.Fori(1, HEADS) as i:
                ret_head(i, RET_FIRST, i - 1, RET_HEAD, RET_FIRST_UNITS, RET_HEAD_UNITS)
            head_square_sum(HEADS - 1)
            ret_out(HEADS - 1, RET_SLOTS - 4, 0, RET_UNITS - KT, 0)

            def mlp_quarter(L, norm, q, mid=None):
                linear(MLP_BASE[L], q, 2 * KT, MLP_UNIT[L], 2 * KT, KT, operand[norm],
                       x_tile(norm), mid)
                linear(MLP_BASE[L] + KT, q, 2 * KT, MLP_UNIT[L] + KT, 2 * KT, KT, (hid_hi, hid_lo),
                       lambda k: pe.wait_ge(hid_ready, KT * QUARTERS * L + KT * q + k + 1))

            def ple(L, norm):
                for pos in range(PLE_SLOTS):
                    n = PLE_BASE[L] + pos
                    if pos == 0:
                        linear(n, 0, 0, PLE_UNIT[L], 0, 2, operand[norm], x_tile(norm),
                               lambda: square_sum(norm))
                    elif pos in PLE_PROJ:
                        half = PLE_PROJ.index(pos)
                        arrived(n)
                        if half == 0:
                            pe.wait_ge(p_ready, PF * (L + 1))
                            pe.wait_ge(rstd_ready, norm + 1)
                        for m in range(4):
                            if half:
                                pe.wait_ge(h_ready, KT * L + m + 1)
                            for k in range(PF):
                                last = tile_of(n, 4 + m, (p_hi, p_lo), k, base=m * PF * P, last=PF - 1)
                        last.then_inc(slot_used, 1)
                    elif pos >= 2:
                        unit = PLE_UNIT[L] + PLE_GATE.index(pos)
                        arrived(n)
                        bank_free(unit)
                        for k in range(KT):
                            last = tile_of(n, unit % UB, operand[norm], k)
                        last.then_inc(slot_used, 1)

            def mlp_ple(L, mlp_norm, ple_norm):
                mlp_quarter(L, mlp_norm, 0, lambda: square_sum(mlp_norm))
                with pe.Fori(1, QUARTERS) as q:
                    mlp_quarter(L, mlp_norm, q)
                ple(L, ple_norm)

            mlp_ple(0, MLP0, PLE0)

            for part, width in enumerate((QR, KVR + ROPE)):
                for t in range(TT):
                    bank_free(MLA_UNIT + 4 * part + t)
                for s in range(4):
                    n = MLA_BASE + 4 * part + s
                    arrived(n)
                    for kk in range(2):
                        k = 2 * s + kk
                        if part == 0:
                            pe.wait_ge(x_ready, KT * MIX1 + k + 1)
                        for t in range(TT):
                            last = product(ps[:, t, 0:width], both(*operand[MIX1], k, slice(t * P, (t + 1) * P)),
                                           weights(n, kk * width, (kk + 1) * width), k == 0, k == KT - 1)
                    last.then_inc(slot_used, 1)
                if part == 0:
                    square_sum(MIX1)
                    turn_rstd(MIX1)
            pe.wait_ge(cn_ready, 8)
            pe.wait_ge(tok_ready, 2)
            for f in range(QF + KVF):
                if f >= 4:
                    pe.wait_ge(c_ready, f - 3)
                for t in range(TT):
                    last = nc.tensor.transpose(ps[:, 4 + f % 4, t * P:(t + 1) * P], c_tok[:, t, f * P:(f + 1) * P],
                                               ident[:])
                last.then_inc(cT_done, 1)
            pe.wait_ge(c_ready, QF + KVF)

            def project_q(c, i, per):
                arrived(c + per * i)
                for t in range(TT):
                    lo = t % 2 * QKD
                    for f in range(QF):
                        last = product(ps[:, t // 2, lo:lo + QKD], both(c_hi, c_lo, f, slice(t * P, (t + 1) * P)),
                                       weights(c, f * QKD, (f + 1) * QKD), f == 0, f == QF - 1)
                last.then_inc(slot_used, 1)

            def project_kv(c, i, per):
                arrived(c + 1 + per * i)
                kv = NOPE + VD
                for t in range(TT):
                    lo = t % 2 * kv
                    for f in range(KVF):
                        last = product(ps[:, 2 + t // 2, lo:lo + kv],
                                       both(c_hi, c_lo, QF + f, slice(t * P, (t + 1) * P)),
                                       weights(c + 1, f * kv, (f + 1) * kv), f == 0, f == KVF - 1)
                last.then_inc(slot_used, 1)

            def transpose_qk(y, which):
                tok, rot = (q_tok, rq_tok) if which == 0 else (k_tok, rk_tok)
                pe.wait_ge(qkn_ready, 4 * y + 2 * which + 2)
                if which:
                    pe.wait_ge(mv_ready, 2 * (y + 1))
                for x in range(2):
                    for t in range(TT):
                        src = rot[:, t, :] if x else tok[:, t, 0:NOPE]
                        last = nc.tensor.transpose(ps[:, 2 * which + x, t * P:(t + 1) * P], src, ident[:])
                    last.then_inc(qkT_done, 1)

            def scores(x, par, b):
                kend, u = (b + 1) * P, 4 * x + b
                if not isinstance(u, int) or u >= 2:
                    pe.wait_ge(exp_ready, u - 1)
                rows, cols = slice(par * ROPE, (par + 1) * ROPE), slice(b * P, (b + 1) * P)
                product(ps[:, 4 + b % 2, 0:kend], both(qT_hi, qT_lo, par, cols),
                        both(kT_hi, kT_lo, par, slice(0, kend)), True, False)
                product(ps[:, 4 + b % 2, 0:kend],
                        (qT_hi[rows, 2, cols], qT_lo[rows, 2, cols]),
                        (kT_hi[rows, 2, 0:kend], kT_lo[rows, 2, 0:kend]), False, True).then_inc(sc_done, 1)

            def transpose_p(x, b):
                u = 4 * x + b
                pe.wait_ge(pr_ready, u + 1)
                if not isinstance(u, int) or u >= 1:
                    pe.wait_ge(pT_ready, u)
                for kt in range(b + 1):
                    last = nc.tensor.transpose(ps[:, 6, kt * P:(kt + 1) * P], pr[:, b % 2, kt * P:(kt + 1) * P],
                                               ident[:])
                last.then_inc(pT_done, 1)

            def output(x, par):
                pe.wait_ge(pT_ready, 4 * (x + 1))
                for kt in range(TT):
                    last = product(ps[:, 7, kt * P:T], (mv_hi[:, par, kt, :], mv_lo[:, par, kt, :]),
                                   both(pT_hi, pT_lo, kt, slice(kt * P, T)), kt == 0, kt == TT - 1)
                last.then_inc(o_done, 1)

            def phase(x, par, c=None, i=0, per=0):
                pe.wait_ge(qkT_ready, 4 * (x + 1))
                scores(x, par, 0)
                if not (isinstance(x, int) and x == 0):
                    output(x - 1, 1 - par)
                if c is not None:
                    project_q(c, i, per)
                scores(x, par, 1)
                transpose_p(x, 0)
                if c is not None:
                    project_kv(c, i, per)
                scores(x, par, 2)
                transpose_p(x, 1)
                if c is not None:
                    transpose_qk(x + 1, 0)
                scores(x, par, 3)
                transpose_p(x, 2)
                if c is not None:
                    transpose_qk(x + 1, 1)
                transpose_p(x, 3)

            project_q(MLA_HEAD_BASE, 0, 0)
            project_kv(MLA_HEAD_BASE, 0, 0)
            transpose_qk(0, 0)
            transpose_qk(0, 1)
            phase(0, 0, MLA_HEAD_BASE + 2)
            with pe.Fori(0, 2) as i:
                for j in (1, 2):
                    phase(j + 2 * i, j % 2, MLA_HEAD_BASE + 2 * (j + 1), i, 4)
            for x in (5, 6):
                phase(x, x % 2, MLA_HEAD_BASE + 2 * (x + 1))
            phase(MH - 1, 1)
            output(MH - 1, 1)
            linear(MLA_OUT_BASE, 0, 0, MLA_OUT_UNIT, 0, KT, (x_hi, x_lo),
                   lambda k: pe.wait_ge(o_ready, k + 1))

            mlp_ple(1, MLP1, PLE1)


def rotary(seq, dim):
    inv = np.float32(1.0) / (np.float32(10000.0) ** (np.arange(0, dim, 2, dtype=np.float32) / np.float32(dim)))
    angle = np.arange(seq, dtype=np.float32)[:, None] * inv[None, :]
    return np.cos(angle), np.sin(angle)


def decay_tables():
    gamma_log = np.log(1.0 - 2.0 ** (-5.0 - np.arange(HEADS)))
    p, x = np.arange(P)[:, None], np.arange(T)[None, :]
    seen = x // CHUNK >= p // CHUNK
    table = np.exp(gamma_log[None, :, None] * np.abs(x - p)[:, None, :]) * seen[:, None, :]
    return (table * DK ** -0.5).astype(np.float32)


def std_slots(w):
    k, m = w.shape
    return w.reshape(k // P, P, m // P, P).transpose(2, 1, 0, 3).reshape(m // P, P, k)


def wide_slots(w, rows):
    k, m = w.shape
    return w.reshape(k // P // rows, rows, P, m).transpose(0, 2, 1, 3).reshape(-1, P, rows * m)


def columns(v):
    return v.reshape(-1, P).T


def lay_out(inputs):
    def tiles(x):
        return x.T.reshape(-1, P, x.shape[0]).transpose(1, 0, 2)

    w = {k: np.asarray(v) for k, v in inputs.items()}
    w_in, w_out = w["ret_w_in"][0], w["ret_w_out"][0]
    q, k, v, gate = np.split(w_in, [D, 2 * D, 2 * D + HEADS * DV], axis=1)

    def head_out(i):
        return w_out[i * DV:(i + 1) * DV].reshape(VT, P, KT // 2, 2, P).transpose(2, 1, 3, 0, 4).reshape(-1, P, SLOT)

    def mlp_ple(L):
        parts = []
        w1, w2 = w["mlp_w1"][L], w["mlp_w2"][L]
        for c in range(QUARTERS):
            parts += [std_slots(w1[:, c * D:(c + 1) * D]), std_slots(w2[c * D:(c + 1) * D])]
        gates = std_slots(w["ple_gate_w"][L])
        pp = w["ple_proj_w"][L].reshape(PF, P, 2, 4, P).transpose(2, 1, 3, 0, 4).reshape(2, P, SLOT)
        for pos in range(PLE_SLOTS):
            parts.append(pp[PLE_PROJ.index(pos)][None] if pos in PLE_PROJ else gates[PLE_GATE.index(pos)][None])
        return parts

    parts = []
    for i in range(HEADS):
        dk, dv = slice(i * DK, (i + 1) * DK), slice(i * DV, (i + 1) * DV)
        parts += [std_slots(q[:, dk]), std_slots(k[:, dk])]
        if i:
            parts.append(head_out(i - 1))
        parts += [wide_slots(v[:, dv], 2), std_slots(gate[:, dv])]
    parts.append(head_out(HEADS - 1))
    mla_in, uq, ukv = w["mla_w_in"][0], w["mla_w_uq"][0], w["mla_w_ukv"][0]
    kv = NOPE + VD
    qn, kn = w["mla_q_norm"][0], w["mla_k_norm"][0]
    gains = [w[name][L] for L in range(2) for name in ("mix_norm", "mlp_norm", "ple_norm")]
    gains += [w["ret_gn"][0].reshape(-1), w["mla_q_a_norm"][0], w["mla_kv_a_norm"][0], qn[:NOPE], kn[:NOPE]]
    cos, sin = rotary(T, DK)
    mcos, msin = rotary(T, ROPE)
    mrope = np.stack([mcos, msin]).reshape(2, TT, P, ROPE // 2).transpose(2, 0, 1, 3)
    out = {
        "x": tiles(w["x"][0]),
        "p": np.stack([tiles(w["p"][L, 0]) for L in range(2)]),
        "gains": np.concatenate([columns(g) for g in gains], axis=1),
        "rope": np.stack([cos.T, sin.T], axis=1),
        "decay": decay_tables(),
        "ident": np.eye(P, dtype=np.float32),
        "mrope": mrope,
        "rgain": np.broadcast_to(np.stack([qn[NOPE:], kn[NOPE:]])[None], (P, 2, ROPE)),
        "weights0": np.concatenate(parts + mlp_ple(0)),
        "weights1": np.concatenate(mlp_ple(1)),
        "mla_in_q": wide_slots(mla_in[:, :QR], 2),
        "mla_in_kv": wide_slots(mla_in[:, QR:], 2),
        "mla_uq": np.concatenate([wide_slots(uq[:, c * QKD:(c + 1) * QKD], QF) for c in range(MH)]),
        "mla_ukv": np.concatenate([wide_slots(ukv[:, c * kv:(c + 1) * kv], KVF) for c in range(MH)]),
        "mla_out": std_slots(w["mla_w_out"][0]),
    }
    return {name: np.ascontiguousarray(v) for name, v in out.items()}


def kernel(**inputs):
    import concourse.bacc as bacc
    from concourse.bass_utils import run_bass_kernel_spmd

    nc = bacc.Bacc("TRN2", target_bir_lowering=False, num_devices=1)
    arrays = lay_out(inputs)
    aps = {name: nc.dram_tensor("in_" + name, v.shape, F32, kind="ExternalInput").ap() for name, v in arrays.items()}
    aps["out"] = nc.dram_tensor("out", (P, KT, T), F32, kind="ExternalOutput").ap()
    build(nc, aps)
    got = run_bass_kernel_spmd(nc, [{"in_" + name: v for name, v in arrays.items()}], core_ids=[0]).results[0]["out"]
    return got.transpose(2, 1, 0).reshape(1, T, D)
```

```python
from contextlib import ExitStack

import numpy as np

import concourse.bass as bass
from concourse import mybir
from concourse.alu_op_type import AluOpType as ALU

F32 = mybir.dt.float32
F32R = mybir.dt.float32r
ACT = mybir.ActivationFunctionType
AX = mybir.AxisListType

P = 128
D = 1024
T = 512
KT = D // P
TT = T // P
CHUNK = 64
EPS = 1e-6
RING = 4
AHEAD = 3
SLOT = 1024

HEADS = 4
DK = D // HEADS
DV = 2 * DK
VT = DV // P

MH = 8
NOPE, ROPE, VD = 128, 64, 128
QKD = NOPE + ROPE
QR, KVR = 384, 256
QF, KVF = QR // P, KVR // P
PLE = 256
PF = PLE // P
QUARTERS = 4

RET_FIRST = 12
RET_HEAD = 16
RET_SLOTS = RET_FIRST + (HEADS - 1) * RET_HEAD + 4
MLP_SLOTS = QUARTERS * 2 * KT
PLE_SLOTS = KT + 2
LAYER0_SLOTS = RET_SLOTS + MLP_SLOTS + PLE_SLOTS
MLA_IN_SLOTS = 8
MLA_HEAD_SLOTS = 2
MLA_SLOTS = MLA_IN_SLOTS + MH * MLA_HEAD_SLOTS + KT
LAYER1_SLOTS = MLP_SLOTS + PLE_SLOTS
MLA_BASE = LAYER0_SLOTS
MLA_HEAD_BASE = MLA_BASE + MLA_IN_SLOTS
MLA_OUT_BASE = MLA_HEAD_BASE + MH * MLA_HEAD_SLOTS
MLP_BASE = (RET_SLOTS, MLA_BASE + MLA_SLOTS)
PLE_BASE = (MLP_BASE[0] + MLP_SLOTS, MLP_BASE[1] + MLP_SLOTS)
SLOTS = PLE_BASE[1] + PLE_SLOTS
assert SLOTS == LAYER0_SLOTS + MLA_SLOTS + LAYER1_SLOTS

RET_FIRST_UNITS = 12
RET_HEAD_UNITS = 20
RET_UNITS = RET_FIRST_UNITS + (HEADS - 1) * RET_HEAD_UNITS + KT
MLP_UNITS = MLP_SLOTS
PLE_UNITS = KT
MLA_IN_UNITS = 4
MLP_UNIT = (RET_UNITS, RET_UNITS + MLP_UNITS + PLE_UNITS + MLA_IN_UNITS + KT)
PLE_UNIT = (MLP_UNIT[0] + MLP_UNITS, MLP_UNIT[1] + MLP_UNITS)
MLA_UNIT = PLE_UNIT[0] + PLE_UNITS
MLA_OUT_UNIT = MLA_UNIT + MLA_IN_UNITS
LATENT_BANKS = (0, 1, 2, 2, 3)
WARM_UP = 5
UB = 4
NORM_BANK = 7

MIX0, MLP0, PLE0, MIX1, MLP1, PLE1 = range(6)
G_GN = 6 * KT
G_QA = G_GN + HEADS * VT
G_KVA = G_QA + QF
G_QN = G_KVA + KVF
G_KN = G_QN + 1
GAINS = G_KN + 1


def nth(norm):
    return norm + (HEADS if norm > MIX0 else 0)


def nth_head(i):
    return 1 + i


def nth_spread(nth_norm):
    return nth_norm - (isinstance(nth_norm, int) and nth_norm > nth(MIX1))


def token_bank(nth_norm):
    return 3 if isinstance(nth_norm, int) and nth_norm == nth(MIX1) else NORM_BANK


PLE_PROJ = (3, 7)
PLE_GATE = tuple(s for s in range(KT + 2) if s not in PLE_PROJ)


def gate_unit(v, j, per):
    return RET_FIRST_UNITS - VT + v + (RET_HEAD_UNITS * (j + 1) if per else 0)


def slot_width(n):
    if MLA_BASE <= n < MLA_HEAD_BASE:
        return 2 * QR if n < MLA_BASE + 4 else 2 * (KVR + ROPE)
    if MLA_HEAD_BASE <= n < MLA_OUT_BASE:
        return KVF * (NOPE + VD) if (n - MLA_HEAD_BASE) % MLA_HEAD_SLOTS else QF * QKD
    return SLOT


RET_MARKS = 10
ATT_MARKS = 12
POOL_MARKS = 8


class Chain:

    def __init__(self, engine, sem):
        self.engine, self.sem, self.base, self.local = engine, sem, 0, 0

    def mark(self, ins):
        ins.then_inc(self.sem, 1)
        self.local += 1

    def wait(self):
        self.engine.wait_ge(self.sem, self.base + self.local)

    def enter(self, i, per):
        self.outer = self.base + self.local
        self.base, self.local = self.outer + per * i, 0

    def leave(self, per, turns):
        assert self.local == per, self.local
        self.base, self.local = self.outer + per * turns, 0


def build(nc, a):
    with ExitStack() as ctx:
        def sb(name, shape, dt=F32, scope=ctx):
            return scope.enter_context(nc.sbuf_tensor(name, shape, dt))

        def sem(name):
            return ctx.enter_context(nc.semaphore(name))

        h = sb("h", [P, KT, T])
        x_hi = sb("x_hi", [P, KT, T], F32R)
        x_lo = sb("x_lo", [P, KT, T], F32R)
        w_raw = sb("w_raw", [P, RING, SLOT])
        w_hi = sb("w_hi", [P, RING, SLOT], F32R)
        w_lo = sb("w_lo", [P, RING, SLOT], F32R)
        gains = sb("gains", [P, GAINS])
        ident = sb("ident", [P, P])
        mean_d = sb("mean_d", [P, 1])
        mean_v = sb("mean_v", [P, 1])
        sq = sb("sq", [P, 2, T])
        sq_sum = sb("sq_sum", [P, T])
        rstd = sb("rstd", [P, T])
        rstd_tok = sb("rstd_tok", [P, TT])
        head_tok = sb("head_tok", [P, TT])
        inv_tok = sb("inv_tok", [P, 2, TT])
        tmp = sb("tmp", [P, 4, T])
        t_a, t_b = tmp[:, 0:2, :], tmp[:, 2:4, :]

        with ExitStack() as ret:
            qk_hi = sb("qk_hi", [P, 4, T], F32R, ret)
            qk_lo = sb("qk_lo", [P, 4, T], F32R, ret)
            s_hi = sb("s_hi", [P, TT, T], F32R, ret)
            s_lo = sb("s_lo", [P, TT, T], F32R, ret)
            v_hi = sb("v_hi", [P, TT, DV], F32R, ret)
            v_lo = sb("v_lo", [P, TT, DV], F32R, ret)
            y_hi = sb("y_hi", [P, VT, T], F32R, ret)
            y_lo = sb("y_lo", [P, VT, T], F32R, ret)
            sg = sb("sg", [P, VT, T], F32, ret)
            decay = sb("decay", [P, HEADS, T], F32, ret)
            rope_t = sb("rope_t", [P, 2, T], F32, ret)
            gn = sb("gn", [P, VT], F32, ret)
            head_rstd = sb("head_rstd", [P, T], F32, ret)
        with ExitStack() as mlp:
            x2_hi = sb("x2_hi", [P, KT, T], F32R, mlp)
            x2_lo = sb("x2_lo", [P, KT, T], F32R, mlp)
            hid_hi = sb("hid_hi", [P, KT, T], F32R, mlp)
            hid_lo = sb("hid_lo", [P, KT, T], F32R, mlp)
            p_raw = sb("p_raw", [P, PF, T], F32, mlp)
            p_hi = sb("p_hi", [P, PF, T], F32R, mlp)
            p_lo = sb("p_lo", [P, PF, T], F32R, mlp)
            proj = sb("proj", [P, 2, T], F32, mlp)
        with ExitStack() as mla:
            qT_hi = sb("qT_hi", [P, 3, T], F32R, mla)
            qT_lo = sb("qT_lo", [P, 3, T], F32R, mla)
            kT_hi = sb("kT_hi", [P, 3, T], F32R, mla)
            kT_lo = sb("kT_lo", [P, 3, T], F32R, mla)
            mv_hi = sb("mv_hi", [P, 2, TT, VD], F32R, mla)
            mv_lo = sb("mv_lo", [P, 2, TT, VD], F32R, mla)
            pT_hi = sb("pT_hi", [P, TT, T], F32R, mla)
            pT_lo = sb("pT_lo", [P, TT, T], F32R, mla)
            c_hi = sb("c_hi", [P, QF + KVF, T], F32R, mla)
            c_lo = sb("c_lo", [P, QF + KVF, T], F32R, mla)
            c_tok = sb("c_tok", [P, TT, QR + KVR + ROPE], F32, mla)
            q_tok = c_tok[:, :, 0:QKD]
            k_tok = sb("k_tok", [P, TT, NOPE], F32, mla)
            rq_tok = sb("rq_tok", [P, TT, 2 * ROPE], F32, mla)
            rk_tok = sb("rk_tok", [P, TT, 2 * ROPE], F32, mla)
            kr_tok = sb("kr_tok", [P, TT, ROPE], F32, mla)
            qg_tok = sb("qg_tok", [P, TT, ROPE], F32, mla)
            mrope = sb("mrope", [P, 2, TT, ROPE // 2], F32, mla)
            rgain = sb("rgain", [P, 2, ROPE], F32, mla)
            half_neg = sb("half_neg", [P, TT], F32, mla)
            eps_sum = sb("eps_sum", [P, TT], F32, mla)
            c_ss = sb("c_ss", [P, 2, TT], F32, mla)
            c_rs = sb("c_rs", [P, 2, TT], F32, mla)
            q_ss = sb("q_ss", [P, TT], F32, mla)
            k_ss = sb("k_ss", [P, TT], F32, mla)
            kr_ss = sb("kr_ss", [P, TT], F32, mla)
            q_ms = sb("q_ms", [P, TT], F32, mla)
            k_ms = sb("k_ms", [P, TT], F32, mla)
            k_rs = sb("k_rs", [P, TT], F32, mla)
            qscale = sb("qscale", [P, 2, TT], F32, mla)
            att = sb("att", [P, 4, 8], F32, mla)
            pr = sb("pr", [P, 2, T], F32, mla)

        ps = ctx.enter_context(nc.psum_tensor("ps", [P, 8, 512], F32))

        operand = {n: (x2_hi, x2_lo) if n in (MIX1, MLP1) else (x_hi, x_lo) for n in range(6)}

        raw_loaded = [sem(f"raw_loaded{r}") for r in range(RING)]
        hi_done = sem("hi_done")
        lo_done = sem("lo_done")
        slot_used = sem("slot_used")
        bank_read = sem("bank_read")
        means_set = sem("means_set")
        zeros_set = sem("zeros_set")
        x_loaded = [sem(f"x_loaded{k}") for k in range(KT // 2)]
        gains_loaded = sem("gains_loaded")
        tables_loaded = sem("tables_loaded")
        sq_ready = sem("sq_ready")
        sq_added = sem("sq_added")
        xhi_ready = sem("xhi_ready")
        x_ready = sem("x_ready")
        mean_done = sem("mean_done")
        inv_ready = sem("inv_ready")
        tok_ready = sem("tok_ready")
        spread_done = sem("spread_done")
        rstd_ready = sem("rstd_ready")
        h_ready = sem("h_ready")
        chain = sem("chain")
        out_stored = sem("out_stored")
        qk_rot = sem("qk_rot")
        qkhi_ready = sem("qkhi_ready")
        qk_ready = sem("qk_ready")
        vhi_ready = sem("vhi_ready")
        s_done = sem("s_done")
        s_mul = sem("s_mul")
        shi_ready = sem("shi_ready")
        s_ready = sem("s_ready")
        sig_ready = sem("sig_ready")
        pv_done = sem("pv_done")
        osq_ready = sem("osq_ready")
        osq_added = sem("osq_added")
        y_val = sem("y_val")
        yhi_ready = sem("yhi_ready")
        y_ready = sem("y_ready")
        h_added = sem("h_added")
        sqr_ready = sem("sqr_ready")
        hidhi_ready = sem("hidhi_ready")
        hid_ready = sem("hid_ready")
        p_loaded = [sem(f"p_loaded{l}") for l in range(2)]
        phi_ready = sem("phi_ready")
        p_ready = sem("p_ready")
        psig_ready = sem("psig_ready")
        mla_loaded = sem("mla_loaded")
        css_ready = sem("css_ready")
        cinv_ready = sem("cinv_ready")
        croot_ready = sem("croot_ready")
        ckv_ready = sem("ckv_ready")
        cT_done = sem("cT_done")
        chi_ready = sem("chi_ready")
        c_ready = sem("c_ready")
        kr_ready = sem("kr_ready")
        qtok_ready = sem("qtok_ready")
        ktok_ready = sem("ktok_ready")
        mvhi_ready = sem("mvhi_ready")
        mv_ready = sem("mv_ready")
        pool_chain = sem("pool_chain")
        qscale_ready = sem("qscale_ready")
        qkn_ready = sem("qkn_ready")
        qkT_done = sem("qkT_done")
        qkThi_ready = sem("qkThi_ready")
        qkT_ready = sem("qkT_ready")
        sc_done = sem("sc_done")
        nmax_ready = sem("nmax_ready")
        exp_ready = sem("exp_ready")
        pr_ready = sem("pr_ready")
        pT_done = sem("pT_done")
        pThi_ready = sem("pThi_ready")
        pT_ready = sem("pT_ready")
        o_done = sem("o_done")
        ohi_ready = sem("ohi_ready")
        o_ready = sem("o_ready")

        block = ctx.enter_context(nc.Block())

        def mla_source(n):
            s = n - MLA_BASE
            if s < 4:
                return a["mla_in_q"][s]
            if s < MLA_IN_SLOTS:
                return a["mla_in_kv"][s - 4]
            s = n - MLA_HEAD_BASE
            if s < MH * MLA_HEAD_SLOTS:
                return a["mla_ukv"][s // 2] if s % 2 else a["mla_uq"][s // 2]
            return a["mla_out"][n - MLA_OUT_BASE]

        def walk(engine, one, w, first, count):
            head = RING if first == 0 else -first % RING
            for j in range(head):
                one(first + j, (first + j) % RING, w[j], (first + j) // RING)
            turns = (count - head) // RING
            with engine.Fori(0, turns) as i:
                for r in range(RING):
                    one(first + head + r + RING * i, r,
                        w[bass.ds(head + r + RING * i, 1)].rearrange("a p n -> (a p) n"),
                        (first + head) // RING + i)
            for j in range(head + turns * RING, count):
                one(first + j, (first + j) % RING, w[j], (first + j) // RING)

        @block.sync
        def _(sp):
            def load_x(j):
                sp.dma_start(h[:, 2 * j:2 * j + 2, :], a["x"][:, 2 * j:2 * j + 2, :]).then_inc(x_loaded[j], 16)

            def load_start(n):
                if n == 0:
                    sp.dma_start(gains[:], a["gains"]).then_inc(gains_loaded, 16)
                elif n == 1:
                    load_x(0)
                elif n == 2:
                    for j in range(1, KT // 2):
                        load_x(j)
                elif n == 3:
                    sp.dma_start(rope_t[:], a["rope"]).then_inc(tables_loaded, 16)
                    sp.dma_start(ident[:], a["ident"]).then_inc(tables_loaded, 16)
                    sp.dma_start(decay[:], a["decay"]).then_inc(tables_loaded, 16)

            def load(n, r, source, turn):
                width = slot_width(n) if isinstance(n, int) else SLOT
                if isinstance(n, int) and n < RING:
                    load_start(n)
                if not isinstance(n, int) or n >= RING:
                    sp.wait_ge(lo_done, n - (RING - 1))
                sp.dma_start(w_raw[:, r, 0:width], source).then_inc(raw_loaded[r], 16)
            walk(sp, load, a["weights0"], 0, LAYER0_SLOTS)
            for n in range(MLA_BASE, MLP_BASE[1]):
                load(n, n % RING, mla_source(n), n // RING)
            walk(sp, load, a["weights1"], MLP_BASE[1], LAYER1_SLOTS)
            for k in range(KT):
                sp.wait_ge(h_ready, KT + k + 1)
                sp.dma_start(a["out"][:, k, :], h[:, k, :]).then_inc(out_stored, 16)
            sp.wait_ge(out_stored, 16 * KT)

        @block.gpsimd
        def _(pool):
            nc.gpsimd.memset(mean_d[:], 1.0 / D).then_inc(means_set, 1)
            nc.gpsimd.memset(mean_v[:], 1.0 / DV).then_inc(means_set, 1)

            def low(n, r, source, turn):
                width = slot_width(n) if isinstance(n, int) else SLOT
                pool.wait_ge(hi_done, n + 1)
                nc.gpsimd.tensor_tensor(w_lo[:, r, 0:width], w_raw[:, r, 0:width],
                                        w_hi[:, r, 0:width].bitcast(F32), ALU.subtract).then_inc(lo_done, 1)
            walk(pool, low, a["weights0"], 0, LAYER0_SLOTS)

            own = Chain(pool, pool_chain)

            def low_at(c, i=0, per=0):
                width, r = slot_width(c), c % RING
                pool.wait_ge(hi_done, c + 1 + per * i)
                nc.gpsimd.tensor_tensor(w_lo[:, r, 0:width], w_raw[:, r, 0:width],
                                        w_hi[:, r, 0:width].bitcast(F32), ALU.subtract).then_inc(lo_done, 1)

            for n in range(MLA_BASE, MLA_HEAD_BASE):
                low_at(n)
            pool.wait_ge(tok_ready, nth(MIX1) + 1)
            own.mark(nc.gpsimd.memset(rq_tok[:], 0.0))
            own.mark(nc.gpsimd.memset(rk_tok[:], 0.0))
            own.mark(nc.gpsimd.memset(half_neg[:], -0.5))
            own.mark(nc.gpsimd.memset(eps_sum[:], QKD * EPS))
            for n in range(MLA_HEAD_BASE, MLA_HEAD_BASE + AHEAD):
                low_at(n)
            pool.wait_ge(mla_loaded, 32)

            def by_token(x, width):
                return x.unsqueeze(2).to_broadcast([P, TT, width])

            def project(y, par, c, i=0, per=0):
                half = ROPE // 2
                cos, sin = mrope[:, 0, :, :], mrope[:, 1, :, :]
                mine = slice(par * ROPE, (par + 1) * ROPE)
                first, second = (slice(par * ROPE + o, par * ROPE + o + half) for o in (0, half))
                m1 = tmp[:, 2, 0:TT * half].rearrange("p (t c) -> p t c", t=TT)
                m2 = tmp[:, 3, 0:TT * half].rearrange("p (t c) -> p t c", t=TT)
                pool.wait_ge(qtok_ready, 6 * y + 2)
                own.mark(nc.gpsimd.tensor_tensor(qg_tok[:], q_tok[:, :, NOPE:QKD],
                                                 rgain[:, 0:1, :].to_broadcast([P, TT, ROPE]), ALU.mult))
                own.wait()
                x1, x2 = qg_tok[:, :, 0:half], qg_tok[:, :, half:ROPE]
                own.mark(nc.gpsimd.tensor_tensor(rq_tok[:, :, first], x1, cos, ALU.mult))
                own.mark(nc.gpsimd.tensor_tensor(m1, x2, sin, ALU.mult))
                own.mark(nc.gpsimd.tensor_tensor(rq_tok[:, :, second], x2, cos, ALU.mult))
                own.mark(nc.gpsimd.tensor_tensor(m2, x1, sin, ALU.mult))
                own.wait()
                nc.gpsimd.tensor_tensor(rq_tok[:, :, first], rq_tok[:, :, first], m1,
                                        ALU.subtract).then_inc(qkn_ready, 1)
                nc.gpsimd.tensor_tensor(rq_tok[:, :, second], rq_tok[:, :, second], m2,
                                        ALU.add).then_inc(qkn_ready, 1)
                if isinstance(y, int) and y == 0:
                    pool.wait_ge(kr_ready, 1)
                pool.wait_ge(ktok_ready, 6 * (y + 1))
                own.mark(nc.gpsimd.tensor_tensor(k_ms[:], k_ss[:], kr_ss[:], ALU.add))
                own.wait()
                own.mark(nc.gpsimd.tensor_tensor(k_rs[:], k_ms[:], half_neg[:], ALU.pow))
                own.wait()
                nc.gpsimd.tensor_tensor(k_tok[:], k_tok[:], by_token(k_rs[:], NOPE),
                                        ALU.mult).then_inc(qkn_ready, 1)
                nc.gpsimd.tensor_tensor(rk_tok[:, :, mine], kr_tok[:], by_token(k_rs[:], ROPE),
                                        ALU.mult).then_inc(qkn_ready, 1)
                pool.wait_ge(qtok_ready, 6 * (y + 1))
                own.mark(nc.gpsimd.tensor_tensor(q_ms[:], q_ss[:], eps_sum[:], ALU.add))
                own.wait()
                nc.gpsimd.tensor_tensor(qscale[:, par, :], q_ms[:], half_neg[:], ALU.pow).then_inc(qscale_ready, 1)
                low_at(c + AHEAD, i, per)
                low_at(c + 1 + AHEAD, i, per)

            for y in (0, 1):
                project(y, y, MLA_HEAD_BASE + 2 * y)
            with pool.Fori(0, 2) as i:
                own.enter(i, 2 * POOL_MARKS)
                for j in (0, 1):
                    project(2 + j + 2 * i, j, MLA_HEAD_BASE + 4 + 2 * j, i, 4)
            own.leave(2 * POOL_MARKS, 2)
            for y in (6, 7):
                project(y, y % 2, MLA_HEAD_BASE + 2 * y)
            for n in range(MLA_OUT_BASE + AHEAD, MLP_BASE[1]):
                low_at(n)
            walk(pool, low, a["weights1"], MLP_BASE[1], LAYER1_SLOTS)

        @block.scalar
        def _(act):
            def w_high(c, i=0, per=0):
                if c >= SLOTS:
                    return
                width, r = slot_width(c), c % RING
                if c >= RING:
                    act.wait_ge(slot_used, c - (RING - 1) + per * i)
                act.wait_ge(raw_loaded[r], 16 * (c // RING + 1 + (per // RING) * i))
                nc.scalar.activation(w_hi[:, r, 0:width], w_raw[:, r, 0:width], ACT.Copy).then_inc(hi_done, 1)

            def step(n, i=0, per=0):
                w_high(n + AHEAD, i, per)

            def finish(norm, k):
                n = norm * KT + k
                if n >= 2:
                    act.wait_ge(sq_added, n - 1)
                nc.scalar.activation(sq[:, k % 2, :], h[:, k, :], ACT.Square).then_inc(sq_ready, 1)
                nc.scalar.activation(operand[norm][0][:, k, :], h[:, k, :], ACT.Copy,
                                     scale=gains[:, n:n + 1]).then_inc(xhi_ready, 1)

            def root(n, dst):
                act.wait_ge(inv_ready, n + 1)
                nc.scalar.activation(dst[:], inv_tok[:, 1, :], ACT.Sqrt).then_inc(tok_ready, 1)

            w_high(0)
            act.wait_ge(gains_loaded, 16)
            for k in range(KT):
                act.wait_ge(x_loaded[k // 2], 16)
                finish(MIX0, k)
                if k in (0, 4):
                    w_high(k // 4 + 1)

            def ret_output(i):
                def high(v):
                    act.wait_ge(y_val, VT * i + v + 1)
                    nc.scalar.activation(y_hi[:, v, :], sg[:, v, :], ACT.Copy).then_inc(yhi_ready, 1)
                for v in range(VT):
                    act.wait_ge(pv_done, VT * i + v + 1)
                    if v >= 2:
                        act.wait_ge(osq_added, VT * i + v - 1)
                    nc.scalar.activation(sq[:, v % 2, :], ps[:, 4 + v, :], ACT.Square).then_inc(osq_ready, 1)
                    if v >= 1:
                        high(v - 1)
                high(VT - 1)

            def ret_rotated(i, first):
                for j in range(2):
                    act.wait_ge(qk_rot, 4 * i + first + j + 1)
                    nc.scalar.activation(qk_hi[:, first + j, :], t_a[:, j, :], ACT.Copy).then_inc(qkhi_ready, 1)

            def ret_head(i, n, j, per):
                first = per == 0
                step(n, j, per)
                if first:
                    root(nth(MIX0), rstd_tok)
                else:
                    root(nth_head(i - 1), head_tok)
                step(n + 1, j, per)
                step(n + 2, j, per)
                ret_rotated(i, 0)
                step(n + 3, j, per)
                n += 4
                if not first:
                    step(n, j, per)
                ret_rotated(i, 2)
                if not first:
                    for m in range(1, 4):
                        step(n + m, j, per)
                    n += 4
                for m in range(4):
                    step(n + m, j, per)
                n += 4
                step(n, j, per)
                act.wait_ge(tok_ready, nth(MIX0) + 1)
                for t in range(TT):
                    nc.scalar.activation(v_hi[:, t, :], ps[:, t, :], ACT.Copy,
                                         scale=rstd_tok[:, t:t + 1]).then_inc(vhi_ready, 1)
                for kt in range(TT):
                    act.wait_ge(s_mul, TT * i + kt + 1)
                    nc.scalar.activation(s_hi[:, kt, kt * P:T], tmp[:, kt, kt * P:T],
                                         ACT.Copy).then_inc(shi_ready, 1)
                for v in range(VT):
                    if v + 1 < VT:
                        step(n + v + 1, j, per)
                    act.wait_ge(bank_read, gate_unit(v, j, per) + 1)
                    nc.scalar.activation(t_b[:, v % 2, :], t_a[:, v % 2, :], ACT.Sigmoid).then_inc(sig_ready, 1)
                ret_output(i)

            ret_head(0, 0, 0, 0)
            with act.Fori(1, HEADS) as i:
                ret_head(i, RET_FIRST, i - 1, RET_HEAD)
            n = RET_SLOTS - 4
            for m in range(5):
                if m < 4:
                    step(n + m)
                if m == 0:
                    root(nth_head(HEADS - 1), head_tok)
                else:
                    for k in (2 * m - 2, 2 * m - 1):
                        act.wait_ge(h_added, (HEADS - 1) * KT + k + 1)
                        finish(MLP0, k)

            def hidden(L, q, m):
                act.wait_ge(bank_read, MLP_UNIT[L] + 2 * KT * q + m + 1)
                done = KT * QUARTERS * L + KT * q + m + 1
                nc.scalar.activation(t_b[:, m % 2, :], t_a[:, m % 2, :], ACT.Square).then_inc(sqr_ready, 1)
                act.wait_ge(sqr_ready, done)
                nc.scalar.activation(hid_hi[:, m, :], t_b[:, m % 2, :], ACT.Copy).then_inc(hidhi_ready, 1)

            def mlp_quarter(L, q, looped, start=None, norm=None):
                for s in range(2 * KT):
                    if looped:
                        step(MLP_BASE[L] + s, q, 2 * KT)
                    else:
                        step(MLP_BASE[L] + 2 * KT * q + s)
                    if start is not None and s == 0:
                        start()
                    if 1 <= s <= KT:
                        hidden(L, q, s - 1)
                    if norm is not None and s > KT:
                        act.wait_ge(bank_read, MLP_UNIT[L] + 2 * KT * q + s)
                        finish(norm, s - KT - 1)
                if norm is not None:
                    act.wait_ge(bank_read, MLP_UNIT[L] + MLP_UNITS)
                    finish(norm, KT - 1)

            def mlp_act(L, mlp_norm, ple_norm, before):
                def start():
                    before()
                    root(nth(mlp_norm), rstd_tok)
                mlp_quarter(L, 0, False, start)
                with act.Fori(1, QUARTERS - 1) as q:
                    mlp_quarter(L, q, True)
                mlp_quarter(L, QUARTERS - 1, False, None, ple_norm)

            def ple_act(L, norm, next_norm):
                act.wait_ge(p_loaded[L], 16)
                for f in range(PF):
                    nc.scalar.activation(p_hi[:, f, :], p_raw[:, f, :], ACT.Copy).then_inc(phi_ready, 1)
                m = 0
                for s in range(PLE_SLOTS):
                    step(PLE_BASE[L] + s)
                    if s == 0:
                        root(nth(norm), rstd_tok)
                    if s > 0 and s - 1 not in PLE_PROJ:
                        ple_gate(L, m, next_norm)
                        m += 1
                ple_gate(L, m, next_norm)
                if next_norm is not None:
                    act.wait_ge(h_ready, KT * L + KT)
                    finish(next_norm, KT - 1)

            def ple_gate(L, m, next_norm):
                act.wait_ge(bank_read, PLE_UNIT[L] + m + 1)
                nc.scalar.activation(t_b[:, m % 2, :], t_a[:, m % 2, :], ACT.Sigmoid).then_inc(psig_ready, 1)
                if next_norm is not None and m >= 1:
                    act.wait_ge(h_ready, KT * L + m)
                    finish(next_norm, m - 1)

            def load_p(L, slots):
                def go():
                    act.wait_ge(slot_used, slots)
                    act.dma_start(p_raw[:], a["p"][L]).then_inc(p_loaded[L], 16)
                return go

            mlp_act(0, MLP0, PLE0, load_p(0, RET_SLOTS))
            ple_act(0, PLE0, MIX1)

            act.wait_ge(slot_used, MLA_BASE)
            act.dma_start(mrope[:], a["mrope"]).then_inc(mla_loaded, 16)
            act.dma_start(rgain[:], a["rgain"]).then_inc(mla_loaded, 16)
            for s in range(5):
                step(MLA_BASE + s)

            def square_sums(j, first_bank, width):
                for t in range(TT):
                    if j or t:
                        act.wait_ge(css_ready, 4 * j + t)
                    nc.scalar.activation(junk[:, 0:width], ps[:, first_bank + t, 0:width], ACT.Square,
                                         scale=rstd_tok[:, t:t + 1],
                                         accum_out=c_ss[:, j, t:t + 1]).then_inc(css_ready, 1)

            def latent_root(j):
                act.wait_ge(cinv_ready, j + 1)
                nc.scalar.activation(c_rs[:, j, :], c_ss[:, j, :], ACT.Sqrt).then_inc(croot_ready, 1)

            def latent_high(f):
                act.wait_ge(cT_done, f + 1)
                nc.scalar.activation(c_hi[:, f, :], ps[:, LATENT_BANKS[f], :], ACT.Copy,
                                     scale=gains[:, G_QA + f:G_QA + f + 1]).then_inc(chi_ready, 1)

            junk = sq[:].rearrange("p a t -> p (a t)")
            act.wait_ge(slot_used, MLA_BASE + 4)
            root(nth(MIX1), rstd_tok)
            act.wait_ge(tok_ready, nth(MIX1) + 1)
            square_sums(0, 0, QR)
            latent_root(0)
            for s in range(5, MLA_IN_SLOTS):
                step(MLA_BASE + s)
            for f in range(QF):
                latent_high(f)
            act.wait_ge(slot_used, MLA_HEAD_BASE)
            square_sums(1, 4, KVR)
            latent_root(1)
            def copy_q(y, c, i, per):
                act.wait_ge(slot_used, c + 1 + per * i)
                for b in range(2):
                    nc.scalar.activation(q_tok[:, 2 * b:2 * b + 2, :],
                                         ps[:, b, 0:2 * QKD].rearrange("p (t c) -> p t c", t=2),
                                         ACT.Copy).then_inc(qtok_ready, 1)

            def square_q():
                for t in range(TT):
                    lo = t % 2 * QKD
                    nc.scalar.activation(junk[:, t * QKD:(t + 1) * QKD], ps[:, t // 2, lo:lo + QKD], ACT.Square,
                                         accum_out=q_ss[:, t:t + 1]).then_inc(qtok_ready, 1)

            kv = NOPE + VD
            kv_banks = [ps[:, 2 + b, :].rearrange("p (t c) -> p t c", t=2) for b in range(2)]

            def square_k(c, i, per):
                act.wait_ge(slot_used, c + 2 + per * i)
                for t in range(TT):
                    lo = t % 2 * kv
                    nc.scalar.activation(tmp[:, 0, t * NOPE:(t + 1) * NOPE], ps[:, 2 + t // 2, lo:lo + NOPE],
                                         ACT.Square, scale=QKD ** -0.5,
                                         accum_out=k_ss[:, t:t + 1]).then_inc(ktok_ready, 1)

            def copy_k():
                for b in range(2):
                    nc.scalar.activation(k_tok[:, 2 * b:2 * b + 2, :], kv_banks[b][:, :, 0:NOPE],
                                         ACT.Copy).then_inc(ktok_ready, 1)

            def copy_v(y, par):
                if not isinstance(y, int) or y >= 2:
                    act.wait_ge(o_done, y - 1)
                for b in range(2):
                    nc.scalar.activation(mv_hi[:, par, 2 * b:2 * b + 2, :], kv_banks[b][:, :, NOPE:kv],
                                         ACT.Copy).then_inc(mvhi_ready, 1)

            def transposed_qk(y, par, which):
                dst, gain = (qT_hi, G_QN) if which == 0 else (kT_hi, G_KN)
                act.wait_ge(qkT_done, 4 * y + 2 * which + 1)
                nc.scalar.activation(dst[:, par, :], ps[:, 2 * which, :], ACT.Copy,
                                     scale=gains[:, gain:gain + 1]).then_inc(qkThi_ready, 1)
                rows = slice(par * ROPE, (par + 1) * ROPE)
                act.wait_ge(qkT_done, 4 * y + 2 * which + 2)
                nc.scalar.activation(dst[rows, 2, :], ps[rows, 2 * which + 1, :], ACT.Copy).then_inc(qkThi_ready, 1)

            def exponent(x, par, b):
                kend, u = (b + 1) * P, 4 * par + b
                act.wait_ge(nmax_ready, 4 * x + b + 1)
                if not isinstance(x, int) or 4 * x + b >= 2:
                    act.wait_ge(pT_done, 4 * x + b - 1)
                nc.scalar.activation(pr[:, b % 2, 0:kend], ps[:, 4 + b % 2, 0:kend], ACT.Exp,
                                     bias=att[:, 1, u:u + 1], scale=qscale[:, par, b:b + 1],
                                     accum_out=att[:, 2, u:u + 1]).then_inc(exp_ready, 1)

            def transposed_p(x, b):
                act.wait_ge(pT_done, 4 * x + b + 1)
                nc.scalar.activation(pT_hi[:, 0:b + 1, b * P:(b + 1) * P],
                                     ps[:, 6, 0:(b + 1) * P].rearrange("p (k q) -> p k q", k=b + 1),
                                     ACT.Copy).then_inc(pThi_ready, 1)

            def output(x):
                act.wait_ge(o_done, x + 1)
                dst = x_hi[:, x, :] if isinstance(x, int) else x_hi[:, bass.ds(x, 1), :].rearrange("p a t -> p (a t)")
                nc.scalar.activation(dst, ps[:, 7, :], ACT.Copy).then_inc(ohi_ready, 1)

            def phase(x, par, c=None, i=0, per=0):
                first = isinstance(x, int) and x == 0
                if c is not None:
                    copy_q(x + 1, c, i, per)
                exponent(x, par, 0)
                exponent(x, par, 1)
                if not first:
                    transposed_p(x - 1, 3)
                if c is not None:
                    square_q()
                    square_k(c, i, per)
                else:
                    step(MLA_OUT_BASE)
                transposed_p(x, 0)
                if c is not None:
                    copy_k()
                    copy_v(x + 1, 1 - par)
                if not first:
                    output(x - 1)
                transposed_p(x, 1)
                exponent(x, par, 2)
                if c is not None:
                    transposed_qk(x + 1, 1 - par, 0)
                transposed_p(x, 2)
                if c is not None:
                    transposed_qk(x + 1, 1 - par, 1)
                exponent(x, par, 3)
                if c is not None:
                    step(c, i, per)
                    step(c + 1, i, per)

            copy_q(0, MLA_HEAD_BASE, 0, 0)
            for f in range(QF, QF + KVF):
                latent_high(f)
            square_q()
            act.wait_ge(kr_ready, 1)
            square_k(MLA_HEAD_BASE, 0, 0)
            copy_k()
            copy_v(0, 0)
            transposed_qk(0, 0, 0)
            transposed_qk(0, 0, 1)
            step(MLA_HEAD_BASE)
            step(MLA_HEAD_BASE + 1)
            phase(0, 0, MLA_HEAD_BASE + 2)
            with act.Fori(0, 2) as i:
                for j in (1, 2):
                    phase(j + 2 * i, j % 2, MLA_HEAD_BASE + 2 * (j + 1), i, 4)
            for x in (5, 6):
                phase(x, x % 2, MLA_HEAD_BASE + 2 * (x + 1))
            phase(MH - 1, 1)
            transposed_p(MH - 1, 3)
            output(MH - 1)
            for m in range(KT):
                if m >= 1:
                    step(MLA_OUT_BASE + m)
                if m >= 1:
                    act.wait_ge(bank_read, MLA_OUT_UNIT + m)
                    finish(MLP1, m - 1)
            act.wait_ge(bank_read, MLA_OUT_UNIT + KT)
            finish(MLP1, KT - 1)

            mlp_act(1, MLP1, PLE1, load_p(1, MLA_BASE + MLA_SLOTS))
            ple_act(1, PLE1, None)

        @block.vector
        def _(dve):
            own = Chain(dve, chain)

            def finish(norm, k):
                n = norm * KT + k
                dve.wait_ge(sq_ready, n + 1)
                if k == 0:
                    nc.vector.tensor_copy(sq_sum[:], sq[:, 0, :]).then_inc(sq_added, 1)
                else:
                    dve.wait_ge(sq_added, n)
                    nc.vector.tensor_tensor(sq_sum[:], sq_sum[:], sq[:, k % 2, :], ALU.add).then_inc(sq_added, 1)
                dve.wait_ge(xhi_ready, n + 1)
                hi, lo = operand[norm]
                nc.vector.scalar_tensor_tensor(lo[:, k, :], h[:, k, :], gains[:, n:n + 1],
                                               hi[:, k, :].bitcast(F32), ALU.mult, ALU.subtract
                                               ).then_inc(x_ready, 1)

            def inverse(n):
                dve.wait_ge(mean_done, n + 1)
                own.mark(nc.vector.tensor_scalar(inv_tok[:, 0, :], ps[:, token_bank(n), T - TT:T], EPS, None, ALU.add))
                own.wait()
                nc.vector.reciprocal(inv_tok[:, 1, :], inv_tok[:, 0, :]).then_inc(inv_ready, 1)

            def norm_scale(n, dst):
                inverse(n)
                dve.wait_ge(spread_done, nth_spread(n) + 1)
                nc.vector.tensor_copy(dst, ps[:, NORM_BANK, :]).then_inc(rstd_ready, 1)
                dve.wait_ge(rstd_ready, nth_spread(n) + 1)

            nc.vector.memset(tmp[:, 0, :], 0.0).then_inc(zeros_set, 1)
            dve.wait_ge(gains_loaded, 16)
            for k in range(KT):
                dve.wait_ge(x_loaded[k // 2], 16)
                finish(MIX0, k)

            def rotate(i, first, unit):
                one, two = ps[:, first, :], ps[:, first + 1, :]
                cos, sin = rope_t[:, 0, :], rope_t[:, 1, :]
                if first:
                    dve.wait_ge(qk_ready, 4 * i + 2)
                own.mark(nc.vector.tensor_tensor(t_a[:, 0, :], one, cos, ALU.mult))
                nc.vector.tensor_tensor(t_b[:, 1, :], one, sin, ALU.mult).then_inc(bank_read, 1)
                own.mark(nc.vector.tensor_tensor(t_b[:, 0, :], two, sin, ALU.mult))
                nc.vector.tensor_tensor(t_a[:, 1, :], two, cos, ALU.mult).then_inc(bank_read, 1)
                own.wait()
                nc.vector.tensor_tensor(t_a[:, 0, :], t_a[:, 0, :], t_b[:, 0, :], ALU.subtract).then_inc(qk_rot, 1)
                dve.wait_ge(bank_read, unit + 2)
                nc.vector.tensor_tensor(t_a[:, 1, :], t_a[:, 1, :], t_b[:, 1, :], ALU.add).then_inc(qk_rot, 1)
                for j in range(2):
                    dve.wait_ge(qkhi_ready, 4 * i + first + j + 1)
                    nc.vector.tensor_tensor(qk_lo[:, first + j, :], t_a[:, j, :],
                                            qk_hi[:, first + j, :].bitcast(F32), ALU.subtract).then_inc(qk_ready, 1)

            def ret_output(i):
                def low(v):
                    dve.wait_ge(yhi_ready, VT * i + v + 1)
                    nc.vector.tensor_tensor(y_lo[:, v, :], sg[:, v, :], y_hi[:, v, :].bitcast(F32),
                                            ALU.subtract).then_inc(y_ready, 1)
                for v in range(VT):
                    dve.wait_ge(osq_ready, VT * i + v + 1)
                    nc.vector.tensor_tensor(sg[:, v, :], sg[:, v, :], ps[:, 4 + v, :], ALU.mult).then_inc(y_val, 1)
                    if v == 0:
                        nc.vector.tensor_copy(sq_sum[:], sq[:, 0, :]).then_inc(osq_added, 1)
                    else:
                        dve.wait_ge(osq_added, VT * i + v)
                        nc.vector.tensor_tensor(sq_sum[:], sq_sum[:], sq[:, v % 2, :],
                                                ALU.add).then_inc(osq_added, 1)
                        low(v - 1)
                low(VT - 1)

            def add_head_to_h(i, k, n, unit):
                dve.wait_ge(slot_used, n + k // 2 + 1)
                if k >= 2:
                    dve.wait_ge(h_added, KT * i + k - 1)
                nc.vector.tensor_tensor(t_b[:, k % 2, :], ps[:, k % UB, :], head_rstd[:], ALU.mult
                                        ).then_inc(bank_read, 1)
                dve.wait_ge(bank_read, unit + k + 1)
                nc.vector.tensor_tensor(h[:, k, :], h[:, k, :], t_b[:, k % 2, :], ALU.add).then_inc(h_added, 1)

            def add_to_h(k, bank, unit):
                nc.vector.tensor_tensor(h[:, k, :], h[:, k, :], ps[:, bank, :], ALU.add).then_inc(bank_read, 1)

            def ret_head(i, n, j, per, unit, uper):
                first = per == 0
                n, unit = n + per * j, unit + uper * j
                if first:
                    norm_scale(nth(MIX0), rstd[:])
                    dve.wait_ge(tables_loaded, 48)
                    for c in range(2):
                        own.mark(nc.vector.tensor_tensor(rope_t[:, c, :], rope_t[:, c, :], rstd[:], ALU.mult))
                    own.wait()
                else:
                    norm_scale(nth_head(i - 1), head_rstd[:])
                own.mark(nc.vector.tensor_copy(gn[:], gains[:, G_GN + VT * i:G_GN + VT * (i + 1)]
                                               if isinstance(i, int) else gains[:, bass.ds(G_GN + VT * i, VT)]))
                dve.wait_ge(slot_used, n + 2)
                rotate(i, 0, unit)
                dve.wait_ge(slot_used, n + 4)
                rotate(i, 2, unit + 2)
                n, unit = n + 4, unit + 4
                if not first:
                    dve.wait_ge(qk_ready, 4 * (i + 1))
                    for k in range(KT):
                        add_head_to_h(i - 1, k, n, unit)
                    n, unit = n + 4, unit + KT
                n = n + 4
                dve.wait_ge(slot_used, n)
                for t in range(TT):
                    dve.wait_ge(vhi_ready, TT * i + t + 1)
                    nc.vector.scalar_tensor_tensor(v_lo[:, t, :], ps[:, t, :], rstd_tok[:, t:t + 1],
                                                   v_hi[:, t, :].bitcast(F32), ALU.mult, ALU.subtract
                                                   ).then_inc(bank_read, 1)
                unit = unit + TT

                def low(kt):
                    dve.wait_ge(shi_ready, TT * i + kt + 1)
                    nc.vector.tensor_tensor(s_lo[:, kt, kt * P:T], tmp[:, kt, kt * P:T],
                                            s_hi[:, kt, kt * P:T].bitcast(F32), ALU.subtract).then_inc(s_ready, 1)
                for kt in range(TT):
                    w = T - kt * P
                    table = (decay[:, i, 0:w] if isinstance(i, int)
                             else decay[:, bass.ds(i, 1), 0:w].rearrange("p a t -> p (a t)"))
                    dve.wait_ge(s_done, TT * i + kt + 1)
                    nc.vector.tensor_tensor(tmp[:, kt, kt * P:T], ps[:, 4 + kt, 0:w], table,
                                            ALU.mult).then_inc(s_mul, 1)
                    if kt >= 1:
                        low(kt - 1)
                low(TT - 1)

                def silu(v):
                    dve.wait_ge(sig_ready, VT * i + v + 1)
                    own.mark(nc.vector.scalar_tensor_tensor(sg[:, v, :], t_a[:, v % 2, :], gn[:, v:v + 1],
                                                            t_b[:, v % 2, :], ALU.mult, ALU.mult))
                dve.wait_ge(s_ready, TT * (i + 1))
                for v in range(VT):
                    dve.wait_ge(slot_used, n + v + 1)
                    if v >= 2:
                        own.wait()
                    nc.vector.tensor_tensor(t_a[:, v % 2, :], ps[:, v, :], rstd[:], ALU.mult).then_inc(bank_read, 1)
                    if v >= 1:
                        silu(v - 1)
                dve.wait_ge(bank_read, unit + VT)
                silu(VT - 1)
                own.wait()
                ret_output(i)

            ret_head(0, 0, 0, 0, 0, 0)
            with dve.Fori(1, HEADS) as i:
                own.enter(i - 1, RET_MARKS)
                ret_head(i, RET_FIRST, i - 1, RET_HEAD, RET_FIRST_UNITS, RET_HEAD_UNITS)
            own.leave(RET_MARKS, HEADS - 1)
            norm_scale(nth_head(HEADS - 1), head_rstd[:])
            for k in range(KT):
                add_head_to_h(HEADS - 1, k, RET_SLOTS - 4, RET_UNITS - KT)
                if k >= 2:
                    finish(MLP0, k - 2)
            finish(MLP0, KT - 2)
            finish(MLP0, KT - 1)

            def mlp_quarter(L, q, norm=None):
                n, unit = MLP_BASE[L] + 2 * KT * q, MLP_UNIT[L] + 2 * KT * q

                def low(m):
                    dve.wait_ge(hidhi_ready, KT * QUARTERS * L + KT * q + m + 1)
                    nc.vector.tensor_tensor(hid_lo[:, m, :], t_b[:, m % 2, :], hid_hi[:, m, :].bitcast(F32),
                                            ALU.subtract).then_inc(hid_ready, 1)
                for m in range(KT):
                    dve.wait_ge(slot_used, n + m + 1)
                    nc.vector.scalar_tensor_tensor(t_a[:, m % 2, :], ps[:, m % UB, :], 0.0, rstd[:],
                                                   ALU.max, ALU.mult).then_inc(bank_read, 1)
                    if m >= 1:
                        low(m - 1)
                low(KT - 1)
                for m in range(KT):
                    dve.wait_ge(slot_used, n + KT + m + 1)
                    add_to_h(m, m % UB, unit + KT + m)
                    if norm is not None and m >= 1:
                        finish(norm, m - 1)
                if norm is not None:
                    finish(norm, KT - 1)

            def ple(L, norm, next_norm):
                for f in range(PF):
                    dve.wait_ge(phi_ready, PF * L + f + 1)
                    nc.vector.tensor_tensor(p_lo[:, f, :], p_raw[:, f, :], p_hi[:, f, :].bitcast(F32),
                                            ALU.subtract).then_inc(p_ready, 1)
                norm_scale(nth(norm), rstd[:])

                def mix(m):
                    dve.wait_ge(slot_used, PLE_BASE[L] + PLE_PROJ[m // 4] + 1)
                    dve.wait_ge(psig_ready, KT * L + m + 1)
                    if m >= 2:
                        dve.wait_ge(h_ready, KT * L + m - 1)
                    own.mark(nc.vector.tensor_tensor(proj[:, m % 2, :], t_b[:, m % 2, :], ps[:, 4 + m % 4, :],
                                                     ALU.mult))
                    own.wait()
                    nc.vector.tensor_tensor(h[:, m, :], h[:, m, :], proj[:, m % 2, :], ALU.add).then_inc(h_ready, 1)
                    if next_norm is not None:
                        finish(next_norm, m)
                for m in range(KT):
                    dve.wait_ge(slot_used, PLE_BASE[L] + PLE_GATE[m] + 1)
                    nc.vector.tensor_tensor(t_a[:, m % 2, :], ps[:, m % UB, :], rstd[:],
                                            ALU.mult).then_inc(bank_read, 1)
                    if m >= 1:
                        mix(m - 1)
                mix(KT - 1)

            def mlp_ple(L, mlp_norm, ple_norm, next_norm):
                norm_scale(nth(mlp_norm), rstd[:])
                with dve.Fori(0, QUARTERS - 1) as q:
                    mlp_quarter(L, q)
                mlp_quarter(L, QUARTERS - 1, ple_norm)
                ple(L, ple_norm, next_norm)

            mlp_ple(0, MLP0, PLE0, MIX1)

            C = QR + KVR + ROPE
            inverse(nth(MIX1))

            def latent_scale(j, width):
                dve.wait_ge(css_ready, 4 * (j + 1))
                own.mark(nc.vector.tensor_scalar(c_rs[:, j, :], c_ss[:, j, :], 1.0 / width, EPS, ALU.mult, ALU.add))
                own.wait()
                nc.vector.reciprocal(c_ss[:, j, :], c_rs[:, j, :]).then_inc(cinv_ready, 1)
                dve.wait_ge(croot_ready, j + 1)
                own.mark(nc.vector.tensor_tensor(c_rs[:, j, :], c_rs[:, j, :], rstd_tok[:], ALU.mult))
                own.wait()

            def latent_low(f):
                dve.wait_ge(chi_ready, f + 1)
                nc.vector.scalar_tensor_tensor(c_lo[:, f, :], ps[:, LATENT_BANKS[f], :], gains[:, G_QA + f:G_QA + f + 1],
                                               c_hi[:, f, :].bitcast(F32), ALU.mult, ALU.subtract
                                               ).then_inc(c_ready, 1)

            latent_scale(0, QR)
            for t in range(TT):
                nc.vector.tensor_scalar(c_tok[:, t, 0:QR], ps[:, t, 0:QR], c_rs[:, 0, t:t + 1], None,
                                        ALU.mult).then_inc(bank_read, 1)
            for f in range(QF):
                latent_low(f)
            for t in range(TT):
                dve.wait_ge(css_ready, 4 + t + 1)
                own.mark(nc.vector.tensor_scalar(c_tok[:, t, QR + KVR:C], ps[:, 4 + t, KVR:KVR + ROPE],
                                                 rstd_tok[:, t:t + 1], None, ALU.mult))
            latent_scale(1, KVR)
            for t in range(TT):
                nc.vector.tensor_scalar(c_tok[:, t, QR:QR + KVR], ps[:, 4 + t, 0:KVR], c_rs[:, 1, t:t + 1], None,
                                        ALU.mult).then_inc(ckv_ready, 1)

            for f in range(QF, QF + KVF):
                latent_low(f)

            dve.wait_ge(mla_loaded, 32)
            kr, half = c_tok[:, :, QR + KVR:C], ROPE // 2
            wide = [tmp[:, j, 0:TT * ROPE].rearrange("p (t c) -> p t c", t=TT) for j in (0, 1)]
            own.mark(nc.vector.tensor_tensor(wide[0], kr, kr, ALU.mult))
            own.mark(nc.vector.tensor_tensor(wide[1], kr, rgain[:, 1:2, :].to_broadcast([P, TT, ROPE]), ALU.mult))
            own.wait()
            own.mark(nc.vector.tensor_reduce(kr_ss[:], wide[0], AX.X, ALU.add))
            own.wait()
            own.mark(nc.vector.tensor_scalar(kr_ss[:], kr_ss[:], 1.0 / QKD, EPS, ALU.mult, ALU.add))
            cos, sin = mrope[:, 0, :, :], mrope[:, 1, :, :]
            x1, x2 = wide[1][:, :, 0:half], wide[1][:, :, half:ROPE]
            m1, m2 = wide[0][:, :, 0:half], wide[0][:, :, half:ROPE]
            own.mark(nc.vector.tensor_tensor(kr_tok[:, :, 0:half], x1, cos, ALU.mult))
            own.mark(nc.vector.tensor_tensor(m1, x2, sin, ALU.mult))
            own.mark(nc.vector.tensor_tensor(kr_tok[:, :, half:ROPE], x2, cos, ALU.mult))
            own.mark(nc.vector.tensor_tensor(m2, x1, sin, ALU.mult))
            own.wait()
            own.mark(nc.vector.tensor_tensor(kr_tok[:, :, 0:half], kr_tok[:, :, 0:half], m1, ALU.subtract))
            nc.vector.tensor_tensor(kr_tok[:, :, half:ROPE], kr_tok[:, :, half:ROPE], m2,
                                    ALU.add).then_inc(kr_ready, 1)
            def project_v(y, par):
                for b in range(2):
                    dve.wait_ge(mvhi_ready, 2 * y + b + 1)
                    v = ps[:, 2 + b, :].rearrange("p (t c) -> p t c", t=2)[:, :, NOPE:NOPE + VD]
                    nc.vector.tensor_tensor(mv_lo[:, par, 2 * b:2 * b + 2, :], v,
                                            mv_hi[:, par, 2 * b:2 * b + 2, :].bitcast(F32),
                                            ALU.subtract).then_inc(mv_ready, 1)

            def transposed_qk(y, par, which):
                hi, lo, gain = (qT_hi, qT_lo, G_QN) if which == 0 else (kT_hi, kT_lo, G_KN)
                dve.wait_ge(qkThi_ready, 4 * y + 2 * which + 1)
                nc.vector.scalar_tensor_tensor(lo[:, par, :], ps[:, 2 * which, :], gains[:, gain:gain + 1],
                                               hi[:, par, :].bitcast(F32), ALU.mult, ALU.subtract
                                               ).then_inc(qkT_ready, 1)
                rows = slice(par * ROPE, (par + 1) * ROPE)
                dve.wait_ge(qkThi_ready, 4 * y + 2 * which + 2)
                nc.vector.tensor_tensor(lo[rows, 2, :], ps[rows, 2 * which + 1, :], hi[rows, 2, :].bitcast(F32),
                                        ALU.subtract).then_inc(qkT_ready, 1)

            def maximum(x, par, b):
                kend, u = (b + 1) * P, 4 * par + b
                bank = ps[:, 4 + b % 2, :]
                if b == 0:
                    dve.wait_ge(qscale_ready, x + 1)
                dve.wait_ge(sc_done, 4 * x + b + 1)
                own.mark(nc.vector.memset(bank[0:CHUNK, kend - CHUNK:kend], -1e30))
                own.wait()
                own.mark(nc.vector.reduce_max(att[:, 0, u:u + 1], bank[:, 0:kend], AX.X))
                own.wait()
                nc.vector.tensor_scalar(att[:, 1, u:u + 1], att[:, 0, u:u + 1], qscale[:, par, b:b + 1], -1.0,
                                        ALU.mult, ALU.mult).then_inc(nmax_ready, 1)

            def normalize(x, par, b):
                kend, u = (b + 1) * P, 4 * par + b
                dve.wait_ge(exp_ready, 4 * x + b + 1)
                own.mark(nc.vector.reciprocal(att[:, 3, u:u + 1], att[:, 2, u:u + 1]))
                own.wait()
                nc.vector.tensor_scalar(pr[:, b % 2, 0:kend], pr[:, b % 2, 0:kend], att[:, 3, u:u + 1], None,
                                        ALU.mult).then_inc(pr_ready, 1)

            def transposed_p(x, b):
                dve.wait_ge(pThi_ready, 4 * x + b + 1)
                blocks = slice(b * P, (b + 1) * P)
                nc.vector.tensor_tensor(pT_lo[:, 0:b + 1, blocks],
                                        ps[:, 6, 0:(b + 1) * P].rearrange("p (k q) -> p k q", k=b + 1),
                                        pT_hi[:, 0:b + 1, blocks].bitcast(F32), ALU.subtract).then_inc(pT_ready, 1)

            def output(x):
                dve.wait_ge(ohi_ready, x + 1)

                def at(buffer):
                    return buffer[:, x, :] if isinstance(x, int) else \
                        buffer[:, bass.ds(x, 1), :].rearrange("p a t -> p (a t)")
                nc.vector.tensor_tensor(at(x_lo), ps[:, 7, :], at(x_hi).bitcast(F32),
                                        ALU.subtract).then_inc(o_ready, 1)

            def phase(x, par, project=True):
                first = isinstance(x, int) and x == 0
                maximum(x, par, 0)
                maximum(x, par, 1)
                normalize(x, par, 0)
                if not first:
                    transposed_p(x - 1, 3)
                normalize(x, par, 1)
                transposed_p(x, 0)
                maximum(x, par, 2)
                if project:
                    project_v(x + 1, 1 - par)
                transposed_p(x, 1)
                normalize(x, par, 2)
                if project:
                    transposed_qk(x + 1, 1 - par, 0)
                if not first:
                    output(x - 1)
                maximum(x, par, 3)
                transposed_p(x, 2)
                if project:
                    transposed_qk(x + 1, 1 - par, 1)
                normalize(x, par, 3)

            project_v(0, 0)
            transposed_qk(0, 0, 0)
            transposed_qk(0, 0, 1)
            phase(0, 0)
            with dve.Fori(0, 2) as i:
                own.enter(i, 2 * ATT_MARKS)
                for j in (1, 2):
                    phase(j + 2 * i, j % 2)
            own.leave(2 * ATT_MARKS, 2)
            for x in (5, 6):
                phase(x, x % 2)
            phase(MH - 1, 1, False)
            transposed_p(MH - 1, 3)
            output(MH - 1)
            for k in range(KT):
                dve.wait_ge(slot_used, MLA_OUT_BASE + k + 1)
                add_to_h(k, k % UB, MLA_OUT_UNIT + k)
                if k >= 1:
                    finish(MLP1, k - 1)
            finish(MLP1, KT - 1)

            mlp_ple(1, MLP1, PLE1, None)

        @block.tensor
        def _(pe):
            def product(out, st, mv, start, stop):
                nc.tensor.matmul(out, st[0], mv[1], start=start, stop=False)
                nc.tensor.matmul(out, st[1], mv[0], start=False, stop=False)
                return nc.tensor.matmul(out, st[0], mv[0], start=False, stop=stop)

            def weights(n, lo, hi):
                return w_hi[:, n % RING, lo:hi], w_lo[:, n % RING, lo:hi]

            def arrived(n):
                pe.wait_ge(lo_done, n + 1)

            def bank_free(unit):
                if not isinstance(unit, int) or unit >= UB:
                    pe.wait_ge(bank_read, unit - (UB - 1))

            def both(hi, lo, k, cols=slice(0, T)):
                return hi[:, k, cols], lo[:, k, cols]

            def tile_of(n, bank, operand, k, width=P, base=0, last=KT - 1):
                return product(ps[:, bank, :], weights(n, base + k * width, base + (k + 1) * width),
                               both(*operand, k), k == 0, k == last)

            def linear(n, i, per, unit, uper, count, operand, ready=None, norm=None):
                off, uoff = per * i, uper * i
                for k in range(KT - 1):
                    if ready:
                        ready(k)
                    for m in range(2):
                        if k == 0:
                            arrived(n + m + off)
                            bank_free(unit + m + uoff)
                        tile_of(n + m, (unit + m) % UB, operand, k)
                if ready:
                    ready(KT - 1)
                for m in range(2):
                    tile_of(n + m, (unit + m) % UB, operand, KT - 1).then_inc(slot_used, 1)
                if norm:
                    norm[0]()
                for m in range(2, count):
                    arrived(n + m + off)
                    bank_free(unit + m + uoff)
                    for k in range(KT):
                        last = tile_of(n + m, (unit + m) % UB, operand, k)
                    last.then_inc(slot_used, 1)
                    if norm and m == 2:
                        norm[1]()

            def mean(n, by):
                for t in range(TT):
                    last = nc.tensor.matmul(ps[:, token_bank(n), T - TT + t:T - TT + t + 1],
                                            sq_sum[:, t * P:(t + 1) * P], by[:], start=True, stop=True)
                last.then_inc(mean_done, 1)

            def spread(n, tok):
                if isinstance(n, int) and n == nth(MIX0):
                    pe.wait_ge(tables_loaded, 48)
                pe.wait_ge(tok_ready, n + 1)
                for t in range(TT):
                    last = nc.tensor.matmul(ps[:, NORM_BANK, t * P:(t + 1) * P],
                                            tok[:, t:t + 1].to_broadcast([P, P]), ident[:], start=True, stop=True)
                last.then_inc(spread_done, 1)

            def norm_steps(norm):
                def first():
                    pe.wait_ge(sq_added, KT * (norm + 1))
                    mean(nth(norm), mean_d)
                return first, lambda: spread(nth(norm), rstd_tok)

            def x_tile(norm):
                return lambda k: pe.wait_ge(x_ready, KT * norm + k + 1)

            pe.wait_ge(zeros_set, 1)
            for _ in range(WARM_UP):
                nc.tensor.matmul(ps[:, NORM_BANK, :], tmp[:, 0, 0:P], tmp[:, 0, :], start=True, stop=True)
            pe.wait_ge(means_set, 2)

            def head_norm_steps(i):
                def first():
                    pe.wait_ge(osq_added, VT * (i + 1))
                    mean(nth_head(i), mean_v)
                return first, lambda: spread(nth_head(i), head_tok)

            def ret_out(i, n, off, unit, uoff, norm=None):
                y = (y_hi, y_lo)

                def tiles(m, ks):
                    for k in ks:
                        if m == 0:
                            pe.wait_ge(y_ready, VT * i + k + 1)
                        last = tile_of(n + m // 2, (unit + m) % UB, y, k, base=(m % 2) * VT * P, last=VT - 1)
                    return last

                def start(m):
                    if m % 2 == 0:
                        arrived(n + m // 2 + off)
                    bank_free(unit + m + uoff)
                for m in range(2):
                    start(m)
                    tiles(m, range(VT - 1))
                if norm:
                    norm[0]()
                tiles(0, [VT - 1])
                tiles(1, [VT - 1]).then_inc(slot_used, 1)
                for m in range(2, KT):
                    start(m)
                    last = tiles(m, range(VT))
                    if m % 2:
                        last.then_inc(slot_used, 1)
                    if norm and m == 2:
                        norm[1]()

            def ret_head(i, n, j, per, unit, uper):
                first = per == 0
                off, uoff = per * j, uper * j

                if first:
                    linear(n, 0, 0, unit, 0, 4, operand[MIX0], x_tile(MIX0), norm_steps(MIX0))
                else:
                    steps = head_norm_steps(i - 1)
                    for m in range(4):
                        arrived(n + m + off)
                        bank_free(unit + m + uoff)
                        for k in range(KT):
                            last = tile_of(n + m, (unit + m) % UB, operand[MIX0], k)
                        last.then_inc(slot_used, 1)
                        if m < 2:
                            steps[m]()
                n, unit = n + 4, unit + 4
                if not first:
                    ret_out(i - 1, n, off, unit, uoff)
                    n, unit = n + 4, unit + KT
                for s in range(4):
                    arrived(n + s + off)
                    for t in range(TT):
                        if s == 0:
                            bank_free(unit + t + uoff)
                        for k in (2 * s, 2 * s + 1):
                            kk = k % 2
                            last = product(ps[:, t, :], both(x_hi, x_lo, k, slice(t * P, (t + 1) * P)),
                                           weights(n + s, kk * DV, (kk + 1) * DV), k == 0, k == KT - 1)
                    last.then_inc(slot_used, 1)
                n, unit = n + 4, unit + 4
                pe.wait_ge(qk_ready, 4 * (i + 1))
                if first:
                    pe.wait_ge(rstd_ready, 1)
                else:
                    pe.wait_ge(osq_added, VT * i)
                    pe.wait_ge(rstd_ready, nth_head(i - 1) + 1)
                for kt in range(TT):
                    for c in range(2):
                        last = product(ps[:, 4 + kt, 0:T - kt * P],
                                       both(qk_hi, qk_lo, 2 + c, slice(kt * P, (kt + 1) * P)),
                                       both(qk_hi, qk_lo, c, slice(kt * P, T)), c == 0, c == 1)
                    last.then_inc(s_done, 1)
                for v in range(VT):
                    arrived(n + v + off)
                    bank_free(unit + v + uoff)
                    for k in range(KT):
                        last = tile_of(n + v, (unit + v) % UB, operand[MIX0], k)
                    last.then_inc(slot_used, 1)
                pe.wait_ge(s_ready, TT * (i + 1))
                for v in range(VT):
                    for kt in range(TT):
                        last = product(ps[:, 4 + v, kt * P:T],
                                       both(v_hi, v_lo, kt, slice(v * P, (v + 1) * P)),
                                       both(s_hi, s_lo, kt, slice(kt * P, T)), kt == 0, kt == TT - 1)
                    last.then_inc(pv_done, 1)

            ret_head(0, 0, 0, 0, 0, 0)
            with pe.Fori(1, HEADS) as i:
                ret_head(i, RET_FIRST, i - 1, RET_HEAD, RET_FIRST_UNITS, RET_HEAD_UNITS)
            ret_out(HEADS - 1, RET_SLOTS - 4, 0, RET_UNITS - KT, 0, head_norm_steps(HEADS - 1))

            def mlp_quarter(L, norm, q, norm_of=None):
                linear(MLP_BASE[L], q, 2 * KT, MLP_UNIT[L], 2 * KT, KT, operand[norm],
                       x_tile(norm), norm_of)
                linear(MLP_BASE[L] + KT, q, 2 * KT, MLP_UNIT[L] + KT, 2 * KT, KT, (hid_hi, hid_lo),
                       lambda k: pe.wait_ge(hid_ready, KT * QUARTERS * L + KT * q + k + 1))

            def ple(L, norm):
                for pos in range(PLE_SLOTS):
                    n = PLE_BASE[L] + pos
                    if pos == 0:
                        linear(n, 0, 0, PLE_UNIT[L], 0, 2, operand[norm], x_tile(norm),
                               norm_steps(norm))
                    elif pos in PLE_PROJ:
                        half = PLE_PROJ.index(pos)
                        arrived(n)
                        if half == 0:
                            pe.wait_ge(p_ready, PF * (L + 1))
                            pe.wait_ge(rstd_ready, nth_spread(nth(norm)) + 1)
                        for m in range(4):
                            if half:
                                pe.wait_ge(h_ready, KT * L + m + 1)
                            for k in range(PF):
                                last = tile_of(n, 4 + m, (p_hi, p_lo), k, base=m * PF * P, last=PF - 1)
                        last.then_inc(slot_used, 1)
                    elif pos >= 2:
                        unit = PLE_UNIT[L] + PLE_GATE.index(pos)
                        arrived(n)
                        bank_free(unit)
                        for k in range(KT):
                            last = tile_of(n, unit % UB, operand[norm], k)
                        last.then_inc(slot_used, 1)
                        if pos == 2:
                            norm_steps(norm)[1]()

            def mlp_ple(L, mlp_norm, ple_norm):
                mlp_quarter(L, mlp_norm, 0, norm_steps(mlp_norm))
                with pe.Fori(1, QUARTERS) as q:
                    mlp_quarter(L, mlp_norm, q)
                ple(L, ple_norm)

            mlp_ple(0, MLP0, PLE0)

            def transpose_latent(f):
                for t in range(TT):
                    last = nc.tensor.transpose(ps[:, LATENT_BANKS[f], t * P:(t + 1) * P], c_tok[:, t, f * P:(f + 1) * P],
                                               ident[:])
                last.then_inc(cT_done, 1)

            for t in range(TT):
                bank_free(MLA_UNIT + t)
            for part, width in enumerate((QR, KVR + ROPE)):
                for s in range(4):
                    n = MLA_BASE + 4 * part + s
                    arrived(n)
                    for kk in range(2):
                        k = 2 * s + kk
                        if part == 0:
                            pe.wait_ge(x_ready, KT * MIX1 + k + 1)
                        for t in range(TT):
                            last = product(ps[:, 4 * part + t, 0:width],
                                           both(*operand[MIX1], k, slice(t * P, (t + 1) * P)),
                                           weights(n, kk * width, (kk + 1) * width), k == 0, k == KT - 1)
                    last.then_inc(slot_used, 1)
                    if part == 1 and s == 2:
                        pe.wait_ge(bank_read, MLA_UNIT + MLA_IN_UNITS)
                        for f in range(QF):
                            transpose_latent(f)
                if part == 0:
                    norm_steps(MIX1)[0]()

            def project_q(c, i, per):
                arrived(c + per * i)
                for t in range(TT):
                    lo = t % 2 * QKD
                    for f in range(QF):
                        last = product(ps[:, t // 2, lo:lo + QKD], both(c_hi, c_lo, f, slice(t * P, (t + 1) * P)),
                                       weights(c, f * QKD, (f + 1) * QKD), f == 0, f == QF - 1)
                last.then_inc(slot_used, 1)

            def project_kv(c, i, per):
                arrived(c + 1 + per * i)
                kv = NOPE + VD
                for t in range(TT):
                    lo = t % 2 * kv
                    for f in range(KVF):
                        last = product(ps[:, 2 + t // 2, lo:lo + kv],
                                       both(c_hi, c_lo, QF + f, slice(t * P, (t + 1) * P)),
                                       weights(c + 1, f * kv, (f + 1) * kv), f == 0, f == KVF - 1)
                last.then_inc(slot_used, 1)

            def transpose_qk(y, which):
                tok, rot = (q_tok, rq_tok) if which == 0 else (k_tok, rk_tok)
                if which == 0:
                    pe.wait_ge(qtok_ready, 6 * (y + 1))
                else:
                    pe.wait_ge(qkn_ready, 4 * y + 3)
                    pe.wait_ge(mv_ready, 2 * (y + 1))
                for x in range(2):
                    if x:
                        pe.wait_ge(qkn_ready, 4 * y + 2 * which + 2)
                    for t in range(TT):
                        src = rot[:, t, :] if x else tok[:, t, 0:NOPE]
                        last = nc.tensor.transpose(ps[:, 2 * which + x, t * P:(t + 1) * P], src, ident[:])
                    last.then_inc(qkT_done, 1)

            def scores(x, par, b):
                kend, u = (b + 1) * P, 4 * x + b
                if not isinstance(u, int) or u >= 2:
                    pe.wait_ge(exp_ready, u - 1)
                rows, cols = slice(par * ROPE, (par + 1) * ROPE), slice(b * P, (b + 1) * P)
                product(ps[:, 4 + b % 2, 0:kend], both(qT_hi, qT_lo, par, cols),
                        both(kT_hi, kT_lo, par, slice(0, kend)), True, False)
                product(ps[:, 4 + b % 2, 0:kend],
                        (qT_hi[rows, 2, cols], qT_lo[rows, 2, cols]),
                        (kT_hi[rows, 2, 0:kend], kT_lo[rows, 2, 0:kend]), False, True).then_inc(sc_done, 1)

            def transpose_p(x, b):
                u = 4 * x + b
                pe.wait_ge(pr_ready, u + 1)
                if not isinstance(u, int) or u >= 1:
                    pe.wait_ge(pT_ready, u)
                for kt in range(b + 1):
                    last = nc.tensor.transpose(ps[:, 6, kt * P:(kt + 1) * P], pr[:, b % 2, kt * P:(kt + 1) * P],
                                               ident[:])
                last.then_inc(pT_done, 1)

            def output(x, par):
                pe.wait_ge(pT_ready, 4 * (x + 1))
                for kt in range(TT):
                    last = product(ps[:, 7, kt * P:T], (mv_hi[:, par, kt, :], mv_lo[:, par, kt, :]),
                                   both(pT_hi, pT_lo, kt, slice(kt * P, T)), kt == 0, kt == TT - 1)
                last.then_inc(o_done, 1)

            def phase(x, par, c=None, i=0, per=0):
                first, project = isinstance(x, int) and x == 0, c is not None
                pe.wait_ge(qkT_ready, 4 * x + 2)
                if project:
                    project_q(c, i, per)
                else:
                    out_start(0, 6)
                pe.wait_ge(qkT_ready, 4 * (x + 1))
                scores(x, par, 0)
                scores(x, par, 1)
                if not first:
                    transpose_p(x - 1, 3)
                if project:
                    project_kv(c, i, per)
                else:
                    out_start(6, 9)
                if not first:
                    output(x - 1, 1 - par)
                transpose_p(x, 0)
                scores(x, par, 2)
                if not project:
                    out_start(9, 11)
                transpose_p(x, 1)
                if project:
                    transpose_qk(x + 1, 0)
                scores(x, par, 3)
                if not project:
                    out_start(11, 14)
                transpose_p(x, 2)
                if project:
                    transpose_qk(x + 1, 1)

            def out_product(m, k):
                if k == 0:
                    arrived(MLA_OUT_BASE + m)
                    bank_free(MLA_OUT_UNIT + m)
                pe.wait_ge(o_ready, k + 1)
                return tile_of(MLA_OUT_BASE + m, (MLA_OUT_UNIT + m) % UB, (x_hi, x_lo), k)

            def out_start(first, last):
                for j in range(first, last):
                    out_product(j // (MH - 2), j % (MH - 2))

            pe.wait_ge(c_ready, QF)
            project_q(MLA_HEAD_BASE, 0, 0)
            pe.wait_ge(ckv_ready, TT)
            for f in range(QF, QF + KVF):
                transpose_latent(f)
            pe.wait_ge(c_ready, QF + KVF)
            project_kv(MLA_HEAD_BASE, 0, 0)
            transpose_qk(0, 0)
            transpose_qk(0, 1)
            phase(0, 0, MLA_HEAD_BASE + 2)
            with pe.Fori(0, 2) as i:
                for j in (1, 2):
                    phase(j + 2 * i, j % 2, MLA_HEAD_BASE + 2 * (j + 1), i, 4)
            for x in (5, 6):
                phase(x, x % 2, MLA_HEAD_BASE + 2 * (x + 1))
            phase(MH - 1, 1)
            out_start(14, 17)
            transpose_p(MH - 1, 3)
            out_start(17, 20)
            output(MH - 1, 1)
            out_start(20, UB * (MH - 2))
            for m in range(UB):
                out_product(m, MH - 2)
                out_product(m, MH - 1).then_inc(slot_used, 1)
            for m in range(UB, KT):
                for k in range(KT):
                    last = out_product(m, k)
                last.then_inc(slot_used, 1)

            mlp_ple(1, MLP1, PLE1)


def rotary(seq, dim):
    inv = np.float32(1.0) / (np.float32(10000.0) ** (np.arange(0, dim, 2, dtype=np.float32) / np.float32(dim)))
    angle = np.arange(seq, dtype=np.float32)[:, None] * inv[None, :]
    return np.cos(angle), np.sin(angle)


def decay_tables():
    gamma_log = np.log(1.0 - 2.0 ** (-5.0 - np.arange(HEADS)))
    p, x = np.arange(P)[:, None], np.arange(T)[None, :]
    seen = x // CHUNK >= p // CHUNK
    table = np.exp(gamma_log[None, :, None] * np.abs(x - p)[:, None, :]) * seen[:, None, :]
    return (table * DK ** -0.5).astype(np.float32)


def std_slots(w):
    k, m = w.shape
    return w.reshape(k // P, P, m // P, P).transpose(2, 1, 0, 3).reshape(m // P, P, k)


def wide_slots(w, rows):
    k, m = w.shape
    return w.reshape(k // P // rows, rows, P, m).transpose(0, 2, 1, 3).reshape(-1, P, rows * m)


def columns(v):
    return v.reshape(-1, P).T


def lay_out(inputs):
    def tiles(x):
        return x.T.reshape(-1, P, x.shape[0]).transpose(1, 0, 2)

    w = {k: np.asarray(v) for k, v in inputs.items()}
    w_in, w_out = w["ret_w_in"][0], w["ret_w_out"][0]
    q, k, v, gate = np.split(w_in, [D, 2 * D, 2 * D + HEADS * DV], axis=1)

    def head_out(i):
        return w_out[i * DV:(i + 1) * DV].reshape(VT, P, KT // 2, 2, P).transpose(2, 1, 3, 0, 4).reshape(-1, P, SLOT)

    def mlp_ple(L):
        parts = []
        w1, w2 = w["mlp_w1"][L], w["mlp_w2"][L]
        for c in range(QUARTERS):
            parts += [std_slots(w1[:, c * D:(c + 1) * D]), std_slots(w2[c * D:(c + 1) * D])]
        gates = std_slots(w["ple_gate_w"][L])
        pp = w["ple_proj_w"][L].reshape(PF, P, 2, 4, P).transpose(2, 1, 3, 0, 4).reshape(2, P, SLOT)
        for pos in range(PLE_SLOTS):
            parts.append(pp[PLE_PROJ.index(pos)][None] if pos in PLE_PROJ else gates[PLE_GATE.index(pos)][None])
        return parts

    parts = []
    for i in range(HEADS):
        dk, dv = slice(i * DK, (i + 1) * DK), slice(i * DV, (i + 1) * DV)
        parts += [std_slots(q[:, dk]), std_slots(k[:, dk])]
        if i:
            parts.append(head_out(i - 1))
        parts += [wide_slots(v[:, dv], 2), std_slots(gate[:, dv])]
    parts.append(head_out(HEADS - 1))
    mla_in, uq, ukv = w["mla_w_in"][0], w["mla_w_uq"][0], w["mla_w_ukv"][0]
    kv = NOPE + VD
    qn, kn = w["mla_q_norm"][0], w["mla_k_norm"][0]
    gains = [w[name][L] for L in range(2) for name in ("mix_norm", "mlp_norm", "ple_norm")]
    gains += [w["ret_gn"][0].reshape(-1), w["mla_q_a_norm"][0], w["mla_kv_a_norm"][0], qn[:NOPE], kn[:NOPE]]
    cos, sin = rotary(T, DK)
    mcos, msin = rotary(T, ROPE)
    mrope = np.stack([mcos, msin]).reshape(2, TT, P, ROPE // 2).transpose(2, 0, 1, 3)
    out = {
        "x": tiles(w["x"][0]),
        "p": np.stack([tiles(w["p"][L, 0]) for L in range(2)]),
        "gains": np.concatenate([columns(g) for g in gains], axis=1),
        "rope": np.stack([cos.T, sin.T], axis=1),
        "decay": decay_tables(),
        "ident": np.eye(P, dtype=np.float32),
        "mrope": mrope,
        "rgain": np.broadcast_to(np.stack([qn[NOPE:], kn[NOPE:]])[None], (P, 2, ROPE)),
        "weights0": np.concatenate(parts + mlp_ple(0)),
        "weights1": np.concatenate(mlp_ple(1)),
        "mla_in_q": wide_slots(mla_in[:, :QR], 2),
        "mla_in_kv": wide_slots(mla_in[:, QR:], 2),
        "mla_uq": np.concatenate([wide_slots(uq[:, c * QKD:(c + 1) * QKD], QF) for c in range(MH)]),
        "mla_ukv": np.concatenate([wide_slots(ukv[:, c * kv:(c + 1) * kv], KVF) for c in range(MH)]),
        "mla_out": std_slots(w["mla_w_out"][0]),
    }
    return {name: np.ascontiguousarray(v) for name, v in out.items()}


def kernel(**inputs):
    import concourse.bacc as bacc
    from concourse.bass_utils import run_bass_kernel_spmd

    nc = bacc.Bacc("TRN2", target_bir_lowering=False, num_devices=1)
    arrays = lay_out(inputs)
    aps = {name: nc.dram_tensor("in_" + name, v.shape, F32, kind="ExternalInput").ap() for name, v in arrays.items()}
    aps["out"] = nc.dram_tensor("out", (P, KT, T), F32, kind="ExternalOutput").ap()
    build(nc, aps)
    got = run_bass_kernel_spmd(nc, [{"in_" + name: v for name, v in arrays.items()}], core_ids=[0]).results[0]["out"]
    return got.transpose(2, 1, 0).reshape(1, T, D)
```
